# Optimizing a Trainium2 kernel written in Bass

```python
import math
import jax, jax.numpy as jnp
from jax import lax
import numpy as np

D_MODEL = 1024
BATCH = 1
SEQ = 1024
DEPTH = 2

CTX_LEN = 256
GRID_W = 64
HEAD_DIM = 64
ATTN_WIDTH = D_MODEL // 2
SGU_WIDTH = D_MODEL // 4
FOURIER_WIDTH = D_MODEL // 4
MIX_WIDTH = ATTN_WIDTH + SGU_WIDTH + FOURIER_WIDTH
N_Q_HEADS = ATTN_WIDTH // HEAD_DIM
N_KV_HEADS = N_Q_HEADS // 4
KV_WIDTH = N_KV_HEADS * HEAD_DIM
SGU_HEAD_DIM = 64
N_SGU_HEADS = SGU_WIDTH // SGU_HEAD_DIM
FOURIER_GROUP_DIM = 64
N_FOURIER_GROUPS = FOURIER_WIDTH // FOURIER_GROUP_DIM
IN_WIDTH = ATTN_WIDTH + 2 * KV_WIDTH + 2 * SGU_WIDTH + FOURIER_WIDTH
Q_END = ATTN_WIDTH
K_END = Q_END + KV_WIDTH
V_END = K_END + KV_WIDTH
U_END = V_END + SGU_WIDTH
G_END = U_END + SGU_WIDTH
WINDOW = 128
BLOCK = 128
CHUNK = 128
D_FF = 4 * D_MODEL
ROPE_THETA = 10000.0
EPS = 1e-6
NEG_INF = -1e30


def rmsnorm(x, g):
    xf = x.astype(jnp.float32)
    y = xf * lax.rsqrt(jnp.mean(xf * xf, axis=-1, keepdims=True) + EPS)
    return (y * g.astype(jnp.float32)).astype(x.dtype)

def axial_rope_tables(rows):
    row = jnp.repeat(jnp.arange(rows), GRID_W).astype(jnp.float32)
    col = jnp.tile(jnp.arange(GRID_W), rows).astype(jnp.float32)
    n_freq = HEAD_DIM // 4
    inv_freq = ROPE_THETA ** (-jnp.arange(n_freq, dtype=jnp.float32) / n_freq)
    ang_r = row[:, None] * inv_freq[None, :]
    ang_c = col[:, None] * inv_freq[None, :]
    ang = jnp.concatenate([ang_r, ang_r, ang_c, ang_c], axis=-1)
    return jnp.cos(ang), jnp.sin(ang)

def apply_rope(x, cos, sin):
    x1, x2, x3, x4 = jnp.split(x, 4, axis=-1)
    rot = jnp.concatenate([-x2, x1, -x4, x3], axis=-1)
    out = x * cos[None, :, None, :] + rot * sin[None, :, None, :]
    return out.astype(x.dtype)

def neighbour_blocks(t):
    z = jnp.zeros_like(t[:, :1])
    prev = jnp.concatenate([z, t[:, :-1]], axis=1)
    nxt = jnp.concatenate([t[:, 1:], z], axis=1)
    return jnp.concatenate([prev, t, nxt], axis=2)

def latent_window_attention(q, k, v, ck, cv, sink):
    B, S, H, hd = q.shape
    G = H // N_KV_HEADS
    nb = S // BLOCK
    scale = hd ** -0.5
    qb = q.reshape(B, nb, BLOCK, N_KV_HEADS, G, hd)
    kw = neighbour_blocks(k.reshape(B, nb, BLOCK, N_KV_HEADS, hd))
    vw = neighbour_blocks(v.reshape(B, nb, BLOCK, N_KV_HEADS, hd))
    s_loc = jnp.einsum('bnqhgd,bnkhd->bnhgqk', qb, kw, preferred_element_type=jnp.float32) * scale
    qpos = jnp.arange(BLOCK)[:, None]
    kpos = jnp.arange(3 * BLOCK)[None, :] - BLOCK
    band = jnp.abs(kpos - qpos) <= WINDOW
    kabs = jnp.arange(nb)[:, None, None] * BLOCK + kpos[None]
    valid = band[None] & (kabs >= 0) & (kabs < S)
    s_loc = jnp.where(valid[None, :, None, None], s_loc, NEG_INF)
    s_ctx = jnp.einsum('bnqhgd,bchd->bnhgqc', qb, ck, preferred_element_type=jnp.float32) * scale
    s_sink = jnp.broadcast_to(sink.astype(jnp.float32).reshape(1, 1, N_KV_HEADS, G, 1, 1),
                              s_loc.shape[:-1] + (1,))
    p = jax.nn.softmax(jnp.concatenate([s_loc, s_ctx, s_sink], axis=-1), axis=-1)
    n_loc = 3 * BLOCK
    n_ctx = ck.shape[1]
    p_loc = p[..., :n_loc].astype(v.dtype)
    p_ctx = p[..., n_loc:n_loc + n_ctx].astype(v.dtype)
    out = (jnp.einsum('bnhgqk,bnkhd->bnqhgd', p_loc, vw)
           + jnp.einsum('bnhgqc,bchd->bnqhgd', p_ctx, cv))
    return out.reshape(B, S, H * hd)

def context_attention(cq, ck, cv, sink):
    B, L, H, hd = cq.shape
    G = H // N_KV_HEADS
    qg = cq.reshape(B, L, N_KV_HEADS, G, hd)
    s = jnp.einsum('bqhgd,bkhd->bhgqk', qg, ck, preferred_element_type=jnp.float32) * (hd ** -0.5)
    s_sink = jnp.broadcast_to(sink.astype(jnp.float32).reshape(1, N_KV_HEADS, G, 1, 1),
                              s.shape[:-1] + (1,))
    p = jax.nn.softmax(jnp.concatenate([s, s_sink], axis=-1), axis=-1)[..., :L]
    out = jnp.einsum('bhgqk,bkhd->bqhgd', p.astype(cv.dtype), cv)
    return out.reshape(B, L, H * hd)

def spatial_gating(u, v, w_s, b_s, g_s):
    B, S, _ = u.shape
    vh = rmsnorm(v.reshape(B, S, N_SGU_HEADS, SGU_HEAD_DIM), g_s)
    vc = vh.reshape(B, S // CHUNK, CHUNK, N_SGU_HEADS, SGU_HEAD_DIM)
    mixed = jnp.einsum('hpq,bnqhd->bnphd', w_s, vc) + b_s.T[None, None, :, :, None]
    return u * mixed.reshape(B, S, SGU_WIDTH)

def fourier_mix(f):
    B, S, _ = f.shape
    fg = f.reshape(B, S, N_FOURIER_GROUPS, FOURIER_GROUP_DIM).astype(jnp.float32)
    y = jnp.real(jnp.fft.fft2(fg, axes=(1, 3), norm='ortho'))
    return y.reshape(B, S, FOURIER_WIDTH).astype(f.dtype)

def merge_heads(attn, sgu, four, g_mix, w_out):
    a = rmsnorm(attn, g_mix[:ATTN_WIDTH])
    s = rmsnorm(sgu, g_mix[ATTN_WIDTH:ATTN_WIDTH + SGU_WIDTH])
    f = rmsnorm(four, g_mix[ATTN_WIDTH + SGU_WIDTH:])
    return jnp.concatenate([a, s, f], axis=-1) @ w_out

def squared_relu_mlp(h, w1, w2):
    return jnp.square(jax.nn.relu(h @ w1)) @ w2

def first_inputs(seed: int = 0) -> dict:
    key = jax.random.key(seed)
    ks = jax.random.split(key, 24)
    f32 = jnp.float32
    nrm = lambda k, shape, s: jax.random.normal(k, shape, f32) * s
    gain = lambda k, shape: 1.0 + 0.05 * jax.random.normal(k, shape, f32)
    return {
        "x": nrm(ks[0], (BATCH, SEQ, D_MODEL), 1.0),
        "c": nrm(ks[1], (BATCH, D_MODEL), 1.0),
        "ctx": nrm(ks[2], (BATCH, CTX_LEN, D_MODEL), 1.0),
        "c_ctx": nrm(ks[3], (D_MODEL,), 1.0),
        "w_ada": nrm(ks[4], (DEPTH, D_MODEL, 6 * D_MODEL), 0.5 * D_MODEL ** -0.5),
        "b_ada": nrm(ks[5], (DEPTH, 6 * D_MODEL), 0.02),
        "g_pre_mix": gain(ks[6], (DEPTH, D_MODEL)),
        "w_in": nrm(ks[7], (DEPTH, D_MODEL, IN_WIDTH), D_MODEL ** -0.5),
        "sink": nrm(ks[8], (DEPTH, N_Q_HEADS), 0.5),
        "w_sgu": nrm(ks[9], (DEPTH, N_SGU_HEADS, CHUNK, CHUNK), 0.5 * CHUNK ** -0.5),
        "b_sgu": gain(ks[10], (DEPTH, N_SGU_HEADS, CHUNK)),
        "g_sgu": gain(ks[11], (DEPTH, N_SGU_HEADS, SGU_HEAD_DIM)),
        "g_mix": gain(ks[12], (DEPTH, MIX_WIDTH)),
        "w_out": nrm(ks[13], (DEPTH, MIX_WIDTH, D_MODEL), MIX_WIDTH ** -0.5),
        "g_post_mix": gain(ks[14], (DEPTH, D_MODEL)),
        "g_pre_ff": gain(ks[15], (DEPTH, D_MODEL)),
        "w_ff1": nrm(ks[16], (DEPTH, D_MODEL, D_FF), D_MODEL ** -0.5),
        "w_ff2": nrm(ks[17], (DEPTH, D_FF, D_MODEL), D_FF ** -0.5),
        "g_post_ff": gain(ks[18], (DEPTH, D_MODEL)),
    }

def first_block(x, c, ctx, c_ctx, w_ada, b_ada, g_pre_mix, w_in, sink, w_sgu, b_sgu, g_sgu,
              g_mix, w_out, g_post_mix, g_pre_ff, w_ff1, w_ff2, g_post_ff):
    B, S, _ = x.shape
    ROWS = S // GRID_W
    cos, sin = axial_rope_tables(ROWS)
    h_ctx = ctx
    for l in range(DEPTH):
        last = l == DEPTH - 1
        mod_x = (jax.nn.silu(c) @ w_ada[l] + b_ada[l])[:, None, :]
        sh1, sc1, g1, sh2, sc2, g2 = jnp.split(mod_x, 6, axis=-1)
        mod_c = jax.nn.silu(c_ctx) @ w_ada[l] + b_ada[l]
        csh1, csc1, cg1, csh2, csc2, cg2 = jnp.split(mod_c, 6, axis=-1)

        hc = rmsnorm(h_ctx, g_pre_mix[l]) * (1.0 + csc1) + csh1
        if last:
            ckv = hc @ w_in[l][:, Q_END:V_END]
            ck, cv = jnp.split(ckv, 2, axis=-1)
        else:
            pc = hc @ w_in[l]
            cq, ck, cv, cu, cg, cf = jnp.split(pc, [Q_END, K_END, V_END, U_END, G_END], axis=-1)
        ck = ck.reshape(B, CTX_LEN, N_KV_HEADS, HEAD_DIM)
        cv = cv.reshape(B, CTX_LEN, N_KV_HEADS, HEAD_DIM)
        if not last:
            c_attn = context_attention(cq.reshape(B, CTX_LEN, N_Q_HEADS, HEAD_DIM), ck, cv, sink[l])
            c_sgu = spatial_gating(jax.nn.gelu(cu), jax.nn.gelu(cg), w_sgu[l], b_sgu[l], g_sgu[l])
            c_four = fourier_mix(cf)
            yc = merge_heads(c_attn, c_sgu, c_four, g_mix[l], w_out[l])
            h_ctx = h_ctx + cg1 * rmsnorm(yc, g_post_mix[l])
            hc2 = rmsnorm(h_ctx, g_pre_ff[l]) * (1.0 + csc2) + csh2
            h_ctx = h_ctx + cg2 * rmsnorm(squared_relu_mlp(hc2, w_ff1[l], w_ff2[l]), g_post_ff[l])

        hx = rmsnorm(x, g_pre_mix[l]) * (1.0 + sc1) + sh1
        px = hx @ w_in[l]
        q, k, v, u, gv, f = jnp.split(px, [Q_END, K_END, V_END, U_END, G_END], axis=-1)
        q = apply_rope(q.reshape(B, S, N_Q_HEADS, HEAD_DIM), cos, sin)
        k = apply_rope(k.reshape(B, S, N_KV_HEADS, HEAD_DIM), cos, sin)
        v = v.reshape(B, S, N_KV_HEADS, HEAD_DIM)
        attn = latent_window_attention(q, k, v, ck, cv, sink[l])
        sgu = spatial_gating(jax.nn.gelu(u), jax.nn.gelu(gv), w_sgu[l], b_sgu[l], g_sgu[l])
        four = fourier_mix(f)
        y = merge_heads(attn, sgu, four, g_mix[l], w_out[l])
        x = x + g1 * rmsnorm(y, g_post_mix[l])
        hx2 = rmsnorm(x, g_pre_ff[l]) * (1.0 + sc2) + sh2
        x = x + g2 * rmsnorm(squared_relu_mlp(hx2, w_ff1[l], w_ff2[l]), g_post_ff[l])
    return x


DEPTH_2 = 1

ROPE_THETA_2 = 500000.0
NORM_EPS = 1e-6
NEG_BIG = -1e30
MLA_HEADS = 8
MLA_NOPE_DIM = 64
MLA_ROPE_DIM = 32
MLA_V_DIM = 64
MLA_Q_RANK = 384
MLA_KV_RANK = 256
MLA_WIDTH = MLA_HEADS * MLA_V_DIM
Q_BLOCK = 128
DIL_HEADS = 8
DIL_HEAD_DIM = 64
DIL_WIDTH = DIL_HEADS * DIL_HEAD_DIM
DIL_ROT_DIM = DIL_HEAD_DIM // 4
DIL_BRANCHES = ((128, 1), (512, 4), (2048, 16))
MIX_WIDTH_2 = MLA_WIDTH + DIL_WIDTH
IN_COLS = MLA_Q_RANK + MLA_KV_RANK + MLA_ROPE_DIM + 3 * DIL_WIDTH
N_EXPERTS = 16
EXPERT_FF = 1024
EC_CAPACITY_FACTOR = 2
N_MOD = 6


def rms_norm(x, g):
    xf = x.astype(jnp.float32)
    y = xf * lax.rsqrt(jnp.mean(xf * xf, axis=-1, keepdims=True) + NORM_EPS)
    return (y * g.astype(jnp.float32)).astype(x.dtype)

def rope_cos_sin(positions, dim):
    inv = 1.0 / (ROPE_THETA_2 ** (jnp.arange(0, dim, 2, dtype=jnp.float32) / dim))
    ang = positions.astype(jnp.float32)[..., None] * inv
    return jnp.cos(ang), jnp.sin(ang)

def apply_rope_2(t, cos, sin):
    t1, t2 = jnp.split(t, 2, axis=-1)
    c = cos[:, :, None, :].astype(t.dtype)
    s = sin[:, :, None, :].astype(t.dtype)
    return jnp.concatenate([t1 * c - t2 * s, t1 * s + t2 * c], axis=-1)

def mla_attention(q, k, v):
    B, S, H, Dq = q.shape
    nblk = S // Q_BLOCK
    scale = Dq ** -0.5
    qb = q.reshape(B, nblk, Q_BLOCK, H, Dq).transpose(1, 0, 2, 3, 4)

    def one_block(q_blk):
        s = jnp.einsum('bqhd,bkhd->bhqk', q_blk, k).astype(jnp.float32) * scale
        p = jax.nn.softmax(s, axis=-1).astype(v.dtype)
        return jnp.einsum('bhqk,bkhd->bqhd', p, v)

    o = lax.map(one_block, qb)
    return o.transpose(1, 0, 2, 3, 4).reshape(B, S, H, v.shape[-1])

def dilated_branch(q, k, v, dilation, half):
    B, S, H, Dh = q.shape
    L = S // dilation
    nb = -(-L // half)
    Lp = nb * half
    pad = Lp - L

    def to_sub(t):
        return t.reshape(B, L, dilation, H, Dh).transpose(0, 2, 1, 3, 4)

    qs = jnp.pad(to_sub(q), ((0, 0), (0, 0), (0, pad), (0, 0), (0, 0)))
    kpad = ((0, 0), (0, 0), (half, pad + half), (0, 0), (0, 0))
    ks = jnp.pad(to_sub(k), kpad)
    vs = jnp.pad(to_sub(v), kpad)
    valid = jnp.pad(jnp.ones((L,), dtype=bool), (half, pad + half))

    def bands(t):
        parts = [t[:, :, j * half:j * half + Lp].reshape(B, dilation, nb, half, H, Dh) for j in range(3)]
        return jnp.concatenate(parts, axis=3)

    kb, vb = bands(ks), bands(vs)
    kvalid = jnp.concatenate([valid[j * half:j * half + Lp].reshape(nb, half) for j in range(3)], axis=1)
    qb = qs.reshape(B, dilation, nb, half, H, Dh)
    s = jnp.einsum('brnqhd,brnkhd->brnhqk', qb, kb).astype(jnp.float32) * (Dh ** -0.5)
    rel = jnp.arange(3 * half)[None, :] - half - jnp.arange(half)[:, None]
    mask = (jnp.abs(rel) <= half)[None, :, :] & kvalid[:, None, :]
    s = jnp.where(mask[None, None, :, None, :, :], s, NEG_BIG)
    m = jnp.max(s, axis=-1, keepdims=True)
    e = jnp.exp(s - m)
    den = jnp.sum(e, axis=-1)
    p = (e / den[..., None]).astype(v.dtype)
    o = jnp.einsum('brnhqk,brnkhd->brnqhd', p, vb)
    lse = m[..., 0] + jnp.log(den)
    o = o.reshape(B, dilation, Lp, H, Dh)[:, :, :L].transpose(0, 2, 1, 3, 4).reshape(B, S, H, Dh)
    lse = lse.transpose(0, 1, 2, 4, 3).reshape(B, dilation, Lp, H)[:, :, :L]
    lse = lse.transpose(0, 2, 1, 3).reshape(B, S, H)
    return o, lse

def dilated_attention(q, k, v):
    outs, lses = [], []
    for window, dilation in DIL_BRANCHES:
        o, l = dilated_branch(q, k, v, dilation, window // (2 * dilation))
        outs.append(o)
        lses.append(l)
    wts = jax.nn.softmax(jnp.stack(lses, axis=0), axis=0)
    o = jnp.einsum('nbsh,nbshd->bshd', wts, jnp.stack(outs, axis=0).astype(jnp.float32))
    return o.astype(q.dtype)

def expert_choice_ffn(h, w_router, b_router, w_gate, w_up, w_down):
    B, S, D = h.shape
    cap = EC_CAPACITY_FACTOR * S // N_EXPERTS
    logits = jnp.einsum('bsd,de->bse', h, w_router).astype(jnp.float32) + b_router.astype(jnp.float32)
    aff = jax.nn.softmax(logits, axis=-1)
    gate, idx = lax.top_k(jnp.swapaxes(aff, 1, 2), cap)
    xe = jax.vmap(lambda hb, ib: hb[ib])(h, idx)
    a = jnp.einsum('becd,edf->becf', xe, w_gate)
    u = jnp.einsum('becd,edf->becf', xe, w_up)
    ye = jnp.einsum('becf,efd->becd', jax.nn.silu(a) * u, w_down)
    ye = ye * gate[..., None].astype(ye.dtype)
    return jax.vmap(lambda ib, yb: jnp.zeros((S, D), yb.dtype).at[ib.reshape(-1)].add(yb.reshape(-1, D)))(idx, ye)

def second_inputs(seed: int = 0) -> dict:
    key = jax.random.key(seed)
    ks = jax.random.split(key, 24)
    f32 = jnp.float32
    nrm = lambda k, shape, fan_in: jax.random.normal(k, shape, f32) * (fan_in ** -0.5)
    gain = lambda k, shape: 1.0 + 0.05 * jax.random.normal(k, shape, f32)
    x = jax.random.normal(ks[0], (BATCH, SEQ, D_MODEL), f32)
    c = jax.random.normal(ks[1], (BATCH, D_MODEL), f32)
    offset = jax.random.randint(ks[2], (BATCH, 1), 0, 1024, dtype=jnp.int32)
    positions = offset + jnp.arange(SEQ, dtype=jnp.int32)[None, :]
    return {
        'x': x,
        'c': c,
        'positions': positions,
        'w_ada': 0.5 * nrm(ks[3], (DEPTH_2, D_MODEL, N_MOD * D_MODEL), D_MODEL),
        'b_ada': 0.02 * jax.random.normal(ks[4], (DEPTH_2, N_MOD * D_MODEL), f32),
        'g_mix': gain(ks[5], (DEPTH_2, D_MODEL)),
        'w_in': nrm(ks[6], (DEPTH_2, D_MODEL, IN_COLS), D_MODEL),
        'g_q': gain(ks[7], (DEPTH_2, MLA_Q_RANK)),
        'w_uq': nrm(ks[8], (DEPTH_2, MLA_Q_RANK, MLA_HEADS * (MLA_NOPE_DIM + MLA_ROPE_DIM)), MLA_Q_RANK),
        'g_kv': gain(ks[9], (DEPTH_2, MLA_KV_RANK)),
        'w_ukv': nrm(ks[10], (DEPTH_2, MLA_KV_RANK, MLA_HEADS * (MLA_NOPE_DIM + MLA_V_DIM)), MLA_KV_RANK),
        'w_out': nrm(ks[11], (DEPTH_2, MIX_WIDTH_2, D_MODEL), MIX_WIDTH_2),
        'g_ffn': gain(ks[12], (DEPTH_2, D_MODEL)),
        'w_router': nrm(ks[13], (DEPTH_2, D_MODEL, N_EXPERTS), D_MODEL),
        'b_router': 0.01 * jax.random.normal(ks[14], (DEPTH_2, N_EXPERTS), f32),
        'w_gate': nrm(ks[15], (DEPTH_2, N_EXPERTS, D_MODEL, EXPERT_FF), D_MODEL),
        'w_up': nrm(ks[16], (DEPTH_2, N_EXPERTS, D_MODEL, EXPERT_FF), D_MODEL),
        'w_down': nrm(ks[17], (DEPTH_2, N_EXPERTS, EXPERT_FF, D_MODEL), EXPERT_FF),
        'g_final': gain(ks[18], (D_MODEL,)),
    }

def second_block(x, c, positions, w_ada, b_ada, g_mix, w_in, g_q, w_uq, g_kv, w_ukv, w_out,
              g_ffn, w_router, b_router, w_gate, w_up, w_down, g_final):
    B, S, D = x.shape
    cos_m, sin_m = rope_cos_sin(positions, MLA_ROPE_DIM)
    cos_d, sin_d = rope_cos_sin(positions, DIL_ROT_DIM)
    o1 = MLA_Q_RANK
    o2 = o1 + MLA_KV_RANK
    o3 = o2 + MLA_ROPE_DIM
    o4 = o3 + DIL_WIDTH
    o5 = o4 + DIL_WIDTH
    for l in range(DEPTH_2):
        mod = jnp.einsum('bd,de->be', jax.nn.silu(c), w_ada[l]) + b_ada[l]
        sh_a, sc_a, gt_a, sh_m, sc_m, gt_m = jnp.split(mod[:, None, :], N_MOD, axis=-1)

        h = rms_norm(x, g_mix[l]) * (1.0 + sc_a) + sh_a
        proj = jnp.einsum('bsd,dc->bsc', h, w_in[l])
        cq, ckv, kr = proj[..., :o1], proj[..., o1:o2], proj[..., o2:o3]
        dq, dk, dv = proj[..., o3:o4], proj[..., o4:o5], proj[..., o5:]

        q = jnp.einsum('bsr,rc->bsc', rms_norm(cq, g_q[l]), w_uq[l]).reshape(B, S, MLA_HEADS, MLA_NOPE_DIM + MLA_ROPE_DIM)
        q = jnp.concatenate([q[..., :MLA_NOPE_DIM], apply_rope_2(q[..., MLA_NOPE_DIM:], cos_m, sin_m)], axis=-1)
        kv = jnp.einsum('bsr,rc->bsc', rms_norm(ckv, g_kv[l]), w_ukv[l]).reshape(B, S, MLA_HEADS, MLA_NOPE_DIM + MLA_V_DIM)
        k_rope = apply_rope_2(kr[:, :, None, :], cos_m, sin_m)
        k = jnp.concatenate([kv[..., :MLA_NOPE_DIM], jnp.broadcast_to(k_rope, (B, S, MLA_HEADS, MLA_ROPE_DIM))], axis=-1)
        v = kv[..., MLA_NOPE_DIM:]
        out_a = mla_attention(q, k, v).reshape(B, S, MLA_WIDTH)

        def partial_rope(t):
            t = t.reshape(B, S, DIL_HEADS, DIL_HEAD_DIM)
            return jnp.concatenate([apply_rope_2(t[..., :DIL_ROT_DIM], cos_d, sin_d), t[..., DIL_ROT_DIM:]], axis=-1)
        out_b = dilated_attention(partial_rope(dq), partial_rope(dk), dv.reshape(B, S, DIL_HEADS, DIL_HEAD_DIM))
        out_b = out_b.reshape(B, S, DIL_WIDTH)

        mixed = jnp.einsum('bsc,cd->bsd', jnp.concatenate([out_a, out_b], axis=-1), w_out[l])
        x = x + gt_a * mixed

        h2 = rms_norm(x, g_ffn[l]) * (1.0 + sc_m) + sh_m
        x = x + gt_m * expert_choice_ffn(h2, w_router[l], b_router[l], w_gate[l], w_up[l], w_down[l])
    return rms_norm(x, g_final)


def setup_inputs(seed=0):
    out = dict(first_inputs(seed))
    for name, value in second_inputs(seed + 1).items():
        if name != "x":
            out[name + "_2"] = value
    return out


def reference(
    x, c, ctx, c_ctx, w_ada, b_ada, g_pre_mix, w_in, sink, w_sgu, b_sgu, g_sgu, g_mix, w_out,
    g_post_mix, g_pre_ff, w_ff1, w_ff2, g_post_ff, c_2, positions_2, w_ada_2, b_ada_2, g_mix_2,
    w_in_2, g_q_2, w_uq_2, g_kv_2, w_ukv_2, w_out_2, g_ffn_2, w_router_2, b_router_2, w_gate_2,
    w_up_2, w_down_2, g_final_2,
):
    x = first_block(
        x, c, ctx, c_ctx, w_ada, b_ada, g_pre_mix, w_in, sink, w_sgu, b_sgu, g_sgu, g_mix,
        w_out, g_post_mix, g_pre_ff, w_ff1, w_ff2, g_post_ff,
    )
    return second_block(
        x, c_2, positions_2, w_ada_2, b_ada_2, g_mix_2, w_in_2, g_q_2, w_uq_2, g_kv_2, w_ukv_2,
        w_out_2, g_ffn_2, w_router_2, b_router_2, w_gate_2, w_up_2, w_down_2, g_final_2,
    )


_drawn_inputs = setup_inputs


def setup_inputs(seed=0):
    import zlib

    import numpy as np

    out = dict(_drawn_inputs(seed))
    spreads = {}
    factors = {'g_pre_mix': 2.87,
     'sink': 64.0,
     'b_sgu': 6.63,
     'g_sgu': 8.0,
     'g_mix': 2.857,
     'g_post_ff': 2.704,
     'b_ada_2': 4.94,
     'g_mix_2': 8.0,
     'g_q_2': 8.0,
     'w_uq_2': 4.547,
     'g_kv_2': 8.0,
     'g_ffn_2': 6.761,
     'b_router_2': 8.0}
    for name, (base, spread) in spreads.items():
        noise = np.random.default_rng([zlib.crc32(name.encode()), seed]).standard_normal(out[name].shape)
        drawn = base * np.exp(spread * noise) if base else spread * noise
        out[name] = __import__('jax').numpy.asarray(drawn.astype(out[name].dtype))
    for name, factor in factors.items():
        out[name] = (out[name] * factor).astype(out[name].dtype)
    return out
```

```python
from contextlib import ExitStack

import concourse.bass as bass
from concourse import mybir

F32 = mybir.dt.float32
I32 = mybir.dt.int32
ALU = mybir.AluOpType
ACT = mybir.ActivationFunctionType
AX_X = mybir.AxisListType.X

P = 128
D = 1024
KD = D // P
FF = 4096
EPS = 1e-6
BANK = 512
NEG = -1e30
RING = 4
SLOT = 4096
N_EXP = 16
CAP = 128

ROW_ADA, ROW_PRE, ROW_MIX, ROW_POST, ROW_FF, ROW_POSTFF, ROW_BSGU = 0, 48, 56, 64, 72, 80, 88
ROW_C, ROW_CCTX = 96, 104
ROW2_MIX, ROW2_Q, ROW2_KV, ROW2_FFN, ROW2_FINAL, ROW2_POS = 48, 56, 59, 61, 69, 96

Q0, K0, V0, U0, G0, F0 = 0, 512, 640, 768, 1024, 1280


class Signal:

    def __init__(self, sem):
        self.sem = sem
        self.planned = 0

    def span(self, n):
        base = self.planned
        self.planned += n
        return base


class Steps:

    def __init__(self, sem):
        self.sem = sem
        self.n = 0
        self.var = None

    def loop(self, var, per):
        self.var, self.per, self.start = var, per, self.n

    def loop_end(self, trips):
        assert self.n - self.start == self.per, ("steps per trip", self.n - self.start)
        self.n = self.start + trips * self.per
        self.var = None

    def done(self, eng, ins):
        ins.then_inc(self.sem, 1)
        self.n += 1
        eng.wait_ge(self.sem, self.n if self.var is None else self.var * self.per + self.n)


class Ring:

    def __init__(self, slots, landed, used):
        self.slots, self.landed, self.used, self.n = slots, landed, used, 0

    def take(self, n):
        base = self.n
        self.n += n
        return base

    def load(self, sp, n, src, cols, more=0):
        s = n % RING
        if n >= RING:
            sp.wait_ge(self.used.sem, n - RING + 1 + more)
        dst = self.slots[:, s, 0:cols]
        if len(src.shape) == 3:
            dst = dst.rearrange("p (a b) -> p a b", a=src.shape[1])
        sp.dma_start(dst, src).then_inc(self.landed[s], 16)

    def ready(self, pe, n, trip=0, per=0):
        pe.wait_ge(self.landed[n % RING], 16 * (n // RING + 1) + trip * (16 * per // RING))

    def view(self, n, a):
        return self.slots[:, n % RING, :].rearrange("p (a b) -> p a b", a=a)


class Stage:
    def load(self, sp):
        pass

    def tensor(self, pe):
        pass

    def vector(self, dve):
        pass

    def scalar(self, act):
        pass

    def pool(self, gp):
        pass


def build(nc, A, consts, out):
    ctx = ExitStack()
    with ctx:
        def sb(name, shape, dt=F32):
            return ctx.enter_context(nc.sbuf_tensor(name, shape, dt))

        def signal(name):
            return Signal(ctx.enter_context(nc.semaphore(name)))

        X = sb("X", [P, 8, D])
        WB = sb("WB", [P, RING, SLOT])
        AR = sb("AR", [P, 22528])
        IDENT = sb("IDENT", [P, P])
        ONES = sb("ONES", [P, P])
        EPSC = sb("EPSC", [P, 1])
        VEC = sb("VEC", [P, 3, P])
        SC = sb("SC", [P, 3, 8])
        MODC = sb("MODC", [P, 2, 48])
        DER = sb("DER", [P, 2, 4, 8])
        ROPE = sb("ROPE", [P, 2, 512])
        WMASK = sb("WMASK", [P, 384])
        DFTF = sb("DFTF", [P, 256])
        KCT = sb("KCT", [P, 2, 256])
        VC = sb("VC", [P, 2, P])
        WST = sb("WST", [P, 4, P])
        GSGU = sb("GSGU", [P, 256])
        SINK = sb("SINK", [P, 2, 8])
        STAT = sb("STAT", [P, 128])
        GATE = sb("GATE", [P, D])
        INV = sb("INV", [P, 24])
        IOTA_I = sb("IOTA_I", [P, P + 8], I32)
        IDX = sb("IDX", [P, N_EXP], I32)
        GT = sb("GT", [P, N_EXP])
        RF = ROPE[:, :, :].rearrange("p a b -> p (a b)")
        ROPE2 = RF[:, 0:768].rearrange("p (t a) -> p t a", t=8)
        KR = RF[:, 768:1024].rearrange("p (t a) -> p t a", t=8)
        PS = ctx.enter_context(nc.psum_tensor("PS", [P, 8, BANK], F32))

        def area(off, *shape):
            n = 1
            for s in shape:
                n *= s
            v = AR[:, off:off + n]
            if len(shape) == 2:
                return v.rearrange("p (a b) -> p a b", a=shape[0])
            if len(shape) == 3:
                return v.rearrange("p (a b c) -> p a b c", a=shape[0], b=shape[1])
            return v

        XF = X[:, :, :].rearrange("p a b -> p (a b)")

        def xarea(off, *shape):
            n = 1
            for s in shape:
                n *= s
            v = XF[:, off:off + n]
            if len(shape) == 2:
                return v.rearrange("p (a b) -> p a b", a=shape[0])
            return v

        HT = area(0, 8, 1024)
        XC = area(20480, 2, 1024)

        mm = signal("pe_group_done")
        freed_d = signal("psum_taken_by_dve")
        freed_a = signal("psum_taken_by_act")
        squares = signal("act_square_sums")
        roots = signal("act_roots")
        normed = signal("dve_normed_rows")
        consts_in = signal("consts_landed")
        rows_zero = signal("vector_rows_zeroed")
        rows_in = signal("vector_rows_landed")
        ones_set = signal("ones_set")
        setup_act = signal("act_silu_done")
        block_used = signal("ring_block_used")
        landed = [ctx.enter_context(nc.semaphore(f"ring_slot{i}_landed")) for i in range(RING)]
        ring = Ring(WB, landed, block_used)
        hid_done = signal("act_hidden_done")
        zeroed = signal("pool_zeroed")
        s_staged = signal("dve_qk_staged")
        s_turned = signal("pe_qk_turned")
        s_qt = signal("act_qt_ready")
        s_kt = signal("dve_kt_ready")
        s_score = signal("pe_scores")
        s_max = signal("dve_row_max")
        s_prob = signal("act_probs")
        s_pt = signal("pe_probs_turned")
        s_pta = signal("act_probs_taken")
        s_ptd = signal("dve_probs_taken")
        s_pv = signal("pe_values")
        s_out = signal("dve_heads_out")
        misc_dma = signal("misc_dma_landed")
        out_dma = signal("result_stored")
        s_diag = signal("dve_diagonals")
        s_gather = [signal(f"rows_gathered_{b}") for b in range(2)]
        s_scatter = signal("rows_scattered")
        s_xet = signal("pe_expert_rows_turned")
        s_gu = signal("pe_gate_up")
        s_act = signal("act_silu")
        s_hid = signal("dve_expert_hidden")
        s_ye = signal("dve_expert_out")
        normed_lg = signal("dve_logits_shifted")
        normed_aff = signal("dve_affinities")
        steps_d = Steps(ctx.enter_context(nc.semaphore("dve_steps")))
        steps_a = Steps(ctx.enter_context(nc.semaphore("act_steps")))
        steps_g = Steps(ctx.enter_context(nc.semaphore("pool_steps")))
        stage_end = {e: ctx.enter_context(nc.semaphore(f"{e}_stage_end")) for e in ("pe", "act", "dve", "pool")}
        x_spill = nc.dram_tensor("x_spill", (P, 8 * D), F32).ap()
        h2_dram = nc.dram_tensor("h2_rows", (1024, D), F32).ap()
        y_dram = nc.dram_tensor("y_rows", (1024, D), F32).ap()

        def dstep(dve, ins):
            steps_d.done(dve, ins)

        def astep(act, ins):
            steps_a.done(act, ins)

        def stat(a, b):
            return STAT[:, a:b]

        class Setup(Stage):

            def __init__(self):
                self.rows = area(0, 3, P)
                self.pos_i = sb("pos_i", [P, P], I32)
                self.mm = mm.span(1)
                self.nconst = 9
                self.sgu_raw = None

            def load(self, sp):
                sp.dma_start(IDENT[:, :], consts["ident"]).then_inc(consts_in.sem, 16)
                sp.dma_start(XC, A["ctx"][0].rearrange("(t p) d -> p t d", p=P)).then_inc(consts_in.sem, 16)
                sp.dma_start(ROPE[:, :, :], consts["rope"]).then_inc(consts_in.sem, 16)
                sp.dma_start(WMASK[:, :], consts["wmask"]).then_inc(consts_in.sem, 16)
                sp.dma_start(DFTF[:, :], consts["dftf"]).then_inc(consts_in.sem, 16)
                sp.dma_start(SINK[:, :, :], A["sink"].partition_broadcast(P)).then_inc(consts_in.sem, 16)
                sp.dma_start(INV[:, :], consts["inv"]).then_inc(consts_in.sem, 16)
                sp.dma_start(self.pos_i[ROW2_POS:ROW2_POS + 8, :],
                             A["positions_2"].rearrange("a (t p) -> (a t) p", p=P)).then_inc(consts_in.sem, 16)
                sp.dma_start(X[:, :, :], A["x"][0].rearrange("(t p) d -> p t d", p=P)).then_inc(consts_in.sem, 16)

            def pool(self, gp):
                nc.gpsimd.memset(ONES[:, :], 1.0).then_inc(ones_set.sem, 1)
                nc.gpsimd.memset(EPSC[:, :], EPS).then_inc(ones_set.sem, 1)
                nc.gpsimd.memset(self.rows, 0.0).then_inc(rows_zero.sem, 1)
                gp.wait_ge(rows_zero.sem, 1)

                def rows(l, r, src):
                    n = src.shape[0]
                    gp.dma_start(self.rows[r:r + n, l, :], src).then_inc(rows_in.sem, 16)
                    self.nrows += 1
                self.nrows = 0
                for l in range(2):
                    for r, name in ((ROW_ADA, "b_ada"), (ROW_PRE, "g_pre_mix"), (ROW_MIX, "g_mix"), (ROW_POST, "g_post_mix"),
                                    (ROW_FF, "g_pre_ff"), (ROW_POSTFF, "g_post_ff")):
                        rows(l, r, A[name][l].rearrange("(r p) -> r p", p=P))
                    rows(l, ROW_BSGU, A["b_sgu"][l])
                rows(0, ROW_C, A["c"][0].rearrange("(r p) -> r p", p=P))
                rows(0, ROW_CCTX, A["c_ctx"].rearrange("(r p) -> r p", p=P))
                for r, name in ((ROW_ADA, "b_ada_2"), (ROW2_MIX, "g_mix_2"), (ROW2_Q, "g_q_2"), (ROW2_KV, "g_kv_2"),
                                (ROW2_FFN, "g_ffn_2")):
                    rows(2, r, A[name][0].rearrange("(r p) -> r p", p=P))
                rows(2, ROW2_FINAL, A["g_final_2"].rearrange("(r p) -> r p", p=P))
                rows(1, ROW_C, A["c_2"][0].rearrange("(r p) -> r p", p=P))
                gp.wait_ge(rows_in.sem, 16 * self.nrows)

            def vector(self, dve):
                dve.wait_ge(consts_in.sem, 16 * self.nconst)
                dve.wait_ge(rows_zero.sem, 1)
                ins = nc.vector.tensor_copy(self.rows[ROW2_POS:ROW2_POS + 8, 2, :], self.pos_i[ROW2_POS:ROW2_POS + 8, :])
                dstep(dve, ins)
                dve.wait_ge(mm.sem, self.mm + 1)
                dstep(dve, nc.vector.tensor_copy(VEC[:, :, :], PS[:, 0, 0:384].rearrange("p (a b) -> p a b", a=3)))

            def tensor(self, pe):
                pe.wait_ge(consts_in.sem, 16 * self.nconst)
                pe.wait_ge(rows_in.sem, 16 * 23)
                pe.wait_ge(steps_d.sem, 1)
                for l in range(3):
                    last = nc.tensor.transpose(PS[:, 0, P * l:P * l + P], self.rows[:, l, :], IDENT[:, :])
                last.then_inc(mm.sem, 1)

            def scalar(self, act):
                act.wait_ge(steps_d.sem, 2)
                nc.scalar.activation(SC[:, 0, :], VEC[:, 0, ROW_C:ROW_C + 8], ACT.Silu)
                nc.scalar.activation(SC[:, 1, :], VEC[:, 0, ROW_CCTX:ROW_CCTX + 8], ACT.Silu)
                nc.scalar.activation(SC[:, 2, :], VEC[:, 1, ROW_C:ROW_C + 8], ACT.Silu)

        class Modulate(Stage):

            TURNS = 7

            def __init__(self, l):
                self.l = l
                self.nv = 2 if l < 2 else 1
                self.w = A["w_ada"][l] if l < 2 else A["w_ada_2"][0]
                self.rows = area(0, 12, BANK)
                self.blocks = ring.take(12)
                self.mm = mm.span(13)
                self.fd = freed_d.span(12)

            def load(self, sp):
                for b in range(12):
                    ring.load(sp, self.blocks + b, self.w[:, 512 * b:512 * b + 512].rearrange("(k p) n -> p k n", p=P), SLOT)

            def turn(self, pe, b):
                nv = self.nv
                pe.wait_ge(freed_d.sem, self.fd + b + 1)
                for j in range(4):
                    c = (4 * b + j) * 2
                    last = nc.tensor.transpose(PS[:, self.TURNS, c:c + nv], self.rows[0:nv, b, P * j:P * j + P],
                                               IDENT[0:nv, 0:nv])
                return last

            def tensor(self, pe):
                nv = self.nv
                for b in range(12):
                    ring.ready(pe, self.blocks + b)
                    w = ring.view(self.blocks + b, 8)
                    if b >= 7:
                        pe.wait_ge(freed_d.sem, self.fd + b - 6)
                    for k in range(8):
                        lhs = SC[:, 0:2, k] if nv == 2 else SC[:, 2, k:k + 1]
                        last = nc.tensor.matmul(PS[0:nv, b % 7, :], lhs, w[:, k, :], start=(k == 0), stop=(k == 7))
                    last.then_inc(mm.sem, 1)
                    pe.wait_ge(mm.sem, self.mm + b + 1)
                    pe.sem_inc(block_used.sem, 1)
                    if b:
                        self.turn(pe, b - 1)
                self.turn(pe, 11).then_inc(mm.sem, 1)

            def vector(self, dve):
                nv = self.nv
                for b in range(12):
                    dve.wait_ge(mm.sem, self.mm + b + 1)
                    nc.vector.tensor_copy(self.rows[0:nv, b, :], PS[0:nv, b % 7, :]).then_inc(freed_d.sem, 1)
                l = self.l
                dve.wait_ge(mm.sem, self.mm + 13)
                raw = PS[:, self.TURNS, 0:96].rearrange("p (j s) -> p j s", s=2)
                g1, g2 = (ROW_PRE, ROW_FF) if l < 2 else (ROW2_MIX, ROW2_FFN)
                for s in range(self.nv):
                    dstep(dve, nc.vector.tensor_tensor(MODC[:, s, :], raw[:, :, s], VEC[:, l, 0:48], ALU.add))
                    nc.vector.scalar_tensor_tensor(DER[:, s, 0, :], MODC[:, s, 8:16], 1.0, VEC[:, l, g1:g1 + 8],
                                                   ALU.add, ALU.mult)
                    nc.vector.scalar_tensor_tensor(DER[:, s, 1, :], MODC[:, s, 32:40], 1.0, VEC[:, l, g2:g2 + 8],
                                                   ALU.add, ALU.mult)
                    if l < 2:
                        nc.vector.tensor_tensor(DER[:, s, 2, :], MODC[:, s, 16:24], VEC[:, l, ROW_POST:ROW_POST + 8], ALU.mult)
                        nc.vector.tensor_tensor(DER[:, s, 3, :], MODC[:, s, 40:48], VEC[:, l, ROW_POSTFF:ROW_POSTFF + 8], ALU.mult)

        class Norm(Stage):

            def __init__(self, x, T, scale, shift, ht, xn, width=D, share=None):
                self.x, self.T, self.scale, self.shift, self.ht, self.xn = x, T, scale, shift, ht, xn
                self.K = width // P
                self.width = width
                self.H = max(1, T // 4)
                self.per = T // self.H
                self.G = self.H * self.K
                self.sq = squares.span(T)
                self.rt = roots.span(1)
                self.nm = normed.span(T)
                self.mm = mm.span(self.G)
                self.fa = freed_a.span((self.G + 1) // 2)
                self.fd = freed_d.span(self.G // 2)

            def scalar(self, act):
                T = self.T
                for t in range(T):
                    nc.scalar.activation(self.xn[:, t, :], self.x[:, t, 0:self.width], ACT.Square,
                                         accum_out=stat(t, t + 1)).then_inc(squares.sem, 1)
                act.wait_ge(squares.sem, self.sq + T)
                nc.scalar.activation(stat(8, 8 + T), stat(0, T), ACT.Sqrt, bias=EPSC[:, :],
                                     scale=1.0 / self.width).then_inc(roots.sem, 1)
                for g in range(0, self.G, 2):
                    h, c = g // self.K, g % self.K
                    n = self.per * P
                    act.wait_ge(mm.sem, self.mm + g + 1)
                    if self.shift is None:
                        ins = nc.scalar.activation(self.dst(c, h), PS[:, g % 8, 0:n], ACT.Copy, scale=self.scale[:, c:c + 1])
                    else:
                        ins = nc.scalar.activation(self.dst(c, h), PS[:, g % 8, 0:n], ACT.Identity, bias=self.shift[:, c:c + 1],
                                                   scale=self.scale[:, c:c + 1])
                    ins.then_inc(freed_a.sem, 1)

            def dst(self, c, h):
                n = self.per * P
                if isinstance(self.ht, list):
                    return self.ht[c][:, n * h:n * h + n]
                return self.ht[:, c, n * h:n * h + n]

            def vector(self, dve):
                T = self.T
                dve.wait_ge(roots.sem, self.rt + 1)
                dstep(dve, nc.vector.reciprocal(stat(16, 16 + T), stat(8, 8 + T)))
                for t in range(T):
                    nc.vector.tensor_scalar(self.xn[:, t, :], self.x[:, t, 0:self.width], stat(16 + t, 17 + t), None,
                                            ALU.mult).then_inc(normed.sem, 1)
                for g in range(1, self.G, 2):
                    h, c = g // self.K, g % self.K
                    n = self.per * P
                    dve.wait_ge(mm.sem, self.mm + g + 1)
                    if self.shift is not None:
                        ins = nc.vector.tensor_scalar(self.dst(c, h), PS[:, g % 8, 0:n], self.scale[:, c:c + 1],
                                                      self.shift[:, c:c + 1], ALU.mult, ALU.add)
                    else:
                        ins = nc.vector.tensor_scalar(self.dst(c, h), PS[:, g % 8, 0:n], self.scale[:, c:c + 1],
                                                      None, ALU.mult)
                    ins.then_inc(freed_d.sem, 1)

            def tensor(self, pe):
                for g in range(self.G):
                    h, c = g // self.K, g % self.K
                    pe.wait_ge(normed.sem, self.nm + self.per * (h + 1))
                    if g >= 8:
                        src, base = (freed_d, self.fd) if g % 2 else (freed_a, self.fa)
                        pe.wait_ge(src.sem, base + (g - 8) // 2 + 1)
                    for j in range(self.per):
                        t = self.per * h + j
                        last = nc.tensor.transpose(PS[:, g % 8, P * j:P * j + P], self.xn[:, t, P * c:P * c + P], IDENT[:, :])
                    last.then_inc(mm.sem, 1)

        class Product(Stage):

            def __init__(self, blocks, groups, K):
                self.src = blocks
                self.base = ring.take(len(blocks))
                self.groups = groups
                self.K = K
                self.mm = mm.span(len(groups))
                self.na = sum(1 for g in groups if g[3] == "act")
                self.nd = len(groups) - self.na
                self.fa = freed_a.span(self.na)
                self.fd = freed_d.span(self.nd)

            def load(self, sp):
                for b, (src, cols) in enumerate(self.src):
                    ring.load(sp, self.base + b, src, cols)

            def nth(self, g):
                return sum(1 for x in self.groups[:g + 1] if x[3] == self.groups[g][3])

            def tensor(self, pe):
                seen = -1
                for g, (b, ops, n, who, take) in enumerate(self.groups):
                    while seen < b:
                        if seen >= 0:
                            pass
                        seen += 1
                        ring.ready(pe, self.base + seen)
                    if g >= 8:
                        src, base = (freed_a, self.fa) if self.groups[g - 8][3] == "act" else (freed_d, self.fd)
                        pe.wait_ge(src.sem, base + self.nth(g - 8))
                    for k in range(self.K):
                        lhsT, rhs = ops(self.base + b, k)
                        last = nc.tensor.matmul(PS[:, g % 8, 0:n], lhsT, rhs, start=(k == 0), stop=(k == self.K - 1))
                    last.then_inc(mm.sem, 1)
                    if g + 1 == len(self.groups) or self.groups[g + 1][0] != b:
                        pe.drain().then_inc(block_used.sem, 1)

            def vector(self, dve):
                for g, (b, ops, n, who, take) in enumerate(self.groups):
                    if who == "dve":
                        dve.wait_ge(mm.sem, self.mm + g + 1)
                        take(nc.vector, PS[:, g % 8, 0:n]).then_inc(freed_d.sem, 1)

            def scalar(self, act):
                for g, (b, ops, n, who, take) in enumerate(self.groups):
                    if who == "act":
                        act.wait_ge(mm.sem, self.mm + g + 1)
                        take(nc.scalar, PS[:, g % 8, 0:n]).then_inc(freed_a.sem, 1)

        def to(dst):
            def take(eng, bank):
                if eng is nc.vector:
                    return nc.vector.tensor_copy(dst, bank)
                return nc.scalar.activation(dst, bank, ACT.Copy)
            return take

        def to_gelu(dst):
            def take(eng, bank):
                return nc.scalar.activation(dst, bank, ACT.Gelu_apprx_tanh)
            return take

        def rows_of(w, c0, c1):
            return w[:, c0:c1].rearrange("(k p) n -> p k n", p=P)

        def input_projection(l, T, px, ft):
            w = A["w_in"][l]
            groups = []

            def tok(t, c0, c1):
                return lambda n, k: (HT[:, k, P * t:P * t + P], ring.view(n, 8)[:, k, c0:c1])

            for t in range(T):
                groups.append((0, tok(t, 0, 512), 512, "act" if t % 2 else "dve", to(px[:, t, 0:512])))
            for t in range(T):
                groups.append((1, tok(t, 0, 256), 256, "dve", to(px[:, t, K0:U0])))
            for t in range(T):
                groups.append((1, tok(t, 256, 512), 256, "act", to_gelu(px[:, t, U0:G0])))
            for t in range(T):
                groups.append((2, tok(t, 0, 256), 256, "act", to_gelu(px[:, t, G0:F0])))
            H = max(1, T // 4)
            n = P * T // H
            for c in range(2):
                for h in range(H):
                    def feat(b, k, c=c, h=h):
                        return ring.view(b, 8)[:, k, 256 + P * c:256 + P * c + P], HT[:, k, n * h:n * h + n]
                    groups.append((2, feat, n, "dve", to(ft[:, c, n * h:n * h + n])))
            return Product([(rows_of(w, 512 * b, 512 * b + 512), SLOT) for b in range(3)], groups, KD)

        class Rope(Stage):

            def __init__(self, px, T):
                self.px, self.T = px, T
                self.t1 = area(0, 640)
                self.t2 = area(1024, 640)

            def vector(self, dve):
                for t in range(self.T):
                    x = self.px[:, t, 0:640]
                    cos = ROPE[:, 0, 64 * t:64 * t + 64].unsqueeze(1).broadcast_to([P, 10, 64])
                    rotate(dve, x.rearrange("p (h d) -> p h d", d=64), cos, ROPE[:, 1, 64 * t:64 * t + 64], 10, 2, 16,
                           self.t1, self.t2)

        def rotate(dve, x, cos, sin, heads, parts, half, t1, t2):
            w = parts * 2 * half
            a = t1[:, 0:heads * w].rearrange("p (h d) -> p h d", d=w)
            b = t2[:, 0:heads * w].rearrange("p (h d) -> p h d", d=w)
            nc.vector.tensor_tensor(a, x, cos, ALU.mult)
            for r in range(parts):
                for f in range(2):
                    lo, sw = (2 * r + f) * half, (2 * r + 1 - f) * half
                    s = sin[:, lo:lo + half].unsqueeze(1).broadcast_to([P, heads, half])
                    ins = nc.vector.tensor_tensor(b[:, :, lo:lo + half], x[:, :, sw:sw + half], s, ALU.mult)
            dstep(dve, ins)
            dstep(dve, nc.vector.tensor_tensor(x, a, b, ALU.add))

        class TurnKeys(Stage):

            def __init__(self, px, T, kt, c0, keep_v):
                self.px, self.T, self.kt, self.c0, self.keep_v = px, T, kt, c0, keep_v
                self.H = max(1, T // 4)
                self.per = T // self.H
                self.mm = mm.span(self.H)

            def tensor(self, pe):
                for h in range(self.H):
                    for j in range(self.per):
                        last = nc.tensor.transpose(PS[:, h, P * j:P * j + P],
                                                   self.px[:, self.per * h + j, self.c0:self.c0 + P], IDENT[:, :])
                    last.then_inc(mm.sem, 1)

            def vector(self, dve):
                n = self.per * P
                for h in range(self.H):
                    dve.wait_ge(mm.sem, self.mm + h + 1)
                    nc.vector.tensor_copy(self.kt[0:64, 0, n * h:n * h + n], PS[0:64, h, 0:n])
                    nc.vector.tensor_copy(self.kt[64:128, 1, n * h:n * h + n], PS[64:128, h, 0:n])
                    nc.vector.tensor_copy(self.kt[64:128, 0, n * h:n * h + n], PS[0:64, h, 0:n])
                    nc.vector.tensor_copy(self.kt[0:64, 1, n * h:n * h + n], PS[64:128, h, 0:n])
                if self.keep_v:
                    nc.vector.tensor_copy(VC[:, :, :], self.px[:, :, self.c0 + P:self.c0 + 2 * P])

        class Sgu(Stage):

            def __init__(self, l, px, T):
                self.l, self.px, self.T = l, px, T
                self.raw = area(0, 4, P)
                self.sq = area(2048, T, 256)
                self.vn = area(4096, T, 256)
                self.dma = misc_dma.span(32)
                self.mm = mm.span(5)
                self.rt = roots.span(1)
                self.nm = normed.span(3)

            def pool(self, gp):
                gp.dma_start(self.raw, A["w_sgu"][self.l].rearrange("h p q -> p h q")).then_inc(misc_dma.sem, 16)
                gp.dma_start(GSGU[:, :], A["g_sgu"][self.l].rearrange("h d -> (h d)").partition_broadcast(P)).then_inc(misc_dma.sem, 16)
                gp.wait_ge(misc_dma.sem, self.dma + 32)

            def tensor(self, pe):
                pe.wait_ge(misc_dma.sem, self.dma + 32)
                for h in range(4):
                    last = nc.tensor.transpose(PS[:, 0, P * h:P * h + P], self.raw[:, h, :], IDENT[:, :])
                last.then_inc(mm.sem, 1)
                pe.wait_ge(normed.sem, self.nm + 3)
                T = self.T
                for h in range(4):
                    nc.tensor.matmul(PS[:, 1 + h, 0:64 * T].rearrange("p (t d) -> p t d", d=64), WST[:, h, :],
                                     self.vn[:, :, 64 * h:64 * h + 64], start=True, stop=True).then_inc(mm.sem, 1)

            def scalar(self, act):
                act.wait_ge(normed.sem, self.nm + 1)
                nc.scalar.activation(stat(32, 32 + 4 * self.T), stat(0, 4 * self.T), ACT.Sqrt, bias=EPSC[:, :],
                                     scale=1.0 / 64).then_inc(roots.sem, 1)

            def vector(self, dve):
                T, px = self.T, self.px
                g = px[:, :, G0:F0]
                dve.wait_ge(misc_dma.sem, self.dma + 32)
                dve.wait_ge(mm.sem, self.mm + 1)
                nc.vector.tensor_copy(WST[:, :, :], PS[:, 0, :].rearrange("p (h q) -> p h q", h=4))
                dstep(dve, nc.vector.tensor_tensor(self.sq, g, g, ALU.mult))
                sq = self.sq.rearrange("p t (h d) -> p t h d", d=64)
                nc.vector.tensor_reduce(stat(0, 4 * T).rearrange("p (t h) -> p t h", h=4), sq, AX_X, ALU.add).then_inc(normed.sem, 1)
                dve.wait_ge(roots.sem, self.rt + 1)
                dstep(dve, nc.vector.reciprocal(stat(64, 64 + 4 * T), stat(32, 32 + 4 * T)))
                r = stat(64, 64 + 4 * T).rearrange("p (t h) -> p t h", h=4).unsqueeze(3).broadcast_to([P, T, 4, 64])
                nc.vector.tensor_tensor(self.vn.rearrange("p t (h d) -> p t h d", d=64),
                                        g.rearrange("p t (h d) -> p t h d", d=64), r, ALU.mult).then_inc(normed.sem, 1)
                dve.wait_ge(normed.sem, self.nm + 2)
                gb = GSGU[:, :].unsqueeze(1).broadcast_to([P, T, 256])
                nc.vector.tensor_tensor(self.vn, self.vn, gb, ALU.mult).then_inc(normed.sem, 1)
                for h in range(4):
                    dve.wait_ge(mm.sem, self.mm + 2 + h)
                    u = px[:, :, U0 + 64 * h:U0 + 64 * h + 64]
                    nc.vector.scalar_tensor_tensor(u, PS[:, 1 + h, 0:64 * T].rearrange("p (t d) -> p t d", d=64),
                                                   VEC[:, self.l, ROW_BSGU + h:ROW_BSGU + h + 1], u, ALU.add, ALU.mult)

        class Fourier(Stage):

            def __init__(self, px, ft, T):
                self.px, self.ft, self.T = px, ft, T
                self.fa_ = area(4096, T, 4, P)
                self.nb = max(1, T // 2)
                self.blocks = ring.take(self.nb)
                self.mm = mm.span(2 * T)
                self.fa = freed_a.span(T)
                self.fd = freed_d.span(T)
                self.scale = float(64 * T * P) ** -0.5

            def load(self, sp):
                for b in range(self.nb):
                    src = consts["dfts"][b] if self.T == 8 else consts["dftc"]
                    ring.load(sp, self.blocks + b, src, 512 * self.T)

            def tensor(self, pe):
                T = self.T
                for t in range(T):
                    for c in range(2):
                        last = nc.tensor.matmul(PS[:, t, 256 * c:256 * c + 256], self.ft[:, c, P * t:P * t + P], DFTF[:, :],
                                                start=True, stop=True)
                    last.then_inc(mm.sem, 1)
                for t in range(T):
                    b = t // 2
                    if t % 2 == 0:
                        ring.ready(pe, self.blocks + b)
                    w = self.wview(b)
                    pe.wait_ge(freed_d.sem, self.fd + T)
                    for k in range(T):
                        for f in range(2):
                            c0 = (t % 2) * P
                            last = nc.tensor.matmul(PS[:, t, 0:256].rearrange("p (c n) -> p c n", c=2),
                                                    w[:, 2 * k + f, c0:c0 + P],
                                                    self.fa_[:, k, f:4:2, :],
                                                    start=(k == 0 and f == 0), stop=(k == T - 1 and f == 1))
                    last.then_inc(mm.sem, 1)
                    if t % 2 == 1:
                        pe.drain().then_inc(block_used.sem, 1)

            def wview(self, b):
                return WB[:, (self.blocks + b) % RING, 0:512 * self.T].rearrange("p (a n) -> p a n", n=256)

            def vector(self, dve):
                for t in range(self.T):
                    dve.wait_ge(mm.sem, self.mm + t + 1)
                    nc.vector.tensor_copy(self.fa_[:, t, :, :], PS[:, t, :].rearrange("p (a b) -> p a b", a=4)).then_inc(freed_d.sem, 1)

            def scalar(self, act):
                for t in range(self.T):
                    act.wait_ge(mm.sem, self.mm + self.T + t + 1)
                    nc.scalar.activation(self.px[:, t, G0:F0], PS[:, t, 0:256], ACT.Copy, scale=self.scale).then_inc(freed_a.sem, 1)

        class Attention(Stage):

            def __init__(self, trips, heads, T, dim, scale, sq, qt, sbuf, pts, steps, sk=None, kt=None,
                         stage=None, stage_k=None, keys=None, values=None, out=None, local=None, ctx_keys=0,
                         sink=None, masked=False, wide=0):
                self.trips, self.heads, self.T, self.dim, self.scale = trips, heads, T, dim, scale
                self.sq, self.qt, self.sb, self.pts, self.sk, self.kt = sq, qt, sbuf, pts, sk, kt
                self.stage, self.stage_k, self.keys, self.values, self.out = stage, stage_k, keys, values, out
                self.local, self.ctx_keys, self.sink, self.masked, self.wide = local, ctx_keys, sink, masked, wide
                self.steps = steps
                self.U = heads * T
                n = trips * self.U
                self.b = {s: s.span(n) for s in (s_score, s_max, s_prob, s_pt, s_pta, s_ptd, s_pv, s_out)}
                self.c = {s: s.span(trips) for s in (s_staged, s_turned, s_qt, s_kt)}

            def at(self, s, i, u):
                return self.b[s] + i * self.U + u

            def blocks(self, t):
                lo, hi = self.local(t) if self.local else (0, 0)
                return lo, hi

            def widths(self, t):
                lo, hi = self.blocks(t)
                return P * (hi - lo), self.ctx_keys

            def units(self):
                return [(h, t) for h in range(self.heads) for t in range(self.T)]

            def turns(self):
                q = []
                packed = self.dim == 64
                n = self.heads // 2 if packed else self.heads
                w = P if packed else self.dim
                return n, w

            def tensor(self, pe):
                with pe.Fori(0, self.trips) as i:
                    n, w = self.turns()
                    pe.wait_ge(s_staged.sem, self.c[s_staged] + i + 1)
                    per = max(1, self.T * P // BANK)
                    for j in range(n):
                        for t in range(self.T):
                            c = j * self.T * P + t * P
                            last = nc.tensor.transpose(PS[0:w, c // BANK, c % BANK:c % BANK + P],
                                                       self.sq[:, t, w * j:w * j + w], IDENT[:, :])
                    if self.sk is not None:
                        for j in range(n):
                            for t in range(self.T):
                                c = 4 * BANK + j * self.T * P + t * P
                                last = nc.tensor.transpose(PS[0:w, c // BANK, c % BANK:c % BANK + P],
                                                           self.sk[:, t, w * j:w * j + w], IDENT[:, :])
                    last.then_inc(s_turned.sem, 1)
                    pe.wait_ge(s_qt.sem, self.c[s_qt] + i + 1)
                    pe.wait_ge(s_kt.sem, self.c[s_kt] + i + 1)
                    units = self.units()
                    U = self.U
                    for s in range(U + 2):
                        if s < U:
                            h, t = units[s]
                            if s >= 2:
                                pe.wait_ge(s_prob.sem, self.at(s_prob, i, s - 1))
                            q = self.query(h, t)
                            lw, cw = self.widths(t)
                            bank = 2 * (s % 2)
                            for dst, rhs in self.keys(h, t, PS[:, bank, :], PS[:, bank + 1, :]):
                                last = nc.tensor.matmul(dst, q, rhs, start=True, stop=True)
                            last.then_inc(s_score.sem, 1)
                        if 1 <= s <= U:
                            u = s - 1
                            h, t = units[u]
                            lw, cw = self.widths(t)
                            pe.wait_ge(s_prob.sem, self.at(s_prob, i, u + 1))
                            if u >= 1:
                                pe.wait_ge(s_pta.sem, self.at(s_pta, i, u))
                                pe.wait_ge(s_ptd.sem, self.at(s_ptd, i, u))
                            nb = (lw + cw) // P
                            for j in range(nb):
                                bank, c = (4, P * j) if j < nb // 2 else (5, P * (j - nb // 2))
                                last = nc.tensor.transpose(PS[:, bank, c:c + P],
                                                           self.sb[:, u % 2, P * j:P * j + P], IDENT[:, :])
                            last.then_inc(s_pt.sem, 1)
                        if s >= 2:
                            u = s - 2
                            h, t = units[u]
                            lw, cw = self.widths(t)
                            nb = (lw + cw) // P
                            pe.wait_ge(s_pta.sem, self.at(s_pta, i, u + 1))
                            pe.wait_ge(s_ptd.sem, self.at(s_ptd, i, u + 1))
                            if u >= 2:
                                pe.wait_ge(s_out.sem, self.at(s_out, i, u - 1))
                            for j in range(nb):
                                last = nc.tensor.matmul(PS[:, 6 + u % 2, 0:64], self.pts[:, u % 2, P * j:P * j + P],
                                                        self.values(i, h, t, j), start=(j == 0), stop=(j == nb - 1))
                            last.then_inc(s_pv.sem, 1)

            def query(self, h, t):
                if self.dim == 64:
                    b = 64 * (h % 2)
                    c = (h // 2) * self.T * P + t * P
                    return self.qt[b:b + 64, c:c + P]
                c = h * self.T * P + t * P
                return self.qt[0:self.dim, c:c + P]

            def split(self, t):
                lw, cw = self.widths(t)
                nb = (lw + cw) // P
                return P * (nb // 2), P * nb

            def scalar(self, act):
                with act.Fori(0, self.trips) as i:
                    n, w = self.turns()
                    act.wait_ge(s_turned.sem, self.c[s_turned] + i + 1)
                    cols = n * self.T * P
                    nbank = max(1, cols // BANK)
                    if cols >= BANK:
                        src = PS[0:w, 0:nbank, :]
                        dst = self.qt[0:w, 0:cols].rearrange("p (a b) -> p a b", b=BANK)
                    else:
                        src, dst = PS[0:w, 0, 0:cols], self.qt[0:w, 0:cols]
                    nc.scalar.activation(dst, src, ACT.Copy).then_inc(s_qt.sem, 1)
                    units = self.units()
                    U = self.U
                    for s in range(U + 1):
                        if s < U:
                            h, t = units[s]
                            u = s
                            lw, cw = self.widths(t)
                            act.wait_ge(s_max.sem, self.at(s_max, i, s + 1))
                            nm = STAT[:, 8 + u % 2:9 + u % 2]
                            den = 16 + 4 * (u % 2)
                            ops = []
                            if lw:
                                ops.append((self.sb[:, u % 2, 0:lw], self.sb[:, u % 2, 0:lw], 1.0))
                            if cw:
                                if self.local:
                                    src = PS[:, 2 * (u % 2) + 1, 0:cw]
                                    dst = self.sb[:, u % 2, lw:lw + cw]
                                elif cw > BANK:
                                    src = PS[:, 2 * (u % 2):2 * (u % 2) + 2, :]
                                    dst = self.sb[:, u % 2, 0:cw].rearrange("p (a b) -> p a b", b=BANK)
                                else:
                                    src = PS[:, 2 * (u % 2) + 1, 0:cw]
                                    dst = self.sb[:, u % 2, 0:cw]
                                ops.append((dst, src, self.scale))
                            if self.sink is not None:
                                ops.append((stat(den + 3, den + 4), stat(24 + h, 25 + h), 1.0))
                            for n_, (dst, src, sc) in enumerate(ops):
                                ins = nc.scalar.activation(dst, src, ACT.Exp, bias=nm, scale=sc,
                                                           accum_out=stat(den + n_, den + n_ + 1))
                            self.nden = len(ops)
                            ins.then_inc(s_prob.sem, 1)
                        if s >= 1:
                            u = s - 1
                            h, t = units[u]
                            a, b = self.split(t)
                            act.wait_ge(s_pt.sem, self.at(s_pt, i, u + 1))
                            if u >= 2:
                                act.wait_ge(s_pv.sem, self.at(s_pv, i, u - 1))
                            nc.scalar.activation(self.pts[:, u % 2, 0:a], PS[:, 4, 0:a], ACT.Copy).then_inc(s_pta.sem, 1)

            def vector(self, dve):
                nden = (1 if self.local or self.masked else 0) + (1 if self.ctx_keys else 0) + (1 if self.sink is not None else 0)
                with dve.Fori(0, self.trips) as i:
                    steps_d.loop(i, self.steps)
                    self.stage(i).then_inc(s_staged.sem, 1)
                    if self.stage_k:
                        self.stage_k(i).then_inc(s_kt.sem, 1)
                    else:
                        n, w = self.turns()
                        dve.wait_ge(s_turned.sem, self.c[s_turned] + i + 1)
                        cols = n * self.T * P
                        nc.vector.tensor_copy(self.kt[0:w, 0:cols].rearrange("p (a b) -> p a b", b=BANK),
                                              PS[0:w, 4:4 + cols // BANK, :]).then_inc(s_kt.sem, 1)
                    units = self.units()
                    U = self.U
                    for s in range(U + 2):
                        if s < U:
                            h, t = units[s]
                            u = s
                            lw, cw = self.widths(t)
                            mx, mc, nm = stat(0 + u % 2, 1 + u % 2), stat(2 + u % 2, 3 + u % 2), stat(8 + u % 2, 9 + u % 2)
                            mt = stat(4 + u % 2, 5 + u % 2)
                            dve.wait_ge(s_score.sem, self.at(s_score, i, s + 1))
                            bank = 2 * (u % 2)
                            if lw:
                                src, mask, dst = self.masked_rows(t, bank, u, lw)
                                dstep(dve, nc.vector.scalar_tensor_tensor(dst, src, self.scale, mask, ALU.mult, ALU.add))
                                dstep(dve, nc.vector.tensor_reduce(mx, self.sb[:, u % 2, 0:lw], AX_X, ALU.max))
                            if cw:
                                src = PS[:, bank:bank + 2, :] if cw > BANK else PS[:, bank + 1, 0:cw]
                                dstep(dve, nc.vector.tensor_reduce(mc, src, mybir.AxisListType.XY if cw > BANK else AX_X, ALU.max))
                            top = mx
                            if lw and cw:
                                dstep(dve, nc.vector.scalar_tensor_tensor(mt, mc, self.scale, mx, ALU.mult, ALU.max))
                                top, sc = mt, 1.0
                            elif cw:
                                top, sc = mc, self.scale
                            else:
                                top, sc = mx, 1.0
                            if self.sink is not None:
                                m2 = stat(6 + u % 2, 7 + u % 2)
                                dstep(dve, nc.vector.scalar_tensor_tensor(m2, top, sc, stat(24 + h, 25 + h), ALU.mult, ALU.max))
                                top, sc = m2, 1.0
                            nc.vector.tensor_scalar(nm, top, -sc, None, ALU.mult).then_inc(s_max.sem, 1)
                        if 1 <= s <= U:
                            u = s - 1
                            h, t = units[u]
                            a, b = self.split(t)
                            dve.wait_ge(s_pt.sem, self.at(s_pt, i, u + 1))
                            if u >= 2:
                                dve.wait_ge(s_pv.sem, self.at(s_pv, i, u - 1))
                            nc.vector.tensor_copy(self.pts[:, u % 2, a:b], PS[:, 5, 0:b - a]).then_inc(s_ptd.sem, 1)
                            den = 16 + 4 * (u % 2)
                            rd = stat(12 + u % 2, 13 + u % 2)
                            dv = stat(14 + u % 2, 15 + u % 2)
                            if nden > 1:
                                dstep(dve, nc.vector.reduce_sum(dv, stat(den, den + nden), AX_X))
                                dstep(dve, nc.vector.reciprocal(rd, dv))
                            else:
                                if u >= 2:
                                    dve.wait_ge(s_out.sem, self.at(s_out, i, u - 1))
                                dstep(dve, nc.vector.reciprocal(rd, stat(den, den + 1)))
                        if s >= 2:
                            u = s - 2
                            h, t = units[u]
                            dve.wait_ge(s_pv.sem, self.at(s_pv, i, u + 1))
                            nc.vector.tensor_scalar(self.out(i, h, t), PS[:, 6 + u % 2, 0:64],
                                                    stat(12 + u % 2, 13 + u % 2), None, ALU.mult).then_inc(s_out.sem, 1)
                    steps_d.loop_end(self.trips)

            def masked_rows(self, t, bank, u, lw):
                if self.wide:
                    src = PS[:, bank:bank + 2, :]
                    off = 896 - P * t
                    mask = self.masked[:, off:off + lw].rearrange("p (a b) -> p a b", b=BANK)
                    return src, mask, self.sb[:, u % 2, 0:lw].rearrange("p (a b) -> p a b", b=BANK)
                lo, hi = self.local(t)
                off = P * (lo - (t - 1))
                return PS[:, bank, 0:lw], self.masked[:, off:off + lw], self.sb[:, u % 2, 0:lw]

        def layer_attention(l, px, ft, T, window):
            kt2 = area(0, 2, 1024)
            sq = area(2048, T, 256)
            qt = area(4096, 2048)
            kts = area(6144, 1024)
            kcs = area(7168, 256)
            sbuf = area(2048, 2, 640)
            pts = ft[:, :, :].rearrange("p a b -> p (a b)")[:, 0:1280].rearrange("p (a b) -> p a b", a=2) if T == 8 else area(18432, 2, 256)
            if T != 8:
                sbuf = area(2048, 2, 256)

            def stage(i):
                nc.vector.tensor_copy(STAT[:, 24:28], SINK[:, l, bass.ts(i, 4)])
                return nc.vector.tensor_copy(sq, px[:, :, bass.ts(i, 256)])

            def stage_k(i):
                if window:
                    nc.vector.tensor_copy(kts.unsqueeze(1), kt2[:, bass.ts(i, 1), :])
                return nc.vector.tensor_copy(kcs.unsqueeze(1), KCT[:, bass.ts(i, 1), :])

            def local(t):
                return (max(t - 1, 0), min(t + 1, T - 1) + 1) if window else (0, 0)

            def keys(h, t, bank_a, bank_b):
                b = 64 * (h % 2)
                ops = []
                if window:
                    lo, hi = local(t)
                    ops.append((bank_a[:, 0:P * (hi - lo)], kts[b:b + 64, P * lo:P * hi]))
                ops.append((bank_b[:, 0:256], kcs[b:b + 64, :]))
                return ops

            def values(i, h, t, j):
                lo, hi = local(t)
                if j < hi - lo:
                    return px[:, lo + j, bass.ds(i * 64 + V0, 64)]
                return VC[:, j - (hi - lo), bass.ts(i, 64)]

            def out_(i, h, t):
                return px[:, t, bass.ds(i * 256 + 64 * h, 64)]

            return Attention(2, 4, T, 64, 0.125, sq, qt, sbuf, pts, steps=32 * 7 if window else 8 * 4,
                             stage=stage, stage_k=stage_k, keys=keys, values=values, out=out_, local=local if window else None,
                             ctx_keys=256, sink=SINK, masked=WMASK if window else False)

        class MergeNorm(Stage):

            def __init__(self, px, T):
                self.px, self.T = px, T
                self.parts = ((0, 512), (U0, G0), (G0, F0))
                self.sq = squares.span(3)
                self.rt = roots.span(2)
                self.junk = area(0, T, D)

            def scalar(self, act):
                T = self.T
                for p_, (a, b) in enumerate(self.parts):
                    o = (0, 512, 768)[p_]
                    for t in range(T):
                        ins = nc.scalar.activation(self.junk[:, t, o:o + b - a], self.px[:, t, a:b], ACT.Square,
                                                   accum_out=stat(8 * p_ + t, 8 * p_ + t + 1))
                    ins.then_inc(squares.sem, 1)
                act.wait_ge(squares.sem, self.sq + 3)
                nc.scalar.activation(stat(32, 32 + T), stat(0, T), ACT.Sqrt, bias=EPSC[:, :], scale=1.0 / 512).then_inc(roots.sem, 1)
                for p_ in (1, 2):
                    ins = nc.scalar.activation(stat(32 + 8 * p_, 32 + 8 * p_ + T), stat(8 * p_, 8 * p_ + T), ACT.Sqrt, bias=EPSC[:, :],
                                               scale=1.0 / 256)
                ins.then_inc(roots.sem, 1)

            def vector(self, dve):
                T = self.T
                dve.wait_ge(roots.sem, self.rt + 2)
                for p_ in range(3):
                    ins = nc.vector.reciprocal(stat(64 + 8 * p_, 64 + 8 * p_ + T), stat(32 + 8 * p_, 32 + 8 * p_ + T))
                dstep(dve, ins)
                for p_, (a, b) in enumerate(self.parts):
                    for t in range(T):
                        nc.vector.tensor_scalar(self.px[:, t, a:b], self.px[:, t, a:b], stat(64 + 8 * p_ + t, 65 + 8 * p_ + t),
                                                None, ALU.mult)

        class Turn(Stage):

            def __init__(self, T, src, dst, gain):
                self.T, self.src, self.dst, self.gain = T, src, dst, gain
                self.H = max(1, T // 4)
                self.per = T // self.H
                self.G = self.H * KD
                self.mm = mm.span(self.G)
                self.fa = freed_a.span(self.G // 2)
                self.fd = freed_d.span(self.G // 2)

            def tensor(self, pe):
                for g in range(self.G):
                    h, c = g // KD, g % KD
                    if g >= 8:
                        src, base = (freed_d, self.fd) if g % 2 else (freed_a, self.fa)
                        pe.wait_ge(src.sem, base + (g - 8) // 2 + 1)
                    for j in range(self.per):
                        last = nc.tensor.transpose(PS[:, g % 8, P * j:P * j + P], self.src(self.per * h + j, c), IDENT[:, :])
                    last.then_inc(mm.sem, 1)

            def scalar(self, act):
                n = self.per * P
                for g in range(0, self.G, 2):
                    h, c = g // KD, g % KD
                    act.wait_ge(mm.sem, self.mm + g + 1)
                    nc.scalar.activation(self.dst(c, n * h, n * h + n), PS[:, g % 8, 0:n], ACT.Copy,
                                         scale=self.gain[:, c:c + 1] if self.gain is not None else 1.0).then_inc(freed_a.sem, 1)

            def vector(self, dve):
                n = self.per * P
                for g in range(1, self.G, 2):
                    h, c = g // KD, g % KD
                    dve.wait_ge(mm.sem, self.mm + g + 1)
                    if self.gain is not None:
                        ins = nc.vector.tensor_scalar(self.dst(c, n * h, n * h + n), PS[:, g % 8, 0:n], self.gain[:, c:c + 1], None, ALU.mult)
                    else:
                        ins = nc.vector.tensor_copy(self.dst(c, n * h, n * h + n), PS[:, g % 8, 0:n])
                    ins.then_inc(freed_d.sem, 1)

        class Spread(Stage):

            def __init__(self, col, dst, scratch, copy_to=None):
                self.col, self.dst, self.dg = col, dst, scratch
                self.mm = mm.span(1)
                self.sd = s_diag.span(1)

            def vector(self, dve):
                for c in range(8):
                    ins = nc.vector.tensor_scalar(self.dg[:, P * c:P * c + P], IDENT[:, :], self.col[:, c:c + 1], None, ALU.mult)
                ins.then_inc(s_diag.sem, 1)
                dve.wait_ge(mm.sem, self.mm + 1)
                nc.vector.tensor_copy(self.dst.rearrange("p (a b) -> p a b", b=BANK), PS[:, 0:2, :])

            def tensor(self, pe):
                pe.wait_ge(s_diag.sem, self.sd + 1)
                for n in range(2):
                    last = nc.tensor.matmul(PS[:, n, :], ONES[:, :], self.dg[:, 512 * n:512 * n + 512], start=True, stop=True)
                last.then_inc(mm.sem, 1)

        class OutProduct(Stage):

            def __init__(self, w, mt, x, T, rms, scratch):
                self.w, self.mt, self.x, self.T, self.rms = w, mt, x, T, rms
                self.blocks = ring.take(2)
                self.mm = mm.span(T)
                self.sq = squares.span(T if rms else 0)
                self.rt = roots.span(T if rms else 0)
                self.fd = freed_d.span(T)
                self.tmp = scratch
                self.junk = scratch[:, 2048:3072]

            def load(self, sp):
                for b in range(2):
                    ring.load(sp, self.blocks + b, rows_of(self.w, 512 * b, 512 * b + 512), SLOT)

            def banks(self, t):
                return PS[:, 2 * (t % 4):2 * (t % 4) + 2, :]

            def tensor(self, pe):
                for b in range(2):
                    ring.ready(pe, self.blocks + b)
                for t in range(self.T):
                    if t >= 4:
                        pe.wait_ge(freed_d.sem, self.fd + t - 3)
                    for b in range(2):
                        for k in range(KD):
                            last = nc.tensor.matmul(self.banks(t)[:, b, :], self.mt[:, k, P * t:P * t + P],
                                                    ring.view(self.blocks + b, 8)[:, k, :], start=(k == 0), stop=(k == KD - 1))
                    last.then_inc(mm.sem, 1)
                pe.drain().then_inc(block_used.sem, 2)

            def scalar(self, act):
                if not self.rms:
                    return
                for t in range(self.T):
                    act.wait_ge(mm.sem, self.mm + t + 1)
                    nc.scalar.activation(self.junk.rearrange("p (a b) -> p a b", b=BANK), self.banks(t), ACT.Square,
                                         accum_out=stat(t, t + 1)).then_inc(squares.sem, 1)
                    act.wait_ge(squares.sem, self.sq + t + 1)
                    nc.scalar.activation(stat(8 + t, 9 + t), stat(t, t + 1), ACT.Sqrt, bias=EPSC[:, :], scale=1.0 / D).then_inc(roots.sem, 1)

            def vector(self, dve):
                gate = GATE[:, :].rearrange("p (a b) -> p a b", b=BANK)
                for t in range(self.T):
                    tmp = self.tmp[:, 1024 * (t % 2):1024 * (t % 2) + 1024]
                    tv = tmp.rearrange("p (a b) -> p a b", b=BANK)
                    if self.rms:
                        dve.wait_ge(roots.sem, self.rt + t + 1)
                        dstep(dve, nc.vector.reciprocal(stat(16 + t, 17 + t), stat(8 + t, 9 + t)))
                        ins = nc.vector.scalar_tensor_tensor(tv, self.banks(t), stat(16 + t, 17 + t), gate, ALU.mult, ALU.mult)
                    else:
                        dve.wait_ge(mm.sem, self.mm + t + 1)
                        ins = nc.vector.tensor_tensor(tv, self.banks(t), gate, ALU.mult)
                    ins.then_inc(freed_d.sem, 1)
                    dve.wait_ge(freed_d.sem, self.fd + t + 1)
                    nc.vector.tensor_tensor(self.x[:, t, :], self.x[:, t, :], tmp, ALU.add)

        class Mlp(Stage):

            def __init__(self, l, T, acc, hid):
                self.l, self.T, self.acc, self.hid = l, T, acc, hid
                self.H = max(1, T // 4)
                self.N = P * T // self.H
                self.G = 4 * self.H + 2 * T
                assert self.G % 8 == 0
                self.trips = FF // 1024
                self.blocks = ring.take(4 * self.trips)
                self.mm = mm.span(2 * self.G * self.trips)
                assert freed_d.planned >= 8
                self.fd = freed_d.span(2 * self.G * self.trips)
                self.hd = hid_done.span(8 * self.H * self.trips)
                self.z = zeroed.span(1)

            def load(self, sp):
                w1, w2 = A["w_ff1"][self.l], A["w_ff2"][self.l]
                with sp.Fori(0, self.trips) as i:
                    for b in range(2):
                        c = i * 1024 + 512 * b
                        ring.load(sp, self.blocks + 2 * b, w1[:, bass.ds(c, 512)].rearrange("(k p) n -> p k n", p=P), SLOT, more=4 * i)
                        ring.load(sp, self.blocks + 2 * b + 1, w2[bass.ds(c, 512), :].rearrange("(k p) n -> p k n", p=P), SLOT, more=4 * i)

            def groups(self):
                g = [("hid", c, h) for h in range(self.H) for c in range(4)]
                return g + [("out", t, n) for t in range(self.T) for n in range(2)]

            def tensor(self, pe):
                G, H = self.G, self.H
                with pe.Fori(0, self.trips) as i:
                    for b in range(2):
                        n1 = self.blocks + 2 * b
                        w1, w2 = ring.view(n1, 8), ring.view(n1 + 1, 4)
                        for m, (kind, x, y) in enumerate(self.groups()):
                            g = b * G + m
                            if m == 0:
                                ring.ready(pe, n1, i, 4)
                            if m == 4 * H:
                                ring.ready(pe, n1 + 1, i, 4)
                            pe.wait_ge(freed_d.sem, self.fd + i * 2 * G + g - 7)
                            if kind == "hid":
                                for k in range(KD):
                                    last = nc.tensor.matmul(PS[:, g % 8, 0:self.N], w1[:, k, P * x:P * x + P],
                                                            HT[:, k, self.N * y:self.N * y + self.N], start=(k == 0), stop=(k == KD - 1))
                                last.then_inc(mm.sem, 1)
                                if m == 4 * H - 1:
                                    pe.drain().then_inc(block_used.sem, 1)
                            else:
                                h = x * P // self.N
                                if y == 0 and (x * P) % self.N == 0:
                                    pe.wait_ge(hid_done.sem, self.hd + i * 8 * H + b * 4 * H + 4 * (h + 1))
                                for k in range(4):
                                    last = nc.tensor.matmul(PS[:, g % 8, :], self.hid[:, k, P * x:P * x + P],
                                                            w2[:, k, 512 * y:512 * y + 512], start=(k == 0), stop=(k == 3))
                                last.then_inc(mm.sem, 1)
                        pe.drain().then_inc(block_used.sem, 1)

            def pool(self, gp):
                nc.gpsimd.memset(self.acc, 0.0).then_inc(zeroed.sem, 1)

            def vector(self, dve):
                G, H = self.G, self.H
                dve.wait_ge(zeroed.sem, self.z + 1)
                with dve.Fori(0, self.trips) as i:
                    for b in range(2):
                        for m, (kind, x, y) in enumerate(self.groups()):
                            g = b * G + m
                            dve.wait_ge(mm.sem, self.mm + i * 2 * G + g + 1)
                            if kind == "hid":
                                nc.vector.tensor_scalar(self.hid[:, x, self.N * y:self.N * y + self.N], PS[:, g % 8, 0:self.N], 0.0, None,
                                                        ALU.max).then_inc(freed_d.sem, 1)
                            else:
                                a = self.acc[:, x, 512 * y:512 * y + 512]
                                if x == 0 and y == 0:
                                    dve.wait_ge(freed_d.sem, self.fd + i * 2 * G + g - 4 * H)
                                nc.vector.tensor_tensor(a, a, PS[:, g % 8, :], ALU.add).then_inc(freed_d.sem, 1)

            def scalar(self, act):
                G, H = self.G, self.H
                with act.Fori(0, self.trips) as i:
                    for b in range(2):
                        for m, (kind, x, y) in enumerate(self.groups()):
                            if kind == "hid":
                                act.wait_ge(freed_d.sem, self.fd + i * 2 * G + b * G + m + 1)
                                v = self.hid[:, x, self.N * y:self.N * y + self.N]
                                nc.scalar.activation(v, v, ACT.Square).then_inc(hid_done.sem, 1)

        class AddNormed(Stage):

            def __init__(self, x, T, acc, junk):
                self.x, self.T, self.acc, self.junk = x, T, acc, junk
                self.sq = squares.span(T)
                self.rt = roots.span(1)

            def scalar(self, act):
                T = self.T
                for t in range(T):
                    nc.scalar.activation(self.junk[:, t, :], self.acc[:, t, :], ACT.Square, accum_out=stat(t, t + 1)).then_inc(squares.sem, 1)
                act.wait_ge(squares.sem, self.sq + T)
                nc.scalar.activation(stat(8, 8 + T), stat(0, T), ACT.Sqrt, bias=EPSC[:, :], scale=1.0 / D).then_inc(roots.sem, 1)

            def vector(self, dve):
                T = self.T
                dve.wait_ge(roots.sem, self.rt + 1)
                dstep(dve, nc.vector.reciprocal(stat(16, 16 + T), stat(8, 8 + T)))
                for t in range(T):
                    a = self.acc[:, t, :]
                    dstep(dve, nc.vector.scalar_tensor_tensor(a, a, stat(16 + t, 17 + t), GATE[:, :], ALU.mult, ALU.mult))
                    nc.vector.tensor_tensor(self.x[:, t, :], self.x[:, t, :], a, ALU.add)

        def layer_stream(l, s, x, T):
            px = area(8192, T, 1280)
            ft = area(18432, 2, 1024) if T == 8 else area(16384, 2, 256)
            xn = area(8192, T, D)
            kt = area(0, 2, 1024) if T == 8 else KCT
            st = [Norm(x, T, DER[:, s, 0, :], MODC[:, s, 0:8], HT, xn),
                  input_projection(l, T, px, ft)]
            if T == 8:
                st.append(Rope(px, T))
            st += [Sgu(l, px, T), Fourier(px, ft, T), TurnKeys(px, T, kt, K0, T == 2),
                   layer_attention(l, px, ft, T, T == 8), MergeNorm(px, T)]

            def mixed(t, c):
                a = P * c if c < 4 else U0 + P * (c - 4)
                return px[:, t, a:a + P]

            st += [Turn(T, mixed, lambda c, a, b: HT[:, c, a:b], VEC[:, l, ROW_MIX:ROW_MIX + 8]),
                   Spread(DER[:, s, 2, :], GATE[:, :], area(8192, 1024)),
                   OutProduct(A["w_out"][l], HT, x, T, True, area(8192, 4096)),
                   Norm(x, T, DER[:, s, 1, :], MODC[:, s, 24:32], HT, xn),
                   Spread(DER[:, s, 3, :], GATE[:, :], area(8192, 1024)),
                   Mlp(l, T, area(8192, T, D), area(16384, 4, P * T)),
                   AddNormed(x, T, area(8192, T, D), area(0, T, D))]
            return st

        def context_kv(l):
            px = area(8192, 2, 256)
            groups = [(0, (lambda n, k, t=t: (HT[:, k, P * t:P * t + P], WB[:, n % RING, 0:2048].rearrange("p (k n) -> p k n", k=8)[:, k, :])),
                       256, "dve", to(px[:, t, :])) for t in range(2)]
            return [Norm(XC, 2, DER[:, 1, 0, :], MODC[:, 1, 0:8], HT, area(10240, 2, D)),
                    Product([(rows_of(A["w_in"][l], K0, U0), 2048)], groups, KD),
                    TurnKeys(px, 2, KCT, 0, True)]

        class Rotations(Stage):

            def __init__(self):
                self.d = misc_dma.span(16)
                self.rt = roots.span(1)

            def pool(self, gp):
                gp.dma_start(x_spill, XF).then_inc(misc_dma.sem, 16)
                gp.wait_ge(misc_dma.sem, self.d + 16)

            def vector(self, dve):
                ang, k, k2 = area(0, 8, 24), area(192, 8, 24), area(384, 8, 24)
                pos = VEC[:, 2, ROW2_POS:ROW2_POS + 8].unsqueeze(2).broadcast_to([P, 8, 24])
                dstep(dve, nc.vector.tensor_tensor(ang, pos, INV[:, :].unsqueeze(1).broadcast_to([P, 8, 24]), ALU.mult))
                magic = 12582912.0
                for quarter, r in ((0, area(576, 8, 24)), (1, area(768, 8, 24))):
                    dstep(dve, nc.vector.tensor_scalar(k, ang, 0.15915494309189535, 0.25 * quarter, ALU.mult, ALU.add))
                    dstep(dve, nc.vector.tensor_scalar(k2, k, magic, None, ALU.add))
                    dstep(dve, nc.vector.tensor_scalar(k, k2, -magic, None, ALU.add))
                    dstep(dve, nc.vector.scalar_tensor_tensor(k2, k, -6.28125, ang, ALU.mult, ALU.add))
                    dstep(dve, nc.vector.scalar_tensor_tensor(r, k, -0.0019350051879882812, k2, ALU.mult, ALU.add))
                    dstep(dve, nc.vector.scalar_tensor_tensor(k2, k, -3.0199159819532e-07, r, ALU.mult, ALU.add))
                    dstep(dve, nc.vector.tensor_scalar(r, k2, 1.5707963267948966 * quarter, 3.1415925, ALU.add, ALU.min))
                    ins = nc.vector.tensor_scalar(r, r, -3.1415925, None, ALU.max)
                    dstep(dve, ins)
                ins = nc.vector.tensor_copy(stat(0, 1), stat(0, 1))
                ins.then_inc(roots.sem, 1)

            def scalar(self, act):
                act.wait_ge(roots.sem, self.rt + 1)
                sin, cos = area(576, 8, 24), area(768, 8, 24)
                for src, c0, half, at, signs in ((cos, 0, 16, 0, (1.0, 1.0)), (sin, 0, 16, 32, (-1.0, 1.0)),
                                                 (cos, 16, 8, 64, (1.0, 1.0)), (sin, 16, 8, 80, (-1.0, 1.0))):
                    for j, sign in enumerate(signs):
                        nc.scalar.activation(ROPE2[:, :, at + half * j:at + half * j + half], src[:, :, c0:c0 + half], ACT.Sin, scale=sign)

        class RotateHeads(Stage):

            def __init__(self, xs, at, w, heads, table, keep=None):
                self.xs, self.at, self.w, self.heads, self.table, self.keep = xs, at, w, heads, table, keep

            def vector(self, dve):
                w = self.w
                for t in range(8):
                    cos = ROPE2[:, t, self.table:self.table + w].unsqueeze(1).broadcast_to([P, self.heads, w])
                    sin = ROPE2[:, t, self.table + w:self.table + 2 * w]
                    for x in self.xs:
                        rotate(dve, x[:, t, :, self.at:self.at + w], cos, sin, self.heads, 1, w // 2, xarea(7000, 512), xarea(7600, 512))

        class LoadTable(Stage):
            def __init__(self, dst, src):
                self.dst, self.src = dst, src
                self.d = misc_dma.span(16)

            def pool(self, gp):
                gp.dma_start(self.dst, self.src).then_inc(misc_dma.sem, 16)
                gp.wait_ge(misc_dma.sem, self.d + 16)

        class Copy(Stage):
            def __init__(self, dst, src):
                self.dst, self.src = dst, src

            def vector(self, dve):
                nc.vector.tensor_copy(self.dst, self.src)

        class Rows(Stage):

            def __init__(self, xn, scale, shift, zero):
                self.xn, self.scale, self.shift, self.zero = xn, scale, shift, zero
                self.nm = normed.span(8)
                self.d = out_dma.span(16)
                self.z = zeroed.span(1)
                self.s = s_scatter.span(48)

            def vector(self, dve):
                for t in range(8):
                    x = self.xn[:, t, :]
                    dstep(dve, nc.vector.tensor_tensor(x, x, self.scale, ALU.mult))
                    nc.vector.tensor_tensor(x, x, self.shift, ALU.add).then_inc(normed.sem, 1)

            def scalar(self, act):
                act.wait_ge(normed.sem, self.nm + 8)
                act.dma_start(h2_dram.rearrange("(t p) d -> p t d", p=P), self.xn).then_inc(out_dma.sem, 16)
                act.wait_ge(out_dma.sem, self.d + 16)

            def pool(self, gp):
                nc.gpsimd.memset(self.zero, 0.0).then_inc(zeroed.sem, 1)
                gp.wait_ge(zeroed.sem, self.z + 1)
                gp.dma_start(y_dram.rearrange("(t p) d -> p t d", p=P),
                             self.zero.unsqueeze(1).broadcast_to([P, 8, D])).then_inc(s_scatter.sem, 48)
                gp.wait_ge(s_scatter.sem, self.s + 48)

        class Route(Stage):

            def __init__(self, off):
                self.wr = area(off, 8, N_EXP)
                self.br = area(off + 128, N_EXP)
                self.lg = area(off + 144, 8, N_EXP)
                self.ex = area(off + 272, 8, N_EXP)
                self.aff = area(off + 400, 8, N_EXP)
                self.top = area(off + 528, 8)
                self.iota = area(off + 640, P)
                self.tok = area(off + 768, 8)
                self.pos = area(off + 776, N_EXP, 8)
                self.pair = area(off + 904, N_EXP, 8, 2)
                self.at = area(off + 2048, 1024)[0:N_EXP]
                self.work = area(off + 3072, 1024)[0:N_EXP]
                self.mask = area(off + 4096, 1024)[0:N_EXP]
                self.cum = area(off + 5120, 1024)[0:N_EXP]
                self.hot = [area(off + 6144 + 1024 * b, 8, P) for b in range(2)]
                self.d = misc_dma.span(32)
                self.mm = mm.span(3)
                self.rt = roots.span(1)
                self.z = zeroed.span(2)
                self.hotd = s_diag.span(N_EXP)
                self.used = s_turned.span(N_EXP)

            def pool(self, gp):
                with nc.allow_non_contiguous_dma(reason="16 columns of the router"):
                    gp.dma_start(self.wr, A["w_router_2"][0].rearrange("(k p) e -> p k e", p=P)).then_inc(misc_dma.sem, 16)
                gp.dma_start(self.br, A["b_router_2"][0].partition_broadcast(P)).then_inc(misc_dma.sem, 16)
                nc.gpsimd.iota(IOTA_I[:, 0:P], [[1, P]], base=0, channel_multiplier=0).then_inc(zeroed.sem, 1)
                nc.gpsimd.iota(IOTA_I[:, P:P + 8], [[P, 8]], base=0, channel_multiplier=1).then_inc(zeroed.sem, 1)
                gp.wait_ge(misc_dma.sem, self.d + 32)

            def tensor(self, pe):
                pe.wait_ge(misc_dma.sem, self.d + 32)
                for t in range(8):
                    for k in range(8):
                        last = nc.tensor.matmul(PS[:, 0, N_EXP * t:N_EXP * t + N_EXP], HT[:, k, P * t:P * t + P], self.wr[:, k, :],
                                                start=(k == 0), stop=(k == 7))
                last.then_inc(mm.sem, 1)
                pe.wait_ge(normed_aff.sem, 1)
                for t in range(8):
                    last = nc.tensor.transpose(PS[0:N_EXP, 1 + t // 4, P * (t % 4):P * (t % 4) + P], self.aff[:, t, :], IDENT[:, :])
                last.then_inc(mm.sem, 1)
                pe.wait_ge(normed_aff.sem, 2)
                for t in range(8):
                    last = nc.tensor.transpose(PS[:, 3, N_EXP * t:N_EXP * t + N_EXP], self.cum[:, P * t:P * t + P],
                                               IDENT[0:N_EXP, 0:N_EXP])
                last.then_inc(mm.sem, 1)
                with pe.Fori(0, N_EXP // 2) as i:
                    for b in range(2):
                        pe.wait_ge(s_diag.sem, self.hotd + 2 * i + b + 1)
                        for t in range(8):
                            last = nc.tensor.matmul(PS[:, 4, bass.ds(i * 4 + 2 * b, 2)], self.hot[b][:, t, :],
                                                    self.pair[:, bass.ds(i * 2 + b, 1), t, :], start=(t == 0), stop=(t == 7))
                        last.then_inc(s_turned.sem, 1)

            def scalar(self, act):
                act.wait_ge(normed_lg.sem, 1)
                nc.scalar.activation(self.ex, self.lg, ACT.Exp).then_inc(roots.sem, 1)

            def vector(self, dve):
                dve.wait_ge(misc_dma.sem, self.d + 32)
                dve.wait_ge(mm.sem, self.mm + 1)
                lg, top = self.lg, self.top
                dstep(dve, nc.vector.tensor_tensor(lg, PS[:, 0, 0:P].rearrange("p (t e) -> p t e", e=N_EXP),
                                                   self.br.unsqueeze(1).broadcast_to([P, 8, N_EXP]), ALU.add))
                dstep(dve, nc.vector.tensor_reduce(top, lg, AX_X, ALU.max))
                nc.vector.tensor_tensor(lg, lg, top.unsqueeze(2).broadcast_to([P, 8, N_EXP]), ALU.subtract).then_inc(normed_lg.sem, 1)
                dve.wait_ge(roots.sem, self.rt + 1)
                dstep(dve, nc.vector.tensor_reduce(stat(0, 8), self.ex, AX_X, ALU.add))
                dstep(dve, nc.vector.reciprocal(stat(8, 16), stat(0, 8)))
                nc.vector.tensor_tensor(self.aff, self.ex, stat(8, 16).unsqueeze(2).broadcast_to([P, 8, N_EXP]),
                                        ALU.mult).then_inc(normed_aff.sem, 1)
                dve.wait_ge(mm.sem, self.mm + 2)
                dstep(dve, nc.vector.tensor_copy(self.at.rearrange("p (a b) -> p a b", b=BANK), PS[0:N_EXP, 1:3, :]))
                best = stat(16, 24)[0:N_EXP]
                for r in range(CAP // 8):
                    src = self.at if r == 0 else self.work
                    dstep(dve, nc.vector.max(best, src))
                    dstep(dve, nc.vector.match_replace(self.work, best, src, -1.0))
                dstep(dve, nc.vector.tensor_tensor(self.mask, self.work, self.at, ALU.not_equal))
                dstep(dve, nc.vector.memset(self.work, 1.0))
                dstep(dve, nc.vector.tensor_tensor_scan(self.cum, self.work, self.mask, 0.0, ALU.mult, ALU.add))
                dstep(dve, nc.vector.tensor_tensor(self.cum, self.cum, self.mask, ALU.mult))
                nc.vector.tensor_scalar(self.cum, self.cum, -1.0, None, ALU.add).then_inc(normed_aff.sem, 1)
                dve.wait_ge(zeroed.sem, self.z + 2)
                nc.vector.tensor_copy(self.iota, IOTA_I[:, 0:P])
                dstep(dve, nc.vector.tensor_copy(self.tok, IOTA_I[:, P:P + 8]))
                nc.vector.tensor_copy(self.pair[:, :, :, 0], self.tok.unsqueeze(1).broadcast_to([P, N_EXP, 8]))
                nc.vector.tensor_copy(self.pair[:, :, :, 1], self.aff.rearrange("p t e -> p e t"))
                dve.wait_ge(mm.sem, self.mm + 3)
                dstep(dve, nc.vector.tensor_copy(self.pos, PS[:, 3, 0:P].rearrange("p (t e) -> p e t", e=N_EXP)))
                with dve.Fori(0, N_EXP // 2) as i:
                    for b in range(2):
                        dve.wait_ge(s_turned.sem, self.used + 2 * i + b - 1)
                        for t in range(8):
                            ins = nc.vector.tensor_scalar(self.hot[b][:, t, :], self.iota, self.pos[:, bass.ds(i * 2 + b, 1), t], None,
                                                          ALU.is_equal)
                        ins.then_inc(s_diag.sem, 1)
                dve.wait_ge(s_turned.sem, self.used + N_EXP)
                pairs = PS[:, 4, 0:2 * N_EXP].rearrange("p (e a) -> p e a", a=2)
                nc.vector.tensor_copy(IDX[:, :], pairs[:, :, 0])
                nc.vector.tensor_copy(GT[:, :], pairs[:, :, 1])

        class Experts(Stage):

            def __init__(self):
                self.xe = [area(1024 * b, 1024) for b in range(2)]
                self.xet = [area(2048 + 1024 * b, 8, P) for b in range(2)]
                self.sa = [area(4096 + 1024 * b, 1024) for b in range(2)]
                self.hg = [area(6144 + 1024 * b, 1024) for b in range(2)]
                self.hgt = [area(8192 + 1024 * b, 8, P) for b in range(2)]
                self.ye = [area(10240 + 1024 * b, 1024) for b in range(2)]
                self.blocks = ring.take(6 * N_EXP)
                self.b = {s: s.span(k) for s, k in ((s_scatter, 16 * N_EXP), (s_pt, 2 * N_EXP), (s_xet, N_EXP), (s_pta, 2 * N_EXP),
                                                    (s_ptd, 2 * N_EXP), (s_gu, 4 * N_EXP), (s_act, 2 * N_EXP),
                                                    (s_hid, 2 * N_EXP), (s_pv, N_EXP), (s_ye, N_EXP + 1))}

            def at(self, s, k, i, n):
                return self.b[s] + 2 * k * i + n

            def load(self, sp):
                with sp.Fori(0, N_EXP // 2) as i:
                    for b in range(2):
                        for j, (name, h) in enumerate((("w_gate_2", 0), ("w_up_2", 0), ("w_gate_2", 1), ("w_up_2", 1),
                                                       ("w_down_2", 0), ("w_down_2", 1))):
                            w = A[name][0].rearrange("e k n -> (e k) n")
                            src = w[bass.ds(i * 2048 + 1024 * b, 1024), 512 * h:512 * h + 512].rearrange("(k p) n -> p k n", p=P)
                            ring.load(sp, self.blocks + 6 * b + j, src, SLOT, more=12 * i)

            def trips(self, eng, body):
                with eng.Fori(0, N_EXP // 2 - 1) as i:
                    for b in range(2):
                        body(eng, i, b, True)
                for b in range(2):
                    body(eng, N_EXP // 2 - 1, b, b == 0)

            def turn_rows(self, pe, i, n):
                b = n % 2
                pe.wait_ge(s_gather[b].sem, i * 16 + 16 * (n // 2) + 16)
                for k in range(8):
                    last = nc.tensor.transpose(PS[:, k // 4, P * (k % 4):P * (k % 4) + P], self.xe[b][:, P * k:P * k + P],
                                               IDENT[:, :])
                last.then_inc(s_xet.sem, 1)

            def gate_up(self, pe, i, b, h, f):
                n = self.blocks + 6 * b + 2 * h + f
                ring.ready(pe, n, i, 12)
                w = ring.view(n, 8)
                for k in range(8):
                    last = nc.tensor.matmul(PS[:, 2 + 2 * f + h, :], self.xet[b][:, k, :], w[:, k, :],
                                            start=(k == 0), stop=(k == 7))
                last.then_inc(s_gu.sem, 1)
                pe.drain().then_inc(block_used.sem, 1)

            def turn_hidden(self, pe, b, h):
                for k in range(4):
                    last = nc.tensor.transpose(PS[:, h, P * k:P * k + P], self.hg[b][:, 512 * h + P * k:512 * h + P * k + P],
                                               IDENT[:, :])
                last.then_inc(s_pt.sem, 1)

            def down(self, i, b, h, ks):
                w = ring.view(self.blocks + 6 * b + 4 + h, 8)
                for k in ks:
                    last = nc.tensor.matmul(PS[:, 6 + h, :], self.hgt[b][:, k, :], w[:, k, :], start=(k == 0), stop=(k == 7))
                return last

            def expert_pe(self, pe, i, b, more):
                pe.wait_ge(s_pta.sem, self.at(s_pta, 2, i, 2 * b + 1))
                pe.wait_ge(s_ptd.sem, self.at(s_ptd, 2, i, 2 * b + 1))
                self.gate_up(pe, i, b, 0, 0)
                self.gate_up(pe, i, b, 0, 1)
                if more:
                    self.turn_rows(pe, i, b + 1)
                self.gate_up(pe, i, b, 1, 0)
                pe.wait_ge(s_hid.sem, self.at(s_hid, 2, i, 2 * b + 1))
                if more:
                    pe.wait_ge(s_pta.sem, self.at(s_pta, 2, i, 2 * b + 2))
                self.turn_hidden(pe, b, 0)
                self.gate_up(pe, i, b, 1, 1)
                pe.wait_ge(s_pta.sem, self.at(s_pta, 2, i, 2 * b + (3 if more else 2)))
                pe.wait_ge(s_ye.sem, self.at(s_ye, 1, i, b + 1))
                ring.ready(pe, self.blocks + 6 * b + 4, i, 12)
                self.down(i, b, 0, range(0, 4))
                pe.wait_ge(s_hid.sem, self.at(s_hid, 2, i, 2 * b + 2))
                if more:
                    pe.wait_ge(s_ptd.sem, self.at(s_ptd, 2, i, 2 * b + 2))
                self.turn_hidden(pe, b, 1)
                ring.ready(pe, self.blocks + 6 * b + 5, i, 12)
                self.down(i, b, 1, range(0, 4))
                pe.wait_ge(s_ptd.sem, self.at(s_ptd, 2, i, 2 * b + (3 if more else 2)))
                self.down(i, b, 0, range(4, 8))
                pe.drain().then_inc(block_used.sem, 1)
                self.down(i, b, 1, range(4, 8)).then_inc(s_pv.sem, 1)
                pe.drain().then_inc(block_used.sem, 1)

            def tensor(self, pe):
                self.turn_rows(pe, 0, 0)
                self.trips(pe, self.expert_pe)

            def half(self, bank):
                return PS[:, bank, :].rearrange("p (a b) -> p a b", a=4)

            def expert_act(self, act, i, b, more):
                act.wait_ge(s_gu.sem, self.at(s_gu, 4, i, 4 * b + 1))
                nc.scalar.activation(self.sa[b][:, 0:512], PS[:, 2, :], ACT.Silu).then_inc(s_act.sem, 1)
                if more:
                    act.wait_ge(s_xet.sem, self.at(s_xet, 1, i, b + 2))
                    nc.scalar.activation(self.xet[1 - b][:, 0:4, :], self.half(0), ACT.Copy).then_inc(s_pta.sem, 1)
                act.wait_ge(s_gu.sem, self.at(s_gu, 4, i, 4 * b + 3))
                nc.scalar.activation(self.sa[b][:, 512:1024], PS[:, 3, :], ACT.Silu).then_inc(s_act.sem, 1)
                act.wait_ge(s_pt.sem, self.at(s_pt, 2, i, 2 * b + 1))
                nc.scalar.activation(self.hgt[b][:, 0:4, :], self.half(0), ACT.Copy).then_inc(s_pta.sem, 1)

            def scalar(self, act):
                act.wait_ge(s_xet.sem, self.b[s_xet] + 1)
                nc.scalar.activation(self.xet[0][:, 0:4, :], self.half(0), ACT.Copy).then_inc(s_pta.sem, 1)
                self.trips(act, self.expert_act)

            def hidden(self, dve, i, b, h):
                dve.wait_ge(s_act.sem, self.at(s_act, 2, i, 2 * b + h + 1))
                dve.wait_ge(s_gu.sem, self.at(s_gu, 4, i, 4 * b + 2 * h + 2))
                nc.vector.tensor_tensor(self.hg[b][:, 512 * h:512 * h + 512], self.sa[b][:, 512 * h:512 * h + 512],
                                        PS[:, 4 + h, :], ALU.mult).then_inc(s_hid.sem, 1)

            def expert_dve(self, dve, i, b, more):
                self.hidden(dve, i, b, 0)
                if more:
                    dve.wait_ge(s_xet.sem, self.at(s_xet, 1, i, b + 2))
                    nc.vector.tensor_copy(self.xet[1 - b][:, 4:8, :], self.half(1)).then_inc(s_ptd.sem, 1)
                self.hidden(dve, i, b, 1)
                dve.wait_ge(s_pt.sem, self.at(s_pt, 2, i, 2 * b + 2))
                nc.vector.tensor_copy(self.hgt[b][:, 4:8, :], self.half(1)).then_inc(s_ptd.sem, 1)
                dve.wait_ge(s_pv.sem, self.at(s_pv, 1, i, b + 1))
                dve.wait_ge(s_scatter.sem, self.at(s_scatter, 16, i, 16 * (b - 1)))
                gate = GT[:, bass.ds(i * 2 + b, 1)]
                nc.vector.tensor_scalar(self.ye[b].rearrange("p (a b) -> p a b", a=2), PS[:, 6:8, :], gate, None,
                                        ALU.mult).then_inc(s_ye.sem, 1)

            def vector(self, dve):
                dve.sem_inc(s_ye.sem, 1)
                dve.wait_ge(s_xet.sem, self.b[s_xet] + 1)
                nc.vector.tensor_copy(self.xet[0][:, 4:8, :], self.half(1)).then_inc(s_ptd.sem, 1)
                self.trips(dve, self.expert_dve)

            def gather(self, gp, n):
                b = n % 2
                gp.indirect_dma_start(self.xe[b], None, h2_dram,
                                      bass.IndirectOffsetOnAxis(ap=IDX[:, n:n + 1], axis=0)).then_inc(s_gather[b].sem, 16)

            def pool(self, gp):
                self.gather(gp, 0)
                self.gather(gp, 1)
                for n in range(N_EXP):
                    if n + 2 < N_EXP:
                        gp.wait_ge(s_xet.sem, self.b[s_xet] + n + 1)
                        self.gather(gp, n + 2)
                    gp.wait_ge(s_ye.sem, self.b[s_ye] + n + 2)
                    gp.wait_ge(s_scatter.sem, self.b[s_scatter] + 16 * n)
                    gp.indirect_dma_start(y_dram, bass.IndirectOffsetOnAxis(ap=IDX[:, n:n + 1], axis=0), self.ye[n % 2], None,
                                          compute_op=ALU.add).then_inc(s_scatter.sem, 16)
                gp.wait_ge(s_scatter.sem, self.b[s_scatter] + 16 * N_EXP)

        class Finish(Stage):

            def __init__(self, y, gf):
                self.y, self.gf = y, gf
                self.d = misc_dma.span(16)
                self.sq = squares.span(8)
                self.rt = roots.span(1)
                self.nm = normed.span(16)
                self.o = out_dma.span(128)

            def pool(self, gp):
                gp.dma_start(self.y, y_dram.rearrange("(t p) d -> p t d", p=P)).then_inc(misc_dma.sem, 16)
                gp.wait_ge(misc_dma.sem, self.d + 16)

            def vector(self, dve):
                dve.wait_ge(misc_dma.sem, self.d + 16)
                for t in range(8):
                    dstep(dve, nc.vector.tensor_tensor(self.y[:, t, :], self.y[:, t, :], GATE[:, :], ALU.mult))
                    nc.vector.tensor_tensor(X[:, t, :], X[:, t, :], self.y[:, t, :], ALU.add).then_inc(normed.sem, 1)
                dve.wait_ge(roots.sem, self.rt + 1)
                dstep(dve, nc.vector.reciprocal(stat(16, 24), stat(8, 16)))
                for t in range(8):
                    nc.vector.scalar_tensor_tensor(X[:, t, :], X[:, t, :], stat(16 + t, 17 + t), self.gf, ALU.mult, ALU.mult).then_inc(normed.sem, 1)

            def scalar(self, act):
                for t in range(8):
                    act.wait_ge(normed.sem, self.nm + t + 1)
                    nc.scalar.activation(self.y[:, t, :], X[:, t, :], ACT.Square, accum_out=stat(t, t + 1)).then_inc(squares.sem, 1)
                act.wait_ge(squares.sem, self.sq + 8)
                nc.scalar.activation(stat(8, 16), stat(0, 8), ACT.Sqrt, bias=EPSC[:, :], scale=1.0 / D).then_inc(roots.sem, 1)
                for t in range(8):
                    act.wait_ge(normed.sem, self.nm + 8 + t + 1)
                    act.dma_start(out[0, P * t:P * t + P, :], X[:, t, :]).then_inc(out_dma.sem, 16)
                act.wait_ge(out_dma.sem, self.o + 128)

        def second_block():
            w_in = A["w_in_2"][0]
            dq, dk, dv = area(8192, 8, 512), area(12288, 8, 512), area(16384, 8, 512)
            p672 = area(12288, 8, 672)
            ckvt = area(0, 2, 1024)
            cqt = [area(20480, 1024), area(21504, 1024), area(7168, 1024)]
            kv = area(12288, 8, 1024)
            q = area(0, 8, 768)
            dil = area(20480, 1920)

            def tok(t, c0, c1, width=512):
                return lambda n, k: (HT[:, k, P * t:P * t + P],
                                     WB[:, n % RING, 0:8 * width].rearrange("p (k n) -> p k n", k=8)[:, k, c0:c1])

            def heads(x, d):
                return x.rearrange("p t (h d) -> p t h d", d=d)

            st = [Rotations(),
                  Norm(X, 8, DER[:, 0, 0, :], MODC[:, 0, 0:8], HT, area(8192, 8, D)),
                  Product([(rows_of(w_in, 672 + 512 * b, 1184 + 512 * b), SLOT) for b in range(3)],
                          [(b, tok(t, 0, 512), 512, "act" if t % 2 else "dve", to(dst[:, t, :]))
                           for b, dst in enumerate((dq, dk, dv)) for t in range(8)], KD),
                  RotateHeads([heads(dq, 64), heads(dk, 64)], 0, 16, 8, 64),
                  LoadTable(dil, consts["dil"])]

            sq, sk = xarea(0, 8, 128), xarea(1024, 8, 128)
            kt = xarea(3072, 1024)

            def stage_d(i):
                nc.vector.tensor_copy(sq, dq[:, :, bass.ts(i, 128)])
                return nc.vector.tensor_copy(sk, dk[:, :, bass.ts(i, 128)])

            def keys_d(h, t, bank_a, bank_b):
                b = 64 * (h % 2)
                return [(bank_a, kt[b:b + 64, 0:512]), (bank_b, kt[b:b + 64, 512:1024])]

            st.append(Attention(4, 2, 8, 64, 0.125, sq, xarea(2048, 1024), xarea(4096, 2, 1024), xarea(6144, 2, 1024), steps=48,
                                sk=sk, kt=kt, stage=stage_d, keys=keys_d,
                                values=lambda i, h, t, j: dv[:, j, bass.ds(i * 128 + 64 * h, 64)],
                                out=lambda i, h, t: dq[:, t, bass.ds(i * 128 + 64 * h, 64)],
                                local=lambda t: (0, 8), masked=dil, wide=1))

            st.append(Product([(rows_of(w_in, 0, 512), SLOT), (rows_of(w_in, 512, 672), 1280)],
                              [(0, tok(t, 0, 512), 512, "act" if t % 2 else "dve", to(p672[:, t, 0:512])) for t in range(8)]
                              + [(1, tok(t, 0, 160, 160), 160, "act" if t % 2 else "dve", to(p672[:, t, 512:672])) for t in range(8)], KD))
            st += [Norm(p672[:, :, 0:384], 8, VEC[:, 2, ROW2_Q:ROW2_Q + 3], None, cqt, xarea(0, 8, 384), width=384),
                   Norm(p672[:, :, 384:640], 8, VEC[:, 2, ROW2_KV:ROW2_KV + 2], None, ckvt, xarea(3072, 8, 256), width=256),
                   RotateHeads([heads(p672[:, :, 640:672], 32)], 0, 32, 1, 0),
                   Copy(KR, p672[:, :, 640:672])]

            def small(x, K, width, c0, c1):
                def ops(n, k):
                    w = WB[:, n % RING, 0:K * width].rearrange("p (k n) -> p k n", k=K)
                    return x(k), w[:, k, c0:c1]
                return ops

            st.append(Product([(A["w_ukv_2"][0].rearrange("(k p) n -> p k n", p=P), 2048)],
                              [(0, small(lambda k, t=t: ckvt[:, k, P * t:P * t + P], 2, 1024, 512 * n, 512 * n + 512), 512,
                                "act" if n else "dve", to(kv[:, t, 512 * n:512 * n + 512])) for t in range(8) for n in range(2)], 2))
            st.append(Product([(A["w_uq_2"][0].rearrange("(k p) n -> p k n", p=P), 2304)],
                              [(0, small(lambda k, t=t: cqt[k][:, P * t:P * t + P], 3, 768, 384 * n, 384 * n + 384), 384,
                                "act" if n else "dve", to(q[:, t, 384 * n:384 * n + 384])) for t in range(8) for n in range(2)], 3))
            st.append(RotateHeads([heads(q, 96)], 64, 32, 8, 0))

            sq2, sk2 = area(6144, 8, 192), area(20480, 8, 192)
            kt2 = xarea(2048, 2048)

            def stage_m(i):
                nc.vector.tensor_copy(sq2, q[:, :, bass.ts(i, 192)])
                for h in range(2):
                    nc.vector.tensor_copy(sk2[:, :, 96 * h:96 * h + 64], kv[:, :, bass.ds(i * 256 + 128 * h, 64)])
                    ins = nc.vector.tensor_copy(sk2[:, :, 96 * h + 64:96 * h + 96], KR)
                return ins

            def keys_m(h, t, bank_a, bank_b):
                return [(bank_a, kt2[0:96, 1024 * h:1024 * h + 512]), (bank_b, kt2[0:96, 1024 * h + 512:1024 * h + 1024])]

            st.append(Attention(4, 2, 8, 96, 96.0 ** -0.5, sq2, xarea(0, 2048), xarea(4096, 2, 1024), xarea(6144, 2, 1024), steps=32,
                                sk=sk2, kt=kt2, stage=stage_m, keys=keys_m,
                                values=lambda i, h, t, j: kv[:, j, bass.ds(i * 256 + 128 * h + 64, 64)],
                                out=lambda i, h, t: q[:, t, bass.ds(i * 128 + 64 * h, 64)], ctx_keys=1024))

            mt = area(12288, 8, 1024)

            def mixed(t, c):
                if c < 4:
                    return q[:, t, P * c:P * c + P]
                return dq[:, t, P * (c - 4):P * (c - 4) + P]

            st += [Turn(8, mixed, lambda c, a, b: mt[:, c, a:b], None),
                   LoadTable(XF, x_spill),
                   Spread(MODC[:, 0, 16:24], GATE[:, :], area(0, 1024)),
                   OutProduct(A["w_out_2"][0], mt, X, 8, False, area(0, 4096)),
                   Norm(X, 8, DER[:, 0, 1, :], MODC[:, 0, 24:32], HT, area(8192, 8, D)),
                   Spread(DER[:, 0, 1, :], area(20480, 1024), area(16384, 1024)),
                   Spread(MODC[:, 0, 24:32], area(21504, 1024), area(16384, 1024)),
                   Rows(area(8192, 8, D), area(20480, 1024), area(21504, 1024), area(16384, 1024)),
                   Route(8192),
                   Experts(),
                   Spread(MODC[:, 0, 40:48], GATE[:, :], area(0, 1024)),
                   Spread(VEC[:, 2, ROW2_FINAL:ROW2_FINAL + 8], area(2048, 1024), area(0, 1024)),
                   Finish(area(8192, 8, D), area(2048, 1024))]
            return st

        stages = [Setup(), Modulate(0)] + layer_stream(0, 1, XC, 2) + layer_stream(0, 0, X, 8)
        stages += [Modulate(1)] + context_kv(1) + layer_stream(1, 0, X, 8)
        stages += [Modulate(2)] + second_block()
        fence_no = {e: 0 for e in stage_end}

        def fence(eng, me):
            eng.drain().then_inc(stage_end[me], 1)
            fence_no[me] += 1
            for other in stage_end:
                if other != me:
                    eng.wait_ge(stage_end[other], fence_no[me])

        block = ctx.enter_context(nc.Block())

        @block.sync
        def _(sp):
            for st in stages:
                st.load(sp)

        @block.tensor
        def _(pe):
            for st in stages:
                st.tensor(pe)
                fence(pe, "pe")

        @block.scalar
        def _(act):
            for st in stages:
                st.scalar(act)
                fence(act, "act")

        @block.vector
        def _(dve):
            for st in stages:
                st.vector(dve)
                fence(dve, "dve")

        @block.gpsimd
        def _(gp):
            for st in stages:
                st.pool(gp)
                fence(gp, "pool")


def shape_tables():
    import numpy as np

    t = {"ident": np.eye(128, dtype=np.float32)}
    n_freq = 16
    inv = (10000.0 ** (-np.arange(n_freq, dtype=np.float32) / n_freq)).astype(np.float32)
    row = np.repeat(np.arange(16), 64).astype(np.float32)
    col = np.tile(np.arange(64), 16).astype(np.float32)
    ar, ac = row[:, None] * inv[None], col[:, None] * inv[None]
    cos = np.cos(np.concatenate([ar, ar, ac, ac], -1))
    sin = np.sin(np.concatenate([-ar, ar, -ac, ac], -1))
    rope = np.stack([cos, sin]).reshape(2, 8, 128, 64).transpose(2, 0, 1, 3).reshape(128, 2, 512)
    t["rope"] = np.ascontiguousarray(rope, dtype=np.float32)
    q, k = np.arange(128)[:, None], np.arange(384)[None] - 128
    t["wmask"] = np.where(np.abs(k - q) <= 128, 0.0, -1e30).astype(np.float32)
    rel = np.arange(1920)[None] - 896 - np.arange(128)[:, None]
    count = sum(((rel % d == 0) & (np.abs(rel) <= 64 * d)).astype(np.float64) for d in (1, 4, 16))
    t["dil"] = np.where(count > 0, np.log(np.maximum(count, 1)), -1e30).astype(np.float32)
    a = 2 * np.pi * np.outer(np.arange(64), np.arange(64)) / 64
    f = np.zeros((128, 256))
    for g in range(2):
        f[64 * g:64 * g + 64, 64 * g:64 * g + 64] = np.cos(a)
        f[64 * g:64 * g + 64, 128 + 64 * g:128 + 64 * g + 64] = -np.sin(a)
    t["dftf"] = f.astype(np.float32)

    def seq(n):
        m = np.outer(np.arange(n), np.arange(n)) % n
        cs = np.stack([np.cos(2 * np.pi * m / n), np.sin(2 * np.pi * m / n)])
        cs = cs.reshape(2, n // 128, 128, n // 256, 256).transpose(3, 2, 1, 0, 4)
        return np.ascontiguousarray(cs.reshape(n // 256, 128, -1), dtype=np.float32)

    t["dfts"] = seq(1024)
    t["dftc"] = seq(256)[0]
    inv_m = 1.0 / (500000.0 ** (np.arange(0, 32, 2, dtype=np.float32) / np.float32(32)))
    inv_d = 1.0 / (500000.0 ** (np.arange(0, 16, 2, dtype=np.float32) / np.float32(16)))
    t["inv"] = np.tile(np.concatenate([inv_m, inv_d]).astype(np.float32)[None], (128, 1))
    return t


_INS = ["x", "c", "ctx", "c_ctx", "w_ada", "b_ada", "g_pre_mix", "w_in", "sink", "w_sgu", "b_sgu", "g_sgu", "g_mix", "w_out",
        "g_post_mix", "g_pre_ff", "w_ff1", "w_ff2", "g_post_ff", "c_2", "positions_2", "w_ada_2", "b_ada_2", "g_mix_2",
        "w_in_2", "g_q_2", "w_uq_2", "g_kv_2", "w_ukv_2", "w_out_2", "g_ffn_2", "w_router_2", "b_router_2", "w_gate_2",
        "w_up_2", "w_down_2", "g_final_2"]


def kernel(**inputs):
    import numpy as _np
    import concourse.bacc as _bacc
    from concourse import mybir as _mybir
    from concourse.bass_utils import run_bass_kernel_spmd as _run

    nc = _bacc.Bacc("TRN2", target_bir_lowering=False, num_devices=1)
    arrays, args, consts = {}, {}, {}
    for name in _INS:
        a = _np.ascontiguousarray(inputs[name])
        arrays[f"in_{name}_dram"] = a
        args[name] = nc.dram_tensor(f"in_{name}_dram", a.shape, _mybir.dt.from_np(a.dtype), kind="ExternalInput").ap()
    for name, a in shape_tables().items():
        arrays[f"table_{name}_dram"] = a
        consts[name] = nc.dram_tensor(f"table_{name}_dram", a.shape, _mybir.dt.from_np(a.dtype), kind="ExternalInput").ap()
    out = nc.dram_tensor("out_0_dram", (1, 1024, 1024), _mybir.dt.float32, kind="ExternalOutput").ap()
    build(nc, args, consts, out)
    r = _run(nc, [arrays], core_ids=[0])
    return r.results[0]["out_0_dram"]
```

```python
from contextlib import ExitStack

import concourse.bass as bass
from concourse import mybir

F32 = mybir.dt.float32
I32 = mybir.dt.int32
ALU = mybir.AluOpType
ACT = mybir.ActivationFunctionType
AX_X = mybir.AxisListType.X

P = 128
D = 1024
KD = D // P
FF = 4096
EPS = 1e-6
BANK = 512
NEG = -1e30
RING = 4
SLOT = 4096
N_EXP = 16
CAP = 128

ROW_ADA, ROW_PRE, ROW_MIX, ROW_POST, ROW_FF, ROW_POSTFF, ROW_BSGU = 0, 48, 56, 64, 72, 80, 88
ROW_C, ROW_CCTX = 96, 104
ROW2_MIX, ROW2_Q, ROW2_KV, ROW2_FFN, ROW2_FINAL, ROW2_POS = 48, 56, 59, 61, 69, 96

Q0, K0, V0, U0, G0, F0 = 0, 512, 640, 768, 1024, 1280


class Signal:

    def __init__(self, sem):
        self.sem = sem
        self.planned = 0

    def span(self, n):
        base = self.planned
        self.planned += n
        return base


class Steps:

    def __init__(self, sem):
        self.sem = sem
        self.n = 0
        self.var = None

    def loop(self, var, per):
        self.var, self.per, self.start = var, per, self.n

    def loop_end(self, trips):
        assert self.n - self.start == self.per, ("steps per trip", self.n - self.start)
        self.n = self.start + trips * self.per
        self.var = None

    def done(self, eng, ins):
        ins.then_inc(self.sem, 1)
        self.n += 1
        eng.wait_ge(self.sem, self.n if self.var is None else self.var * self.per + self.n)


class Ring:

    def __init__(self, slots, landed, used):
        self.slots, self.landed, self.used, self.n = slots, landed, used, 0

    def take(self, n):
        base = self.n
        self.n += n
        return base

    def load(self, sp, n, src, cols, more=0):
        s = n % RING
        if n >= RING:
            sp.wait_ge(self.used.sem, n - RING + 1 + more)
        dst = self.slots[:, s, 0:cols]
        if len(src.shape) == 3:
            dst = dst.rearrange("p (a b) -> p a b", a=src.shape[1])
        sp.dma_start(dst, src).then_inc(self.landed[s], 16)

    def ready(self, pe, n, trip=0, per=0):
        pe.wait_ge(self.landed[n % RING], 16 * (n // RING + 1) + trip * (16 * per // RING))

    def view(self, n, a):
        return self.slots[:, n % RING, :].rearrange("p (a b) -> p a b", a=a)


class Stage:
    def load(self, sp):
        pass

    def tensor(self, pe):
        pass

    def vector(self, dve):
        pass

    def scalar(self, act):
        pass

    def pool(self, gp):
        pass


def build(nc, A, consts, out):
    ctx = ExitStack()
    with ctx:
        def sb(name, shape, dt=F32):
            return ctx.enter_context(nc.sbuf_tensor(name, shape, dt))

        def signal(name):
            return Signal(ctx.enter_context(nc.semaphore(name)))

        X = sb("X", [P, 8, D])
        WB = sb("WB", [P, RING, SLOT])
        AR = sb("AR", [P, 22528])
        IDENT = sb("IDENT", [P, P])
        ONES = sb("ONES", [P, P])
        EPSC = sb("EPSC", [P, 1])
        VEC = sb("VEC", [P, 3, P])
        SC = sb("SC", [P, 3, 8])
        MODC = sb("MODC", [P, 2, 48])
        MODN = sb("MODN", [P, 2, 48])
        DER = sb("DER", [P, 2, 4, 8])
        ROPE = sb("ROPE", [P, 2, 512])
        WMASK = sb("WMASK", [P, 384])
        DFTF = sb("DFTF", [P, 256])
        KCT = sb("KCT", [P, 2, 256])
        VC = sb("VC", [P, 2, P])
        WST = sb("WST", [P, 4, P])
        GSGU = sb("GSGU", [P, 256])
        SINK = sb("SINK", [P, 2, 8])
        STAT = sb("STAT", [P, 128])
        GATE = sb("GATE", [P, D])
        INV = sb("INV", [P, 24])
        IOTA_I = sb("IOTA_I", [P, P + 8], I32)
        IDX = sb("IDX", [P, N_EXP], I32)
        GT = sb("GT", [P, N_EXP])
        RF = ROPE[:, :, :].rearrange("p a b -> p (a b)")
        ROPE2 = RF[:, 0:768].rearrange("p (t a) -> p t a", t=8)
        KR = RF[:, 768:1024].rearrange("p (t a) -> p t a", t=8)
        PS = ctx.enter_context(nc.psum_tensor("PS", [P, 8, BANK], F32))

        def area(off, *shape):
            n = 1
            for s in shape:
                n *= s
            v = AR[:, off:off + n]
            if len(shape) == 2:
                return v.rearrange("p (a b) -> p a b", a=shape[0])
            if len(shape) == 3:
                return v.rearrange("p (a b c) -> p a b c", a=shape[0], b=shape[1])
            return v

        XF = X[:, :, :].rearrange("p a b -> p (a b)")

        def xarea(off, *shape):
            n = 1
            for s in shape:
                n *= s
            v = XF[:, off:off + n]
            if len(shape) == 2:
                return v.rearrange("p (a b) -> p a b", a=shape[0])
            return v

        HT = area(0, 8, 1024)
        XC = area(20480, 2, 1024)

        mm = signal("pe_group_done")
        freed_d = signal("psum_taken_by_dve")
        freed_a = signal("psum_taken_by_act")
        squares = signal("act_square_sums")
        roots = signal("act_roots")
        normed = signal("dve_normed_rows")
        consts_in = signal("consts_landed")
        x_in = signal("x_landed")
        rows_zero = signal("vector_rows_zeroed")
        rows_in = signal("vector_rows_landed")
        ones_set = signal("ones_set")
        setup_act = signal("act_silu_done")
        block_used = signal("ring_block_used")
        landed = [ctx.enter_context(nc.semaphore(f"ring_slot{i}_landed")) for i in range(RING)]
        ring = Ring(WB, landed, block_used)
        hid_done = signal("act_hidden_done")
        zeroed = signal("pool_zeroed")
        s_staged = signal("dve_qk_staged")
        s_turned = signal("pe_qk_turned")
        s_qt = signal("act_qt_ready")
        s_kt = signal("dve_kt_ready")
        s_score = signal("pe_scores")
        s_max = signal("dve_row_max")
        s_prob = signal("act_probs")
        s_pt = signal("pe_probs_turned")
        s_pta = signal("act_probs_taken")
        s_ptd = signal("dve_probs_taken")
        s_pv = signal("pe_values")
        s_out = signal("dve_heads_out")
        misc_dma = signal("misc_dma_landed")
        out_dma = signal("result_stored")
        s_diag = signal("dve_diagonals")
        s_gather = [signal(f"rows_gathered_{b}") for b in range(2)]
        s_scatter = signal("rows_scattered")
        s_xet = signal("pe_expert_rows_turned")
        s_gu = signal("pe_gate_up")
        s_act = signal("act_silu")
        s_hid = signal("dve_expert_hidden")
        s_ye = signal("dve_expert_out")
        normed_lg = signal("dve_logits_shifted")
        normed_aff = signal("dve_affinities")
        rows_final = signal("dve_final_rows")
        rows_in_act = signal("vector_rows_landed_by_act_queue")
        mod_sums = signal("dve_ada_sums")
        mod_columns = signal("pe_ada_columns")
        mod_kept = signal("dve_ada_columns_kept")
        steps_d = Steps(ctx.enter_context(nc.semaphore("dve_steps")))
        steps_a = Steps(ctx.enter_context(nc.semaphore("act_steps")))
        steps_g = Steps(ctx.enter_context(nc.semaphore("pool_steps")))
        stage_end = {e: ctx.enter_context(nc.semaphore(f"{e}_stage_end")) for e in ("pe", "act", "dve", "pool")}
        x_spill = nc.dram_tensor("x_spill", (P, 8 * D), F32).ap()
        h2_dram = nc.dram_tensor("h2_rows", (1024, D), F32).ap()
        y_dram = nc.dram_tensor("y_rows", (1024, D), F32).ap()

        def dstep(dve, ins):
            steps_d.done(dve, ins)

        def astep(act, ins):
            steps_a.done(act, ins)

        def stat(a, b):
            return STAT[:, a:b]

        class Setup(Stage):

            def __init__(self):
                self.rows = area(0, 3, P)
                self.pos_i = sb("pos_i", [P, P], I32)
                self.mm = mm.span(1)
                self.nconst = 8
                self.sgu_raw = None

            def load(self, sp):
                sp.dma_start(IDENT[:, :], consts["ident"]).then_inc(consts_in.sem, 16)
                sp.dma_start(XC, A["ctx"][0].rearrange("(t p) d -> p t d", p=P)).then_inc(consts_in.sem, 16)
                sp.dma_start(ROPE[:, :, :], consts["rope"]).then_inc(consts_in.sem, 16)
                sp.dma_start(WMASK[:, :], consts["wmask"]).then_inc(consts_in.sem, 16)
                sp.dma_start(DFTF[:, :], consts["dftf"]).then_inc(consts_in.sem, 16)
                sp.dma_start(SINK[:, :, :], A["sink"].partition_broadcast(P)).then_inc(consts_in.sem, 16)
                sp.dma_start(INV[:, :], consts["inv"]).then_inc(consts_in.sem, 16)
                sp.dma_start(self.pos_i[ROW2_POS:ROW2_POS + 8, :],
                             A["positions_2"].rearrange("a (t p) -> (a t) p", p=P)).then_inc(consts_in.sem, 16)

            def pool(self, gp):
                nc.gpsimd.memset(ONES[:, :], 1.0).then_inc(ones_set.sem, 1)
                nc.gpsimd.memset(EPSC[:, :], EPS).then_inc(ones_set.sem, 1)
                nc.gpsimd.memset(self.rows, 0.0).then_inc(rows_zero.sem, 1)
                gp.wait_ge(rows_zero.sem, 1)

                gp.wait_ge(ones_set.sem, 2)
                n = self.rows_by(gp, rows_in, 0)
                assert n == self.N_POOL
                gp.wait_ge(rows_in.sem, 16 * n)

            N_POOL, N_ACT = 9, 14

            def rows_by(self, eng, sig, part):
                jobs = []
                for l in range(2):
                    for r, name in ((ROW_ADA, "b_ada"), (ROW_PRE, "g_pre_mix"), (ROW_MIX, "g_mix"), (ROW_POST, "g_post_mix"),
                                    (ROW_FF, "g_pre_ff"), (ROW_POSTFF, "g_post_ff")):
                        jobs.append((l, r, A[name][l].rearrange("(r p) -> r p", p=P)))
                    jobs.append((l, ROW_BSGU, A["b_sgu"][l]))
                for r, name in ((ROW_ADA, "b_ada_2"), (ROW2_MIX, "g_mix_2"), (ROW2_Q, "g_q_2"), (ROW2_KV, "g_kv_2"),
                                (ROW2_FFN, "g_ffn_2")):
                    jobs.append((2, r, A[name][0].rearrange("(r p) -> r p", p=P)))
                jobs.append((2, ROW2_FINAL, A["g_final_2"].rearrange("(r p) -> r p", p=P)))
                jobs.append((0, ROW_C, A["c"][0].rearrange("(r p) -> r p", p=P)))
                jobs.append((0, ROW_CCTX, A["c_ctx"].rearrange("(r p) -> r p", p=P)))
                jobs.append((1, ROW_C, A["c_2"][0].rearrange("(r p) -> r p", p=P)))
                jobs = [x for x in jobs if (x[0] > 0) == (part > 0)]
                for l, r, src in jobs:
                    eng.dma_start(self.rows[r:r + src.shape[0], l, :], src).then_inc(sig.sem, 16)
                return len(jobs)

            def vector(self, dve):
                dve.wait_ge(consts_in.sem, 16 * self.nconst)
                dve.wait_ge(rows_zero.sem, 1)
                ins = nc.vector.tensor_copy(self.rows[ROW2_POS:ROW2_POS + 8, 2, :], self.pos_i[ROW2_POS:ROW2_POS + 8, :])
                dstep(dve, ins)
                dve.wait_ge(mm.sem, self.mm + 1)
                dstep(dve, nc.vector.tensor_copy(VEC[:, :, :], PS[:, 0, 0:384].rearrange("p (a b) -> p a b", a=3)))

            def tensor(self, pe):
                pe.wait_ge(consts_in.sem, 16 * self.nconst)
                pe.wait_ge(rows_in.sem, 16 * self.N_POOL)
                pe.wait_ge(rows_in_act.sem, 16 * self.N_ACT)
                pe.wait_ge(steps_d.sem, 1)
                for l in range(3):
                    last = nc.tensor.transpose(PS[:, 0, P * l:P * l + P], self.rows[:, l, :], IDENT[:, :])
                last.then_inc(mm.sem, 1)

            def scalar(self, act):
                act.wait_ge(rows_zero.sem, 1)
                n = self.rows_by(act, rows_in_act, 1)
                assert n == self.N_ACT
                act.wait_ge(rows_in_act.sem, 16 * n)
                act.wait_ge(steps_d.sem, 2)
                nc.scalar.activation(SC[:, 0, :], VEC[:, 0, ROW_C:ROW_C + 8], ACT.Silu)
                nc.scalar.activation(SC[:, 1, :], VEC[:, 0, ROW_CCTX:ROW_CCTX + 8], ACT.Silu)
                nc.scalar.activation(SC[:, 2, :], VEC[:, 1, ROW_C:ROW_C + 8], ACT.Silu)

        class Modulate(Stage):

            TURNS = 7

            def __init__(self, l):
                self.l = l
                self.nv = 2 if l < 2 else 1
                self.w = A["w_ada"][l] if l < 2 else A["w_ada_2"][0]
                self.rows = area(0, 12, BANK)
                self.blocks = ring.take(12)
                self.mm = mm.span(13)
                self.fd = freed_d.span(12)

            def load(self, sp):
                for b in range(12):
                    ring.load(sp, self.blocks + b, self.w[:, 512 * b:512 * b + 512].rearrange("(k p) n -> p k n", p=P), SLOT)
                if self.l == 0:
                    sp.dma_start(X[:, :, :], A["x"][0].rearrange("(t p) d -> p t d", p=P)).then_inc(x_in.sem, 16)

            def pool(self, gp):
                if self.l == 0:
                    gp.wait_ge(x_in.sem, 16)

            def turn(self, pe, b):
                nv = self.nv
                pe.wait_ge(freed_d.sem, self.fd + b + 1)
                for j in range(4):
                    c = (4 * b + j) * 2
                    last = nc.tensor.transpose(PS[:, self.TURNS, c:c + nv], self.rows[0:nv, b, P * j:P * j + P],
                                               IDENT[0:nv, 0:nv])
                return last

            def tensor(self, pe):
                nv = self.nv
                for b in range(12):
                    ring.ready(pe, self.blocks + b)
                    w = ring.view(self.blocks + b, 8)
                    if b >= 7:
                        pe.wait_ge(freed_d.sem, self.fd + b - 6)
                    for k in range(8):
                        lhs = SC[:, 0:2, k] if nv == 2 else SC[:, 2, k:k + 1]
                        last = nc.tensor.matmul(PS[0:nv, b % 7, :], lhs, w[:, k, :], start=(k == 0), stop=(k == 7))
                    last.then_inc(mm.sem, 1)
                    pe.wait_ge(mm.sem, self.mm + b + 1)
                    pe.sem_inc(block_used.sem, 1)
                    if b:
                        self.turn(pe, b - 1)
                self.turn(pe, 11).then_inc(mm.sem, 1)

            def vector(self, dve):
                nv = self.nv
                for b in range(12):
                    dve.wait_ge(mm.sem, self.mm + b + 1)
                    nc.vector.tensor_copy(self.rows[0:nv, b, :], PS[0:nv, b % 7, :]).then_inc(freed_d.sem, 1)
                dve.wait_ge(mm.sem, self.mm + 13)
                raw = PS[:, self.TURNS, 0:96].rearrange("p (j s) -> p s j", s=2)
                gains(dve, self.l, self.nv, raw)

        class Gains(Stage):

            def __init__(self, l):
                self.l = l

            def vector(self, dve):
                gains(dve, self.l, 2 if self.l < 2 else 1, MODN)

        def gains(dve, l, nv, raw):
            g1, g2 = (ROW_PRE, ROW_FF) if l < 2 else (ROW2_MIX, ROW2_FFN)
            for s in range(nv):
                dstep(dve, nc.vector.tensor_tensor(MODC[:, s, :], raw[:, s, :], VEC[:, l, 0:48], ALU.add))
                nc.vector.scalar_tensor_tensor(DER[:, s, 0, :], MODC[:, s, 8:16], 1.0, VEC[:, l, g1:g1 + 8], ALU.add, ALU.mult)
                nc.vector.scalar_tensor_tensor(DER[:, s, 1, :], MODC[:, s, 32:40], 1.0, VEC[:, l, g2:g2 + 8], ALU.add, ALU.mult)
                if l < 2:
                    nc.vector.tensor_tensor(DER[:, s, 2, :], MODC[:, s, 16:24], VEC[:, l, ROW_POST:ROW_POST + 8], ALU.mult)
                    nc.vector.tensor_tensor(DER[:, s, 3, :], MODC[:, s, 40:48], VEC[:, l, ROW_POSTFF:ROW_POSTFF + 8], ALU.mult)

        class Norm(Stage):

            def __init__(self, x, T, scale, shift, ht, xn, width=D, share=None):
                self.x, self.T, self.scale, self.shift, self.ht, self.xn = x, T, scale, shift, ht, xn
                self.K = width // P
                self.width = width
                self.H = max(1, T // 4)
                self.per = T // self.H
                self.G = self.H * self.K
                self.sq = squares.span(T)
                self.rt = roots.span(self.H)
                self.nm = normed.span(T)
                self.mm = mm.span(self.G)
                self.fa = freed_a.span((self.G + 1) // 2)
                self.fd = freed_d.span(self.G // 2)

            def scalar(self, act):
                for h in range(self.H):
                    a, b = self.per * h, self.per * (h + 1)
                    for t in range(a, b):
                        nc.scalar.activation(self.xn[:, t, :], self.x[:, t, 0:self.width], ACT.Square,
                                             accum_out=stat(t, t + 1)).then_inc(squares.sem, 1)
                    act.wait_ge(squares.sem, self.sq + b)
                    nc.scalar.activation(stat(8 + a, 8 + b), stat(a, b), ACT.Sqrt, bias=EPSC[:, :],
                                         scale=1.0 / self.width).then_inc(roots.sem, 1)
                for g in range(0, self.G, 2):
                    h, c = g // self.K, g % self.K
                    n = self.per * P
                    act.wait_ge(mm.sem, self.mm + g + 1)
                    if self.shift is None:
                        ins = nc.scalar.activation(self.dst(c, h), PS[:, g % 8, 0:n], ACT.Copy, scale=self.scale[:, c:c + 1])
                    else:
                        ins = nc.scalar.activation(self.dst(c, h), PS[:, g % 8, 0:n], ACT.Identity, bias=self.shift[:, c:c + 1],
                                                   scale=self.scale[:, c:c + 1])
                    ins.then_inc(freed_a.sem, 1)

            def dst(self, c, h):
                n = self.per * P
                if isinstance(self.ht, list):
                    return self.ht[c][:, n * h:n * h + n]
                return self.ht[:, c, n * h:n * h + n]

            def vector(self, dve):
                for h in range(self.H):
                    a, b = self.per * h, self.per * (h + 1)
                    dve.wait_ge(roots.sem, self.rt + h + 1)
                    dstep(dve, nc.vector.reciprocal(stat(16 + a, 16 + b), stat(8 + a, 8 + b)))
                    for t in range(a, b):
                        nc.vector.tensor_scalar(self.xn[:, t, :], self.x[:, t, 0:self.width], stat(16 + t, 17 + t), None,
                                                ALU.mult).then_inc(normed.sem, 1)
                for g in range(1, self.G, 2):
                    h, c = g // self.K, g % self.K
                    n = self.per * P
                    dve.wait_ge(mm.sem, self.mm + g + 1)
                    if self.shift is not None:
                        ins = nc.vector.tensor_scalar(self.dst(c, h), PS[:, g % 8, 0:n], self.scale[:, c:c + 1],
                                                      self.shift[:, c:c + 1], ALU.mult, ALU.add)
                    else:
                        ins = nc.vector.tensor_scalar(self.dst(c, h), PS[:, g % 8, 0:n], self.scale[:, c:c + 1],
                                                      None, ALU.mult)
                    ins.then_inc(freed_d.sem, 1)

            def tensor(self, pe):
                for g in range(self.G):
                    h, c = g // self.K, g % self.K
                    pe.wait_ge(normed.sem, self.nm + self.per * (h + 1))
                    if g >= 8:
                        src, base = (freed_d, self.fd) if g % 2 else (freed_a, self.fa)
                        pe.wait_ge(src.sem, base + (g - 8) // 2 + 1)
                    for j in range(self.per):
                        t = self.per * h + j
                        last = nc.tensor.transpose(PS[:, g % 8, P * j:P * j + P], self.xn[:, t, P * c:P * c + P], IDENT[:, :])
                    last.then_inc(mm.sem, 1)

        class Product(Stage):

            def __init__(self, blocks, groups, K):
                self.src = blocks
                self.base = ring.take(len(blocks))
                self.groups = groups
                self.K = K
                self.mm = mm.span(len(groups))
                self.na = sum(1 for g in groups if g[3] == "act")
                self.nd = len(groups) - self.na
                self.fa = freed_a.span(self.na)
                self.fd = freed_d.span(self.nd)

            def load(self, sp):
                for b, (src, cols) in enumerate(self.src):
                    ring.load(sp, self.base + b, src, cols)

            def nth(self, g):
                return sum(1 for x in self.groups[:g + 1] if x[3] == self.groups[g][3])

            def tensor(self, pe):
                seen = -1
                for g, (b, ops, n, who, take) in enumerate(self.groups):
                    while seen < b:
                        seen += 1
                        ring.ready(pe, self.base + seen)
                    if g >= 8:
                        src, base = (freed_a, self.fa) if self.groups[g - 8][3] == "act" else (freed_d, self.fd)
                        pe.wait_ge(src.sem, base + self.nth(g - 8))
                    for k in range(self.K):
                        lhsT, rhs = ops(self.base + b, k)
                        last = nc.tensor.matmul(PS[:, g % 8, 0:n], lhsT, rhs, start=(k == 0), stop=(k == self.K - 1))
                    last.then_inc(mm.sem, 1)
                    if g + 1 == len(self.groups) or self.groups[g + 1][0] != b:
                        pe.drain().then_inc(block_used.sem, 1)

            def vector(self, dve):
                for g, (b, ops, n, who, take) in enumerate(self.groups):
                    if who == "dve":
                        dve.wait_ge(mm.sem, self.mm + g + 1)
                        take(nc.vector, PS[:, g % 8, 0:n]).then_inc(freed_d.sem, 1)

            def scalar(self, act):
                for g, (b, ops, n, who, take) in enumerate(self.groups):
                    if who == "act":
                        act.wait_ge(mm.sem, self.mm + g + 1)
                        take(nc.scalar, PS[:, g % 8, 0:n]).then_inc(freed_a.sem, 1)

        def to(dst):
            def take(eng, bank):
                if eng is nc.vector:
                    return nc.vector.tensor_copy(dst, bank)
                return nc.scalar.activation(dst, bank, ACT.Copy)
            return take

        def to_gelu(dst):
            def take(eng, bank):
                return nc.scalar.activation(dst, bank, ACT.Gelu_apprx_tanh)
            return take

        def rows_of(w, c0, c1):
            return w[:, c0:c1].rearrange("(k p) n -> p k n", p=P)

        def input_projection(l, T, px, ft):
            w = A["w_in"][l]
            groups = []

            def tok(t, c0, c1):
                return lambda n, k: (HT[:, k, P * t:P * t + P], ring.view(n, 8)[:, k, c0:c1])

            for t in range(T):
                groups.append((0, tok(t, 0, 512), 512, "act" if t % 2 else "dve", to(px[:, t, 0:512])))
            for t in range(T):
                groups.append((1, tok(t, 0, 256), 256, "dve", to(px[:, t, K0:U0])))
            for t in range(T):
                groups.append((1, tok(t, 256, 512), 256, "act", to_gelu(px[:, t, U0:G0])))
            for t in range(T):
                groups.append((2, tok(t, 0, 256), 256, "act", to_gelu(px[:, t, G0:F0])))
            H = max(1, T // 4)
            n = P * T // H
            for c in range(2):
                for h in range(H):
                    def feat(b, k, c=c, h=h):
                        return ring.view(b, 8)[:, k, 256 + P * c:256 + P * c + P], HT[:, k, n * h:n * h + n]
                    groups.append((2, feat, n, "dve", to(ft[:, c, n * h:n * h + n])))
            return Product([(rows_of(w, 512 * b, 512 * b + 512), SLOT) for b in range(3)], groups, KD)

        def rotate(dve, x, cos, sin, heads, parts, half, t1, t2):
            w = parts * 2 * half
            a = t1[:, 0:heads * w].rearrange("p (h d) -> p h d", d=w)
            b = t2[:, 0:heads * w].rearrange("p (h d) -> p h d", d=w)
            nc.vector.tensor_tensor(a, x, cos, ALU.mult)
            for r in range(parts):
                for f in range(2):
                    lo, sw = (2 * r + f) * half, (2 * r + 1 - f) * half
                    s = sin[:, lo:lo + half].unsqueeze(1).broadcast_to([P, heads, half])
                    ins = nc.vector.tensor_tensor(b[:, :, lo:lo + half], x[:, :, sw:sw + half], s, ALU.mult)
            dstep(dve, ins)
            dstep(dve, nc.vector.tensor_tensor(x, a, b, ALU.add))

        class TurnKeys(Stage):

            def __init__(self, px, T, kt, c0, keep_v):
                self.px, self.T, self.kt, self.c0, self.keep_v = px, T, kt, c0, keep_v
                self.H = max(1, T // 4)
                self.per = T // self.H
                self.mm = mm.span(self.H)

            def tensor(self, pe):
                for h in range(self.H):
                    for j in range(self.per):
                        last = nc.tensor.transpose(PS[:, h, P * j:P * j + P],
                                                   self.px[:, self.per * h + j, self.c0:self.c0 + P], IDENT[:, :])
                    last.then_inc(mm.sem, 1)

            def vector(self, dve):
                n = self.per * P
                for h in range(self.H):
                    dve.wait_ge(mm.sem, self.mm + h + 1)
                    nc.vector.tensor_copy(self.kt[0:64, 0, n * h:n * h + n], PS[0:64, h, 0:n])
                    nc.vector.tensor_copy(self.kt[64:128, 1, n * h:n * h + n], PS[64:128, h, 0:n])
                    nc.vector.tensor_copy(self.kt[64:128, 0, n * h:n * h + n], PS[0:64, h, 0:n])
                    nc.vector.tensor_copy(self.kt[0:64, 1, n * h:n * h + n], PS[64:128, h, 0:n])
                if self.keep_v:
                    nc.vector.tensor_copy(VC[:, :, :], self.px[:, :, self.c0 + P:self.c0 + 2 * P])

        class Mixers(Stage):

            def __init__(self, l, px, ft, T):
                self.l, self.px, self.ft, self.T = l, px, ft, T
                self.t1, self.t2 = area(0, 640), area(640, 640)
                self.raw = area(1280, 4, P)
                self.vn = area(1792, T, 256)
                self.fa_ = area(4096, T, 4, P)
                self.nb = max(1, T // 2)
                self.blocks = ring.take(self.nb)
                self.dma = misc_dma.span(32)
                self.mm = mm.span(2 * T + 5)
                self.rt = roots.span(1)
                self.nm = normed.span(3)
                self.fa = freed_a.span(2 * T)
                self.fd = freed_d.span(1)
                self.scale = float(64 * T * P) ** -0.5

            def load(self, sp):
                for b in range(self.nb):
                    src = consts["dfts"][b] if self.T == 8 else consts["dftc"]
                    ring.load(sp, self.blocks + b, src, 512 * self.T)

            def pool(self, gp):
                gp.dma_start(self.raw, A["w_sgu"][self.l].rearrange("h p q -> p h q")).then_inc(misc_dma.sem, 16)
                gp.dma_start(GSGU[:, :], A["g_sgu"][self.l].rearrange("h d -> (h d)").partition_broadcast(P)).then_inc(misc_dma.sem, 16)
                gp.wait_ge(misc_dma.sem, self.dma + 32)

            def tensor(self, pe):
                T = self.T
                for t in range(T):
                    for c in range(2):
                        last = nc.tensor.matmul(PS[:, t, 256 * c:256 * c + 256], self.ft[:, c, P * t:P * t + P], DFTF[:, :],
                                                start=True, stop=True)
                    last.then_inc(mm.sem, 1)
                pe.wait_ge(freed_a.sem, self.fa + 1)
                pe.wait_ge(misc_dma.sem, self.dma + 32)
                for h in range(4):
                    last = nc.tensor.transpose(PS[:, 0, P * h:P * h + P], self.raw[:, h, :], IDENT[:, :])
                last.then_inc(mm.sem, 1)
                pe.wait_ge(freed_a.sem, self.fa + T)
                pe.wait_ge(freed_d.sem, self.fd + 1)
                for t in range(T):
                    b = t // 2
                    if t % 2 == 0:
                        ring.ready(pe, self.blocks + b)
                    w = WB[:, (self.blocks + b) % RING, 0:512 * T].rearrange("p (a n) -> p a n", n=256)
                    for k in range(T):
                        for f in range(2):
                            c0 = (t % 2) * P
                            last = nc.tensor.matmul(PS[:, t, 0:256].rearrange("p (c n) -> p c n", c=2),
                                                    w[:, 2 * k + f, c0:c0 + P], self.fa_[:, k, f:4:2, :],
                                                    start=(k == 0 and f == 0), stop=(k == T - 1 and f == 1))
                    last.then_inc(mm.sem, 1)
                    if t % 2 == 1:
                        pe.drain().then_inc(block_used.sem, 1)
                pe.wait_ge(normed.sem, self.nm + 3)
                for h in range(4):
                    pe.wait_ge(freed_a.sem, self.fa + T + min(T, h + 2))
                    nc.tensor.matmul(PS[:, 1 + h, 0:64 * T].rearrange("p (t d) -> p t d", d=64), WST[:, h, :],
                                     self.vn[:, :, 64 * h:64 * h + 64], start=True, stop=True).then_inc(mm.sem, 1)

            def scalar(self, act):
                T = self.T
                for t in range(T):
                    act.wait_ge(mm.sem, self.mm + t + 1)
                    nc.scalar.activation(self.fa_[:, t, :, :], PS[:, t, :].rearrange("p (a b) -> p a b", a=4),
                                         ACT.Copy).then_inc(freed_a.sem, 1)
                act.wait_ge(normed.sem, self.nm + 1)
                nc.scalar.activation(stat(32, 32 + 4 * T), stat(0, 4 * T), ACT.Sqrt, bias=EPSC[:, :],
                                     scale=1.0 / 64).then_inc(roots.sem, 1)
                act.wait_ge(normed.sem, self.nm + 2)
                for t in range(T):
                    act.wait_ge(mm.sem, self.mm + T + 1 + t + 1)
                    nc.scalar.activation(self.px[:, t, G0:F0], PS[:, t, 0:256], ACT.Copy, scale=self.scale).then_inc(freed_a.sem, 1)

            def rotate_rows(self, dve, t):
                x = self.px[:, t, 0:640]
                cos = ROPE[:, 0, 64 * t:64 * t + 64].unsqueeze(1).broadcast_to([P, 10, 64])
                rotate(dve, x.rearrange("p (h d) -> p h d", d=64), cos, ROPE[:, 1, 64 * t:64 * t + 64], 10, 2, 16,
                       self.t1, self.t2)

            def vector(self, dve):
                T, px = self.T, self.px
                g = px[:, :, G0:F0]
                dstep(dve, nc.vector.tensor_tensor(self.vn, g, g, ALU.mult))
                sq = self.vn.rearrange("p t (h d) -> p t h d", d=64)
                nc.vector.tensor_reduce(stat(0, 4 * T).rearrange("p (t h) -> p t h", h=4), sq, AX_X, ALU.add).then_inc(normed.sem, 1)
                dve.wait_ge(mm.sem, self.mm + T + 1)
                nc.vector.tensor_copy(WST[:, :, :], PS[:, 0, :].rearrange("p (h q) -> p h q", h=4)).then_inc(freed_d.sem, 1)
                dve.wait_ge(roots.sem, self.rt + 1)
                dstep(dve, nc.vector.reciprocal(stat(64, 64 + 4 * T), stat(32, 32 + 4 * T)))
                r = stat(64, 64 + 4 * T).rearrange("p (t h) -> p t h", h=4).unsqueeze(3).broadcast_to([P, T, 4, 64])
                nc.vector.tensor_tensor(sq, g.rearrange("p t (h d) -> p t h d", d=64), r, ALU.mult).then_inc(normed.sem, 1)
                dve.wait_ge(normed.sem, self.nm + 2)
                gb = GSGU[:, :].unsqueeze(1).broadcast_to([P, T, 256])
                nc.vector.tensor_tensor(self.vn, self.vn, gb, ALU.mult).then_inc(normed.sem, 1)
                if T == 8:
                    for t in range(T):
                        self.rotate_rows(dve, t)
                for h in range(4):
                    dve.wait_ge(mm.sem, self.mm + 2 * T + 2 + h)
                    u = px[:, :, U0 + 64 * h:U0 + 64 * h + 64]
                    nc.vector.scalar_tensor_tensor(u, PS[:, 1 + h, 0:64 * T].rearrange("p (t d) -> p t d", d=64),
                                                   VEC[:, self.l, ROW_BSGU + h:ROW_BSGU + h + 1], u, ALU.add, ALU.mult)

        class Attention(Stage):

            def __init__(self, trips, heads, T, dim, scale, sq, qt, sbuf, pts, steps, sk=None, kt=None,
                         stage=None, stage_k=None, keys=None, values=None, out=None, local=None, ctx_keys=0,
                         sink=None, masked=False, wide=0):
                self.trips, self.heads, self.T, self.dim, self.scale = trips, heads, T, dim, scale
                self.sq, self.qt, self.sb, self.pts, self.sk, self.kt = sq, qt, sbuf, pts, sk, kt
                self.stage, self.stage_k, self.keys, self.values, self.out = stage, stage_k, keys, values, out
                self.local, self.ctx_keys, self.sink, self.masked, self.wide = local, ctx_keys, sink, masked, wide
                self.steps = steps
                self.U = heads * T
                n = trips * self.U
                self.b = {s: s.span(n) for s in (s_score, s_max, s_prob, s_pt, s_pta, s_ptd, s_pv, s_out)}
                self.c = {s: s.span(trips) for s in (s_staged, s_turned, s_qt, s_kt)}

            def at(self, s, i, u):
                return self.b[s] + i * self.U + u

            def blocks(self, t):
                lo, hi = self.local(t) if self.local else (0, 0)
                return lo, hi

            def widths(self, t):
                lo, hi = self.blocks(t)
                return P * (hi - lo), self.ctx_keys

            def units(self):
                return [(h, t) for h in range(self.heads) for t in range(self.T)]

            def turns(self):
                q = []
                packed = self.dim == 64
                n = self.heads // 2 if packed else self.heads
                w = P if packed else self.dim
                return n, w

            def tensor(self, pe):
                with pe.Fori(0, self.trips) as i:
                    n, w = self.turns()
                    pe.wait_ge(s_staged.sem, self.c[s_staged] + i + 1)
                    per = max(1, self.T * P // BANK)
                    for j in range(n):
                        for t in range(self.T):
                            c = j * self.T * P + t * P
                            last = nc.tensor.transpose(PS[0:w, c // BANK, c % BANK:c % BANK + P],
                                                       self.sq[:, t, w * j:w * j + w], IDENT[:, :])
                    if self.sk is not None:
                        for j in range(n):
                            for t in range(self.T):
                                c = 4 * BANK + j * self.T * P + t * P
                                last = nc.tensor.transpose(PS[0:w, c // BANK, c % BANK:c % BANK + P],
                                                           self.sk[:, t, w * j:w * j + w], IDENT[:, :])
                    last.then_inc(s_turned.sem, 1)
                    pe.wait_ge(s_qt.sem, self.c[s_qt] + i + 1)
                    pe.wait_ge(s_kt.sem, self.c[s_kt] + i + 1)
                    units = self.units()
                    U = self.U
                    for s in range(U + 3):
                        if 2 <= s < U + 2:
                            u = s - 2
                            h, t = units[u]
                            lw, cw = self.widths(t)
                            pe.wait_ge(s_prob.sem, self.at(s_prob, i, u + 1))
                            if u >= 1:
                                pe.wait_ge(s_pta.sem, self.at(s_pta, i, u))
                                pe.wait_ge(s_ptd.sem, self.at(s_ptd, i, u))
                            nb = (lw + cw) // P
                            share = (nb + 1) // 2
                            for j in range(nb):
                                bank, c = (4, P * j) if j < share else (5, P * (j - share))
                                last = nc.tensor.transpose(PS[:, bank, c:c + P],
                                                           self.sb[:, u % 2, P * j:P * j + P], IDENT[:, :])
                            last.then_inc(s_pt.sem, 1)
                        if s < U:
                            h, t = units[s]
                            q = self.query(h, t)
                            bank = 2 * (s % 2)
                            for dst, rhs in self.keys(h, t, PS[:, bank, :], PS[:, bank + 1, :]):
                                last = nc.tensor.matmul(dst, q, rhs, start=True, stop=True)
                            last.then_inc(s_score.sem, 1)
                        if s >= 3:
                            u = s - 3
                            h, t = units[u]
                            lw, cw = self.widths(t)
                            nb = (lw + cw) // P
                            pe.wait_ge(s_pta.sem, self.at(s_pta, i, u + 1))
                            pe.wait_ge(s_ptd.sem, self.at(s_ptd, i, u + 1))
                            if u >= 2:
                                pe.wait_ge(s_out.sem, self.at(s_out, i, u - 1))
                            for j in range(nb):
                                last = nc.tensor.matmul(PS[:, 6 + u % 2, 0:64], self.pts[:, u % 2, P * j:P * j + P],
                                                        self.values(i, h, t, j), start=(j == 0), stop=(j == nb - 1))
                            last.then_inc(s_pv.sem, 1)

            def query(self, h, t):
                if self.dim == 64:
                    b = 64 * (h % 2)
                    c = (h // 2) * self.T * P + t * P
                    return self.qt[b:b + 64, c:c + P]
                c = h * self.T * P + t * P
                return self.qt[0:self.dim, c:c + P]

            def split(self, t):
                lw, cw = self.widths(t)
                nb = (lw + cw) // P
                return P * ((nb + 1) // 2), P * nb

            def scalar(self, act):
                with act.Fori(0, self.trips) as i:
                    n, w = self.turns()
                    act.wait_ge(s_turned.sem, self.c[s_turned] + i + 1)
                    cols = n * self.T * P
                    nbank = max(1, cols // BANK)
                    if cols >= BANK:
                        src = PS[0:w, 0:nbank, :]
                        dst = self.qt[0:w, 0:cols].rearrange("p (a b) -> p a b", b=BANK)
                    else:
                        src, dst = PS[0:w, 0, 0:cols], self.qt[0:w, 0:cols]
                    nc.scalar.activation(dst, src, ACT.Copy).then_inc(s_qt.sem, 1)
                    units = self.units()
                    U = self.U
                    for s in range(U + 2):
                        if s >= 2:
                            u = s - 2
                            h, t = units[u]
                            a, b = self.split(t)
                            act.wait_ge(s_pt.sem, self.at(s_pt, i, u + 1))
                            if u >= 2:
                                act.wait_ge(s_pv.sem, self.at(s_pv, i, u - 1))
                            nc.scalar.activation(self.pts[:, u % 2, 0:a], PS[:, 4, 0:a], ACT.Copy).then_inc(s_pta.sem, 1)
                        if s < U:
                            h, t = units[s]
                            u = s
                            lw, cw = self.widths(t)
                            act.wait_ge(s_max.sem, self.at(s_max, i, s + 1))
                            nm = STAT[:, 8 + u % 2:9 + u % 2]
                            den = 16 + 4 * (u % 2)
                            ops = []
                            if lw:
                                ops.append((self.sb[:, u % 2, 0:lw], self.sb[:, u % 2, 0:lw], 1.0))
                            if cw:
                                if self.local:
                                    src = PS[:, 2 * (u % 2) + 1, 0:cw]
                                    dst = self.sb[:, u % 2, lw:lw + cw]
                                elif cw > BANK:
                                    src = PS[:, 2 * (u % 2):2 * (u % 2) + 2, :]
                                    dst = self.sb[:, u % 2, 0:cw].rearrange("p (a b) -> p a b", b=BANK)
                                else:
                                    src = PS[:, 2 * (u % 2) + 1, 0:cw]
                                    dst = self.sb[:, u % 2, 0:cw]
                                ops.append((dst, src, self.scale))
                            if self.sink is not None:
                                ops.append((stat(den + 3, den + 4), stat(24 + h, 25 + h), 1.0))
                            for n_, (dst, src, sc) in enumerate(ops):
                                ins = nc.scalar.activation(dst, src, ACT.Exp, bias=nm, scale=sc,
                                                           accum_out=stat(den + n_, den + n_ + 1))
                            self.nden = len(ops)
                            ins.then_inc(s_prob.sem, 1)

            def vector(self, dve):
                nden = (1 if self.local or self.masked else 0) + (1 if self.ctx_keys else 0) + (1 if self.sink is not None else 0)
                with dve.Fori(0, self.trips) as i:
                    steps_d.loop(i, self.steps)
                    self.stage(i).then_inc(s_staged.sem, 1)
                    if self.stage_k:
                        self.stage_k(i).then_inc(s_kt.sem, 1)
                    else:
                        n, w = self.turns()
                        dve.wait_ge(s_turned.sem, self.c[s_turned] + i + 1)
                        cols = n * self.T * P
                        nc.vector.tensor_copy(self.kt[0:w, 0:cols].rearrange("p (a b) -> p a b", b=BANK),
                                              PS[0:w, 4:4 + cols // BANK, :]).then_inc(s_kt.sem, 1)
                    units = self.units()
                    U = self.U
                    for s in range(U + 3):
                        if 2 <= s < U + 2:
                            u = s - 2
                            h, t = units[u]
                            a, b = self.split(t)
                            dve.wait_ge(s_pt.sem, self.at(s_pt, i, u + 1))
                            if u >= 2:
                                dve.wait_ge(s_pv.sem, self.at(s_pv, i, u - 1))
                            nc.vector.tensor_copy(self.pts[:, u % 2, a:b], PS[:, 5, 0:b - a]).then_inc(s_ptd.sem, 1)
                            den = 16 + 4 * (u % 2)
                            rd = stat(12 + u % 2, 13 + u % 2)
                            dv = stat(14 + u % 2, 15 + u % 2)
                            if nden > 1:
                                dstep(dve, nc.vector.reduce_sum(dv, stat(den, den + nden), AX_X))
                                dstep(dve, nc.vector.reciprocal(rd, dv))
                            else:
                                if u >= 2:
                                    dve.wait_ge(s_out.sem, self.at(s_out, i, u - 1))
                                dstep(dve, nc.vector.reciprocal(rd, stat(den, den + 1)))
                        if s < U:
                            h, t = units[s]
                            u = s
                            lw, cw = self.widths(t)
                            mx, mc, nm = stat(0 + u % 2, 1 + u % 2), stat(2 + u % 2, 3 + u % 2), stat(8 + u % 2, 9 + u % 2)
                            mt = stat(4 + u % 2, 5 + u % 2)
                            dve.wait_ge(s_score.sem, self.at(s_score, i, s + 1))
                            bank = 2 * (u % 2)
                            if lw:
                                src, mask, dst = self.masked_rows(t, bank, u, lw)
                                dstep(dve, nc.vector.scalar_tensor_tensor(dst, src, self.scale, mask, ALU.mult, ALU.add))
                                dstep(dve, nc.vector.tensor_reduce(mx, self.sb[:, u % 2, 0:lw], AX_X, ALU.max))
                            if cw:
                                src = PS[:, bank:bank + 2, :] if cw > BANK else PS[:, bank + 1, 0:cw]
                                dstep(dve, nc.vector.tensor_reduce(mc, src, mybir.AxisListType.XY if cw > BANK else AX_X, ALU.max))
                            top = mx
                            if lw and cw:
                                dstep(dve, nc.vector.scalar_tensor_tensor(mt, mc, self.scale, mx, ALU.mult, ALU.max))
                                top, sc = mt, 1.0
                            elif cw:
                                top, sc = mc, self.scale
                            else:
                                top, sc = mx, 1.0
                            if self.sink is not None:
                                m2 = stat(6 + u % 2, 7 + u % 2)
                                dstep(dve, nc.vector.scalar_tensor_tensor(m2, top, sc, stat(24 + h, 25 + h), ALU.mult, ALU.max))
                                top, sc = m2, 1.0
                            nc.vector.tensor_scalar(nm, top, -sc, None, ALU.mult).then_inc(s_max.sem, 1)
                        if s >= 3:
                            u = s - 3
                            h, t = units[u]
                            dve.wait_ge(s_pv.sem, self.at(s_pv, i, u + 1))
                            nc.vector.tensor_scalar(self.out(i, h, t), PS[:, 6 + u % 2, 0:64],
                                                    stat(12 + u % 2, 13 + u % 2), None, ALU.mult).then_inc(s_out.sem, 1)
                    steps_d.loop_end(self.trips)

            def masked_rows(self, t, bank, u, lw):
                if self.wide:
                    src = PS[:, bank:bank + 2, :]
                    off = 896 - P * t
                    mask = self.masked[:, off:off + lw].rearrange("p (a b) -> p a b", b=BANK)
                    return src, mask, self.sb[:, u % 2, 0:lw].rearrange("p (a b) -> p a b", b=BANK)
                lo, hi = self.local(t)
                off = P * (lo - (t - 1))
                return PS[:, bank, 0:lw], self.masked[:, off:off + lw], self.sb[:, u % 2, 0:lw]

        def layer_attention(l, px, ft, T, window):
            kt2 = area(0, 2, 1024)
            sq = area(2048, T, 256)
            qt = area(4096, 2048)
            kts = area(6144, 1024)
            kcs = area(7168, 256)
            sbuf = area(2048, 2, 640)
            pts = ft[:, :, :].rearrange("p a b -> p (a b)")[:, 0:1280].rearrange("p (a b) -> p a b", a=2) if T == 8 else area(18432, 2, 256)
            if T != 8:
                sbuf = area(2048, 2, 256)

            def stage(i):
                nc.vector.tensor_copy(STAT[:, 24:28], SINK[:, l, bass.ts(i, 4)])
                return nc.vector.tensor_copy(sq, px[:, :, bass.ts(i, 256)])

            def stage_k(i):
                if window:
                    nc.vector.tensor_copy(kts.unsqueeze(1), kt2[:, bass.ts(i, 1), :])
                return nc.vector.tensor_copy(kcs.unsqueeze(1), KCT[:, bass.ts(i, 1), :])

            def local(t):
                return (max(t - 1, 0), min(t + 1, T - 1) + 1) if window else (0, 0)

            def keys(h, t, bank_a, bank_b):
                b = 64 * (h % 2)
                ops = []
                if window:
                    lo, hi = local(t)
                    ops.append((bank_a[:, 0:P * (hi - lo)], kts[b:b + 64, P * lo:P * hi]))
                ops.append((bank_b[:, 0:256], kcs[b:b + 64, :]))
                return ops

            def values(i, h, t, j):
                lo, hi = local(t)
                if j < hi - lo:
                    return px[:, lo + j, bass.ds(i * 64 + V0, 64)]
                return VC[:, j - (hi - lo), bass.ts(i, 64)]

            def out_(i, h, t):
                return px[:, t, bass.ds(i * 256 + 64 * h, 64)]

            return Attention(2, 4, T, 64, 0.125, sq, qt, sbuf, pts, steps=32 * 7 if window else 8 * 4,
                             stage=stage, stage_k=stage_k, keys=keys, values=values, out=out_, local=local if window else None,
                             ctx_keys=256, sink=SINK, masked=WMASK if window else False)

        class MergeNorm(Stage):

            def __init__(self, px, T, spread):
                self.px, self.T, self.spread = px, T, spread
                self.H = max(1, T // 4)
                self.per = T // self.H
                self.parts = ((0, 512), (U0, G0), (G0, F0))
                self.sq = squares.span(3 * self.H)
                self.rt = roots.span(self.H)
                self.junk = area(0, T, D)

            def tensor(self, pe):
                self.spread.tensor(pe)

            def scalar(self, act):
                for h in range(self.H):
                    t0, t1 = self.per * h, self.per * (h + 1)
                    for p_, (a, b) in enumerate(self.parts):
                        o = (0, 512, 768)[p_]
                        for t in range(t0, t1):
                            ins = nc.scalar.activation(self.junk[:, t, o:o + b - a], self.px[:, t, a:b], ACT.Square,
                                                       accum_out=stat(8 * p_ + t, 8 * p_ + t + 1))
                        ins.then_inc(squares.sem, 1)
                    act.wait_ge(squares.sem, self.sq + 3 * (h + 1))
                    for p_, (a, b) in enumerate(self.parts):
                        o = 8 * p_
                        ins = nc.scalar.activation(stat(32 + o + t0, 32 + o + t1), stat(o + t0, o + t1), ACT.Sqrt,
                                                   bias=EPSC[:, :], scale=1.0 / (b - a))
                    ins.then_inc(roots.sem, 1)

            def vector(self, dve):
                self.spread.vector(dve)
                for h in range(self.H):
                    t0, t1 = self.per * h, self.per * (h + 1)
                    dve.wait_ge(roots.sem, self.rt + h + 1)
                    for p_ in range(3):
                        o = 8 * p_
                        ins = nc.vector.reciprocal(stat(64 + o + t0, 64 + o + t1), stat(32 + o + t0, 32 + o + t1))
                    dstep(dve, ins)
                    for p_, (a, b) in enumerate(self.parts):
                        for t in range(t0, t1):
                            nc.vector.tensor_scalar(self.px[:, t, a:b], self.px[:, t, a:b],
                                                    stat(64 + 8 * p_ + t, 65 + 8 * p_ + t), None, ALU.mult)

        class Turn(Stage):

            def __init__(self, T, src, dst, gain):
                self.T, self.src, self.dst, self.gain = T, src, dst, gain
                self.H = max(1, T // 4)
                self.per = T // self.H
                self.G = self.H * KD
                self.mm = mm.span(self.G)
                self.fa = freed_a.span(self.G // 2)
                self.fd = freed_d.span(self.G // 2)

            def tensor(self, pe):
                for g in range(self.G):
                    h, c = g // KD, g % KD
                    if g >= 8:
                        src, base = (freed_d, self.fd) if g % 2 else (freed_a, self.fa)
                        pe.wait_ge(src.sem, base + (g - 8) // 2 + 1)
                    for j in range(self.per):
                        last = nc.tensor.transpose(PS[:, g % 8, P * j:P * j + P], self.src(self.per * h + j, c), IDENT[:, :])
                    last.then_inc(mm.sem, 1)

            def scalar(self, act):
                n = self.per * P
                for g in range(0, self.G, 2):
                    h, c = g // KD, g % KD
                    act.wait_ge(mm.sem, self.mm + g + 1)
                    nc.scalar.activation(self.dst(c, n * h, n * h + n), PS[:, g % 8, 0:n], ACT.Copy,
                                         scale=self.gain[:, c:c + 1] if self.gain is not None else 1.0).then_inc(freed_a.sem, 1)

            def vector(self, dve):
                n = self.per * P
                for g in range(1, self.G, 2):
                    h, c = g // KD, g % KD
                    dve.wait_ge(mm.sem, self.mm + g + 1)
                    if self.gain is not None:
                        ins = nc.vector.tensor_scalar(self.dst(c, n * h, n * h + n), PS[:, g % 8, 0:n], self.gain[:, c:c + 1], None, ALU.mult)
                    else:
                        ins = nc.vector.tensor_copy(self.dst(c, n * h, n * h + n), PS[:, g % 8, 0:n])
                    ins.then_inc(freed_d.sem, 1)

        class Beside(Stage):

            def __init__(self, *parts):
                self.parts = parts

            def load(self, sp):
                for part in self.parts:
                    part.load(sp)

            def tensor(self, pe):
                for part in self.parts:
                    part.tensor(pe)

            def vector(self, dve):
                for part in self.parts:
                    part.vector(dve)

            def scalar(self, act):
                for part in self.parts:
                    part.scalar(act)

            def pool(self, gp):
                for part in self.parts:
                    part.pool(gp)

        class Spread(Stage):

            def __init__(self, col, dst, scratch, bank=0):
                self.col, self.dst, self.dg, self.bank = col, dst, scratch, bank
                self.mm = mm.span(1)
                self.sd = s_diag.span(1)

            def vector(self, dve):
                for c in range(8):
                    ins = nc.vector.tensor_scalar(self.dg[:, P * c:P * c + P], IDENT[:, :], self.col[:, c:c + 1], None, ALU.mult)
                ins.then_inc(s_diag.sem, 1)
                dve.wait_ge(mm.sem, self.mm + 1)
                nc.vector.tensor_copy(self.dst.rearrange("p (a b) -> p a b", b=BANK), PS[:, self.bank:self.bank + 2, :])

            def tensor(self, pe):
                pe.wait_ge(s_diag.sem, self.sd + 1)
                for n in range(2):
                    last = nc.tensor.matmul(PS[:, self.bank + n, :], ONES[:, :], self.dg[:, 512 * n:512 * n + 512], start=True, stop=True)
                last.then_inc(mm.sem, 1)

        class OutProduct(Stage):

            def __init__(self, w, mt, x, T, rms, scratch):
                self.w, self.mt, self.x, self.T, self.rms = w, mt, x, T, rms
                self.blocks = ring.take(2)
                self.mm = mm.span(T)
                self.sq = squares.span(T if rms else 0)
                self.rt = roots.span(T if rms else 0)
                self.fd = freed_d.span(T)
                self.tmp = scratch
                self.junk = scratch[:, 2048:3072]

            def load(self, sp):
                for b in range(2):
                    ring.load(sp, self.blocks + b, rows_of(self.w, 512 * b, 512 * b + 512), SLOT)

            def banks(self, t):
                return PS[:, 2 * (t % 4):2 * (t % 4) + 2, :]

            def tensor(self, pe):
                for b in range(2):
                    ring.ready(pe, self.blocks + b)
                for t in range(self.T):
                    if t >= 4:
                        pe.wait_ge(freed_d.sem, self.fd + t - 3)
                    for b in range(2):
                        for k in range(KD):
                            last = nc.tensor.matmul(self.banks(t)[:, b, :], self.mt[:, k, P * t:P * t + P],
                                                    ring.view(self.blocks + b, 8)[:, k, :], start=(k == 0), stop=(k == KD - 1))
                    last.then_inc(mm.sem, 1)
                pe.drain().then_inc(block_used.sem, 2)

            def scalar(self, act):
                if not self.rms:
                    return
                for t in range(self.T):
                    act.wait_ge(mm.sem, self.mm + t + 1)
                    nc.scalar.activation(self.junk.rearrange("p (a b) -> p a b", b=BANK), self.banks(t), ACT.Square,
                                         accum_out=stat(t, t + 1)).then_inc(squares.sem, 1)
                    act.wait_ge(squares.sem, self.sq + t + 1)
                    nc.scalar.activation(stat(8 + t, 9 + t), stat(t, t + 1), ACT.Sqrt, bias=EPSC[:, :], scale=1.0 / D).then_inc(roots.sem, 1)

            def vector(self, dve):
                gate = GATE[:, :].rearrange("p (a b) -> p a b", b=BANK)
                for t in range(self.T):
                    tmp = self.tmp[:, 1024 * (t % 2):1024 * (t % 2) + 1024]
                    tv = tmp.rearrange("p (a b) -> p a b", b=BANK)
                    if self.rms:
                        dve.wait_ge(roots.sem, self.rt + t + 1)
                        dstep(dve, nc.vector.reciprocal(stat(16 + t, 17 + t), stat(8 + t, 9 + t)))
                        ins = nc.vector.scalar_tensor_tensor(tv, self.banks(t), stat(16 + t, 17 + t), gate, ALU.mult, ALU.mult)
                    else:
                        dve.wait_ge(mm.sem, self.mm + t + 1)
                        ins = nc.vector.tensor_tensor(tv, self.banks(t), gate, ALU.mult)
                    ins.then_inc(freed_d.sem, 1)
                    dve.wait_ge(freed_d.sem, self.fd + t + 1)
                    nc.vector.tensor_tensor(self.x[:, t, :], self.x[:, t, :], tmp, ALU.add)

        class Mlp(Stage):

            def __init__(self, l, T, acc, hid, coming=None):
                self.l, self.T, self.acc, self.hid, self.coming = l, T, acc, hid, coming
                self.H = max(1, T // 4)
                self.N = P * T // self.H
                self.G = 4 * self.H + 2 * T
                assert self.G % 8 == 0
                self.trips = FF // 1024
                self.per = 4 if coming is None else 8
                self.blocks = ring.take(self.per * self.trips)
                self.mm = mm.span(2 * self.G * self.trips)
                assert freed_d.planned >= 8
                self.fd = freed_d.span(2 * self.G * self.trips)
                self.hd = hid_done.span(8 * self.H * self.trips)
                self.z = zeroed.span(1)
                if coming is not None:
                    self.cond = (0, 1) if coming < 2 else (2,)
                    self.wada = A["w_ada"][coming] if coming < 2 else A["w_ada_2"][0]
                    self.nops = 16 * len(self.cond)
                    self.sums = mod_sums.span(2 * self.nops * self.trips)
                    self.cols = mod_columns.span(2 * self.trips + 1)
                    self.kept = mod_kept.span(2 * self.trips + 1)

            def load(self, sp):
                w1, w2 = A["w_ff1"][self.l], A["w_ff2"][self.l]
                with sp.Fori(0, self.trips) as i:
                    for b in range(2):
                        c = i * 1024 + 512 * b
                        n = self.block(b)
                        more = self.per * i
                        ring.load(sp, n, w1[:, bass.ds(c, 512)].rearrange("(k p) n -> p k n", p=P), SLOT, more=more)
                        ring.load(sp, n + 1, w2[bass.ds(c, 512), :].rearrange("(k p) n -> p k n", p=P), SLOT, more=more)
                        if self.coming is not None:
                            for a in range(2):
                                src = self.wada[:, bass.ds(i * 1536 + 768 * b + 384 * a, 384)]
                                ring.load(sp, n + 2 + a, src.rearrange("(k p) n -> p k n", p=P), 3072, more=more)

            def block(self, b):
                return self.blocks + self.per // 2 * b

            def ada(self, b, a):
                slot = WB[:, (self.block(b) + 2 + a) % RING, :]
                return slot[:, 0:3072].rearrange("p (k n) -> p k n", k=8), slot[:, 3072:3072 + 384 * len(self.cond)].rearrange(
                    "p (s n) -> p s n", n=384)

            def groups(self):
                g = [("hid", c, h) for h in range(self.H) for c in range(4)]
                return g + [("out", t, n) for t in range(self.T) for n in range(2)]

            def tensor(self, pe):
                G, H = self.G, self.H
                with pe.Fori(0, self.trips) as i:
                    for b in range(2):
                        n1 = self.block(b)
                        w1, w2 = ring.view(n1, 8), ring.view(n1 + 1, 4)
                        for m, (kind, x, y) in enumerate(self.groups()):
                            g = b * G + m
                            if m == 0:
                                ring.ready(pe, n1, i, self.per)
                                if self.coming is not None:
                                    pe.wait_ge(mod_kept.sem, self.kept + 2 * i + b + 1)
                            if m == 4 * H:
                                ring.ready(pe, n1 + 1, i, self.per)
                            if self.coming is not None and m == G - 2:
                                self.sum_partitions(pe, i, b)
                            pe.wait_ge(freed_d.sem, self.fd + i * 2 * G + g - 7)
                            if kind == "hid":
                                for k in range(KD):
                                    last = nc.tensor.matmul(PS[:, g % 8, 0:self.N], w1[:, k, P * x:P * x + P],
                                                            HT[:, k, self.N * y:self.N * y + self.N], start=(k == 0), stop=(k == KD - 1))
                                last.then_inc(mm.sem, 1)
                                if m == 4 * H - 1:
                                    pe.drain().then_inc(block_used.sem, 1)
                            else:
                                h = x * P // self.N
                                if y == 0 and (x * P) % self.N == 0:
                                    pe.wait_ge(hid_done.sem, self.hd + i * 8 * H + b * 4 * H + 4 * (h + 1))
                                for k in range(4):
                                    last = nc.tensor.matmul(PS[:, g % 8, :], self.hid[:, k, P * x:P * x + P],
                                                            w2[:, k, 512 * y:512 * y + 512], start=(k == 0), stop=(k == 3))
                                last.then_inc(mm.sem, 1)
                        pe.drain().then_inc(block_used.sem, 1 if self.coming is None else 3)

            def sum_partitions(self, pe, i, b):
                pe.wait_ge(mod_sums.sem, self.sums + i * 2 * self.nops + (b + 1) * self.nops)
                pe.wait_ge(freed_d.sem, self.fd + i * 2 * self.G + (b + 1) * self.G - 7)
                for a in range(2):
                    sums = self.ada(b, a)[1]
                    for si in range(len(self.cond)):
                        for j in range(3):
                            c = 6 * si + 3 * a + j
                            last = nc.tensor.matmul(PS[:, 0, c:c + 1], sums[:, si, P * j:P * j + P], ONES[:, 0:1],
                                                    start=True, stop=True)
                last.then_inc(mod_columns.sem, 1)

            def add_rows(self, dve, i, b, o):
                nv = len(self.cond)
                a, k, si = o // (8 * nv), o // nv % 8, o % nv
                w, sums = self.ada(b, a)
                col = SC[:, self.cond[si], k:k + 1]
                if k == 0:
                    if si == 0:
                        ring.ready(dve, self.block(b) + 2 + a, i, self.per)
                        dve.wait_ge(mod_columns.sem, self.cols + 2 * i + b + 1)
                    ins = nc.vector.tensor_scalar(sums[:, si, :], w[:, k, :], col, None, ALU.mult)
                else:
                    dve.wait_ge(mod_sums.sem, self.sums + i * 2 * self.nops + b * self.nops + o - nv + 1)
                    ins = nc.vector.scalar_tensor_tensor(sums[:, si, :], w[:, k, :], col, sums[:, si, :], ALU.mult, ALU.add)
                ins.then_inc(mod_sums.sem, 1)

            def keep_columns(self, dve, i, b):
                dve.wait_ge(mod_columns.sem, self.cols + 2 * i + b + 2)
                n = 6 * len(self.cond)
                nc.vector.tensor_copy(MODN[:, 0:len(self.cond), bass.ds(i * 12 + 6 * b, 6)],
                                      PS[:, 0, 0:n].rearrange("p (s j) -> p s j", j=6)).then_inc(mod_kept.sem, 1)

            def pool(self, gp):
                nc.gpsimd.memset(self.acc, 0.0).then_inc(zeroed.sem, 1)

            def vector(self, dve):
                G, H = self.G, self.H
                dve.wait_ge(zeroed.sem, self.z + 1)
                if self.coming is not None:
                    dve.sem_inc(mod_columns.sem, 1)
                    dve.sem_inc(mod_kept.sem, 1)
                with dve.Fori(0, self.trips) as i:
                    for b in range(2):
                        for m, (kind, x, y) in enumerate(self.groups()):
                            g = b * G + m
                            if self.coming is not None and m == G - 2:
                                self.keep_columns(dve, i, b)
                            dve.wait_ge(mm.sem, self.mm + i * 2 * G + g + 1)
                            if kind == "hid":
                                nc.vector.tensor_scalar(self.hid[:, x, self.N * y:self.N * y + self.N], PS[:, g % 8, 0:self.N], 0.0, None,
                                                        ALU.max).then_inc(freed_d.sem, 1)
                            else:
                                a = self.acc[:, x, 512 * y:512 * y + 512]
                                if x == 0 and y == 0:
                                    dve.wait_ge(freed_d.sem, self.fd + i * 2 * G + g - 4 * H)
                                nc.vector.tensor_tensor(a, a, PS[:, g % 8, :], ALU.add).then_inc(freed_d.sem, 1)
                            if self.coming is not None:
                                n = G - 5
                                for o in range(m * self.nops // n, min((m + 1) * self.nops // n, self.nops)):
                                    self.add_rows(dve, i, b, o)

            def scalar(self, act):
                G, H = self.G, self.H
                with act.Fori(0, self.trips) as i:
                    for b in range(2):
                        for m, (kind, x, y) in enumerate(self.groups()):
                            if kind == "hid":
                                act.wait_ge(freed_d.sem, self.fd + i * 2 * G + b * G + m + 1)
                                v = self.hid[:, x, self.N * y:self.N * y + self.N]
                                nc.scalar.activation(v, v, ACT.Square).then_inc(hid_done.sem, 1)

        class AddNormed(Stage):

            def __init__(self, x, T, acc, junk):
                self.x, self.T, self.acc, self.junk = x, T, acc, junk
                self.sq = squares.span(T)
                self.rt = roots.span(T)

            def scalar(self, act):
                for t in range(self.T):
                    nc.scalar.activation(self.junk[:, t, :], self.acc[:, t, :], ACT.Square, accum_out=stat(t, t + 1)).then_inc(squares.sem, 1)
                    act.wait_ge(squares.sem, self.sq + t + 1)
                    nc.scalar.activation(stat(8 + t, 9 + t), stat(t, t + 1), ACT.Sqrt, bias=EPSC[:, :], scale=1.0 / D).then_inc(roots.sem, 1)

            def vector(self, dve):
                for t in range(self.T):
                    dve.wait_ge(roots.sem, self.rt + t + 1)
                    dstep(dve, nc.vector.reciprocal(stat(16 + t, 17 + t), stat(8 + t, 9 + t)))
                    a = self.acc[:, t, :]
                    dstep(dve, nc.vector.scalar_tensor_tensor(a, a, stat(16 + t, 17 + t), GATE[:, :], ALU.mult, ALU.mult))
                    nc.vector.tensor_tensor(self.x[:, t, :], self.x[:, t, :], a, ALU.add)

        def layer_stream(l, s, x, T):
            px = area(8192, T, 1280)
            ft = area(18432, 2, 1024) if T == 8 else area(16384, 2, 256)
            xn = area(8192, T, D)
            kt = area(0, 2, 1024) if T == 8 else KCT
            st = [Norm(x, T, DER[:, s, 0, :], MODC[:, s, 0:8], HT, xn),
                  input_projection(l, T, px, ft)]
            st += [Mixers(l, px, ft, T), TurnKeys(px, T, kt, K0, T == 2),
                   layer_attention(l, px, ft, T, T == 8), MergeNorm(px, T, Spread(DER[:, s, 2, :], GATE[:, :], area(18432, 1024)))]

            def mixed(t, c):
                a = P * c if c < 4 else U0 + P * (c - 4)
                return px[:, t, a:a + P]

            st += [Turn(T, mixed, lambda c, a, b: HT[:, c, a:b], VEC[:, l, ROW_MIX:ROW_MIX + 8]),
                   OutProduct(A["w_out"][l], HT, x, T, True, area(8192, 4096)),
                   Norm(x, T, DER[:, s, 1, :], MODC[:, s, 24:32], HT, xn),
                   Spread(DER[:, s, 3, :], GATE[:, :], area(8192, 1024)),
                   Mlp(l, T, area(8192, T, D), area(16384, 4, P * T), l + 1 if T == 8 else None),
                   AddNormed(x, T, area(8192, T, D), area(0, T, D))]
            return st

        def context_kv(l):
            px = area(8192, 2, 256)
            groups = [(0, (lambda n, k, t=t: (HT[:, k, P * t:P * t + P], WB[:, n % RING, 0:2048].rearrange("p (k n) -> p k n", k=8)[:, k, :])),
                       256, "dve", to(px[:, t, :])) for t in range(2)]
            return [Norm(XC, 2, DER[:, 1, 0, :], MODC[:, 1, 0:8], HT, area(10240, 2, D)),
                    Product([(rows_of(A["w_in"][l], K0, U0), 2048)], groups, KD),
                    TurnKeys(px, 2, KCT, 0, True)]

        class Rotations(Stage):

            def __init__(self):
                self.d = misc_dma.span(16)
                self.rt = roots.span(1)

            def pool(self, gp):
                gp.dma_start(x_spill, XF).then_inc(misc_dma.sem, 16)
                gp.wait_ge(misc_dma.sem, self.d + 16)

            def vector(self, dve):
                ang, k, k2 = area(20480, 8, 24), area(20672, 8, 24), area(20864, 8, 24)
                pos = VEC[:, 2, ROW2_POS:ROW2_POS + 8].unsqueeze(2).broadcast_to([P, 8, 24])
                dstep(dve, nc.vector.tensor_tensor(ang, pos, INV[:, :].unsqueeze(1).broadcast_to([P, 8, 24]), ALU.mult))
                magic = 12582912.0
                for quarter, r in ((0, area(21056, 8, 24)), (1, area(21248, 8, 24))):
                    dstep(dve, nc.vector.tensor_scalar(k, ang, 0.15915494309189535, 0.25 * quarter, ALU.mult, ALU.add))
                    dstep(dve, nc.vector.tensor_scalar(k2, k, magic, None, ALU.add))
                    dstep(dve, nc.vector.tensor_scalar(k, k2, -magic, None, ALU.add))
                    dstep(dve, nc.vector.scalar_tensor_tensor(k2, k, -6.28125, ang, ALU.mult, ALU.add))
                    dstep(dve, nc.vector.scalar_tensor_tensor(r, k, -0.0019350051879882812, k2, ALU.mult, ALU.add))
                    dstep(dve, nc.vector.scalar_tensor_tensor(k2, k, -3.0199159819532e-07, r, ALU.mult, ALU.add))
                    dstep(dve, nc.vector.tensor_scalar(r, k2, 1.5707963267948966 * quarter, 3.1415925, ALU.add, ALU.min))
                    ins = nc.vector.tensor_scalar(r, r, -3.1415925, None, ALU.max)
                    dstep(dve, ins)
                ins = nc.vector.tensor_copy(stat(0, 1), stat(0, 1))
                ins.then_inc(roots.sem, 1)

            def scalar(self, act):
                act.wait_ge(roots.sem, self.rt + 1)
                sin, cos = area(21056, 8, 24), area(21248, 8, 24)
                for src, c0, half, at, signs in ((cos, 0, 16, 0, (1.0, 1.0)), (sin, 0, 16, 32, (-1.0, 1.0)),
                                                 (cos, 16, 8, 64, (1.0, 1.0)), (sin, 16, 8, 80, (-1.0, 1.0))):
                    for j, sign in enumerate(signs):
                        nc.scalar.activation(ROPE2[:, :, at + half * j:at + half * j + half], src[:, :, c0:c0 + half], ACT.Sin, scale=sign)

        class RotateHeads(Stage):

            def __init__(self, xs, at, w, heads, table, keep=None):
                self.xs, self.at, self.w, self.heads, self.table, self.keep = xs, at, w, heads, table, keep

            def vector(self, dve):
                w = self.w
                for t in range(8):
                    cos = ROPE2[:, t, self.table:self.table + w].unsqueeze(1).broadcast_to([P, self.heads, w])
                    sin = ROPE2[:, t, self.table + w:self.table + 2 * w]
                    for x in self.xs:
                        rotate(dve, x[:, t, :, self.at:self.at + w], cos, sin, self.heads, 1, w // 2, xarea(7000, 512), xarea(7600, 512))

        class LoadTable(Stage):

            def __init__(self, dst, src, *spreads):
                self.dst, self.src, self.spreads = dst, src, spreads
                self.d = misc_dma.span(16)

            def pool(self, gp):
                gp.dma_start(self.dst, self.src).then_inc(misc_dma.sem, 16)
                gp.wait_ge(misc_dma.sem, self.d + 16)

            def tensor(self, pe):
                for spread in self.spreads:
                    spread.tensor(pe)

            def vector(self, dve):
                for spread in self.spreads:
                    spread.vector(dve)

        class Copy(Stage):
            def __init__(self, dst, src):
                self.dst, self.src = dst, src

            def vector(self, dve):
                nc.vector.tensor_copy(self.dst, self.src)

        class Rows(Stage):

            def __init__(self, xn, scale, shift, zero, wr, spreads):
                self.spreads = spreads
                self.wr = wr
                self.w_in = misc_dma.span(16)
                self.xn, self.scale, self.shift, self.zero = xn, scale, shift, zero
                self.nm = normed.span(8)
                self.d = out_dma.span(16)
                self.z = zeroed.span(1)
                self.s = s_scatter.span(48)

            def vector(self, dve):
                for t in range(8):
                    x = self.xn[:, t, :]
                    dstep(dve, nc.vector.tensor_tensor(x, x, self.scale, ALU.mult))
                    nc.vector.tensor_tensor(x, x, self.shift, ALU.add).then_inc(normed.sem, 1)
                dve.wait_ge(normed.sem, self.nm + 8)
                for spread in self.spreads:
                    spread.vector(dve)

            def scalar(self, act):
                act.wait_ge(normed.sem, self.nm + 8)
                act.dma_start(h2_dram.rearrange("(t p) d -> p t d", p=P), self.xn).then_inc(out_dma.sem, 16)
                act.wait_ge(out_dma.sem, self.d + 16)

            def pool(self, gp):
                nc.gpsimd.memset(self.zero, 0.0).then_inc(zeroed.sem, 1)
                gp.wait_ge(zeroed.sem, self.z + 1)
                with nc.allow_non_contiguous_dma(reason="16 columns of the router"):
                    gp.dma_start(self.wr, A["w_router_2"][0].rearrange("(k p) e -> p k e", p=P)).then_inc(misc_dma.sem, 16)
                gp.dma_start(y_dram.rearrange("(t p) d -> p t d", p=P),
                             self.zero.unsqueeze(1).broadcast_to([P, 8, D])).then_inc(s_scatter.sem, 48)
                gp.wait_ge(s_scatter.sem, self.s + 48)
                gp.wait_ge(misc_dma.sem, self.w_in + 16)

            def tensor(self, pe):
                pe.wait_ge(misc_dma.sem, self.w_in + 16)
                for t in range(8):
                    for k in range(8):
                        nc.tensor.matmul(PS[:, 0, N_EXP * t:N_EXP * t + N_EXP], HT[:, k, P * t:P * t + P], self.wr[:, k, :],
                                         start=(k == 0), stop=(k == 7))
                for spread in self.spreads:
                    spread.tensor(pe)

        class Route(Stage):

            def __init__(self, off):
                self.br = area(off + 128, N_EXP)
                self.lg = area(off + 144, 8, N_EXP)
                self.ex = area(off + 272, 8, N_EXP)
                self.aff = area(off + 400, 8, N_EXP)
                self.top = area(off + 528, 8)
                self.iota = area(off + 640, P)
                self.tok = area(off + 768, 8)
                self.pos = area(off + 776, N_EXP, 8)
                self.pair = area(off + 904, N_EXP, 8, 2)
                self.at = area(off + 2048, 1024)[0:N_EXP]
                self.work = area(off + 3072, 1024)[0:N_EXP]
                self.mask = area(off + 4096, 1024)[0:N_EXP]
                self.cum = area(off + 5120, 1024)[0:N_EXP]
                self.hot = [area(off + 6144 + 1024 * b, 8, P) for b in range(2)]
                self.d = misc_dma.span(16)
                self.mm = mm.span(2)
                self.rt = roots.span(1)
                self.z = zeroed.span(2)
                self.hotd = s_diag.span(N_EXP)
                self.used = s_turned.span(N_EXP)

            def pool(self, gp):
                gp.dma_start(self.br, A["b_router_2"][0].partition_broadcast(P)).then_inc(misc_dma.sem, 16)
                nc.gpsimd.iota(IOTA_I[:, 0:P], [[1, P]], base=0, channel_multiplier=0).then_inc(zeroed.sem, 1)
                nc.gpsimd.iota(IOTA_I[:, P:P + 8], [[P, 8]], base=0, channel_multiplier=1).then_inc(zeroed.sem, 1)
                gp.wait_ge(misc_dma.sem, self.d + 16)

            def tensor(self, pe):
                pe.wait_ge(normed_aff.sem, 1)
                for t in range(8):
                    last = nc.tensor.transpose(PS[0:N_EXP, 1 + t // 4, P * (t % 4):P * (t % 4) + P], self.aff[:, t, :], IDENT[:, :])
                last.then_inc(mm.sem, 1)
                pe.wait_ge(normed_aff.sem, 2)
                for t in range(8):
                    last = nc.tensor.transpose(PS[:, 3, N_EXP * t:N_EXP * t + N_EXP], self.cum[:, P * t:P * t + P],
                                               IDENT[0:N_EXP, 0:N_EXP])
                last.then_inc(mm.sem, 1)
                with pe.Fori(0, N_EXP // 2) as i:
                    for b in range(2):
                        pe.wait_ge(s_diag.sem, self.hotd + 2 * i + b + 1)
                        for t in range(8):
                            last = nc.tensor.matmul(PS[:, 4, bass.ds(i * 4 + 2 * b, 2)], self.hot[b][:, t, :],
                                                    self.pair[:, bass.ds(i * 2 + b, 1), t, :], start=(t == 0), stop=(t == 7))
                        last.then_inc(s_turned.sem, 1)

            def scalar(self, act):
                act.wait_ge(normed_lg.sem, 1)
                nc.scalar.activation(self.ex, self.lg, ACT.Exp).then_inc(roots.sem, 1)

            def vector(self, dve):
                dve.wait_ge(misc_dma.sem, self.d + 16)
                lg, top = self.lg, self.top
                dstep(dve, nc.vector.tensor_tensor(lg, PS[:, 0, 0:P].rearrange("p (t e) -> p t e", e=N_EXP),
                                                   self.br.unsqueeze(1).broadcast_to([P, 8, N_EXP]), ALU.add))
                dstep(dve, nc.vector.tensor_reduce(top, lg, AX_X, ALU.max))
                nc.vector.tensor_tensor(lg, lg, top.unsqueeze(2).broadcast_to([P, 8, N_EXP]), ALU.subtract).then_inc(normed_lg.sem, 1)
                dve.wait_ge(roots.sem, self.rt + 1)
                dstep(dve, nc.vector.tensor_reduce(stat(0, 8), self.ex, AX_X, ALU.add))
                dstep(dve, nc.vector.reciprocal(stat(8, 16), stat(0, 8)))
                nc.vector.tensor_tensor(self.aff, self.ex, stat(8, 16).unsqueeze(2).broadcast_to([P, 8, N_EXP]),
                                        ALU.mult).then_inc(normed_aff.sem, 1)
                dve.wait_ge(mm.sem, self.mm + 1)
                dstep(dve, nc.vector.tensor_copy(self.at.rearrange("p (a b) -> p a b", b=BANK), PS[0:N_EXP, 1:3, :]))
                best = stat(16, 24)[0:N_EXP]
                for r in range(CAP // 8):
                    src = self.at if r == 0 else self.work
                    dstep(dve, nc.vector.max(best, src))
                    dstep(dve, nc.vector.match_replace(self.work, best, src, -1.0))
                dstep(dve, nc.vector.tensor_tensor(self.mask, self.work, self.at, ALU.not_equal))
                dstep(dve, nc.vector.memset(self.work, 1.0))
                dstep(dve, nc.vector.tensor_tensor_scan(self.cum, self.work, self.mask, 0.0, ALU.mult, ALU.add))
                dstep(dve, nc.vector.tensor_tensor(self.cum, self.cum, self.mask, ALU.mult))
                nc.vector.tensor_scalar(self.cum, self.cum, -1.0, None, ALU.add).then_inc(normed_aff.sem, 1)
                dve.wait_ge(zeroed.sem, self.z + 2)
                nc.vector.tensor_copy(self.iota, IOTA_I[:, 0:P])
                dstep(dve, nc.vector.tensor_copy(self.tok, IOTA_I[:, P:P + 8]))
                nc.vector.tensor_copy(self.pair[:, :, :, 0], self.tok.unsqueeze(1).broadcast_to([P, N_EXP, 8]))
                nc.vector.tensor_copy(self.pair[:, :, :, 1], self.aff.rearrange("p t e -> p e t"))
                dve.wait_ge(mm.sem, self.mm + 2)
                dstep(dve, nc.vector.tensor_copy(self.pos, PS[:, 3, 0:P].rearrange("p (t e) -> p e t", e=N_EXP)))
                with dve.Fori(0, N_EXP // 2) as i:
                    for b in range(2):
                        dve.wait_ge(s_turned.sem, self.used + 2 * i + b - 1)
                        for t in range(8):
                            ins = nc.vector.tensor_scalar(self.hot[b][:, t, :], self.iota, self.pos[:, bass.ds(i * 2 + b, 1), t], None,
                                                          ALU.is_equal)
                        ins.then_inc(s_diag.sem, 1)
                dve.wait_ge(s_turned.sem, self.used + N_EXP)
                pairs = PS[:, 4, 0:2 * N_EXP].rearrange("p (e a) -> p e a", a=2)
                nc.vector.tensor_copy(IDX[:, :], pairs[:, :, 0])
                nc.vector.tensor_copy(GT[:, :], pairs[:, :, 1])

        class Experts(Stage):

            def __init__(self):
                self.xe = [area(1024 * b, 1024) for b in range(2)]
                self.xet = [area(2048 + 1024 * b, 8, P) for b in range(2)]
                self.sa = [area(4096 + 1024 * b, 1024) for b in range(2)]
                self.hg = [area(6144 + 1024 * b, 1024) for b in range(2)]
                self.hgt = [area(8192 + 1024 * b, 8, P) for b in range(2)]
                self.ye = [area(10240 + 1024 * b, 1024) for b in range(2)]
                self.blocks = ring.take(6 * N_EXP)
                self.b = {s: s.span(k) for s, k in ((s_scatter, 16 * N_EXP), (s_pt, 2 * N_EXP), (s_xet, N_EXP), (s_pta, 2 * N_EXP),
                                                    (s_ptd, 2 * N_EXP), (s_gu, 4 * N_EXP), (s_act, 2 * N_EXP),
                                                    (s_hid, 2 * N_EXP), (s_pv, N_EXP), (s_ye, N_EXP + 1))}

            def at(self, s, k, i, n):
                return self.b[s] + 2 * k * i + n

            def load(self, sp):
                with sp.Fori(0, N_EXP // 2) as i:
                    for b in range(2):
                        for j, (name, h) in enumerate((("w_gate_2", 0), ("w_up_2", 0), ("w_gate_2", 1), ("w_up_2", 1),
                                                       ("w_down_2", 0), ("w_down_2", 1))):
                            w = A[name][0].rearrange("e k n -> (e k) n")
                            src = w[bass.ds(i * 2048 + 1024 * b, 1024), 512 * h:512 * h + 512].rearrange("(k p) n -> p k n", p=P)
                            ring.load(sp, self.blocks + 6 * b + j, src, SLOT, more=12 * i)

            def trips(self, eng, body):
                with eng.Fori(0, N_EXP // 2 - 1) as i:
                    for b in range(2):
                        body(eng, i, b, True)
                for b in range(2):
                    body(eng, N_EXP // 2 - 1, b, b == 0)

            def turn_rows(self, pe, i, n):
                b = n % 2
                pe.wait_ge(s_gather[b].sem, i * 16 + 16 * (n // 2) + 16)
                for k in range(8):
                    last = nc.tensor.transpose(PS[:, k // 4, P * (k % 4):P * (k % 4) + P], self.xe[b][:, P * k:P * k + P],
                                               IDENT[:, :])
                last.then_inc(s_xet.sem, 1)

            def gate_up(self, pe, i, b, h, f):
                n = self.blocks + 6 * b + 2 * h + f
                ring.ready(pe, n, i, 12)
                w = ring.view(n, 8)
                for k in range(8):
                    last = nc.tensor.matmul(PS[:, 2 + 2 * f + h, :], self.xet[b][:, k, :], w[:, k, :],
                                            start=(k == 0), stop=(k == 7))
                last.then_inc(s_gu.sem, 1)
                pe.drain().then_inc(block_used.sem, 1)

            def turn_hidden(self, pe, b, h):
                for k in range(4):
                    last = nc.tensor.transpose(PS[:, h, P * k:P * k + P], self.hg[b][:, 512 * h + P * k:512 * h + P * k + P],
                                               IDENT[:, :])
                last.then_inc(s_pt.sem, 1)

            def down(self, i, b, h, ks):
                w = ring.view(self.blocks + 6 * b + 4 + h, 8)
                for k in ks:
                    last = nc.tensor.matmul(PS[:, 6 + h, :], self.hgt[b][:, k, :], w[:, k, :], start=(k == 0), stop=(k == 7))
                return last

            def expert_pe(self, pe, i, b, more):
                pe.wait_ge(s_pta.sem, self.at(s_pta, 2, i, 2 * b + 1))
                pe.wait_ge(s_ptd.sem, self.at(s_ptd, 2, i, 2 * b + 1))
                self.gate_up(pe, i, b, 0, 0)
                self.gate_up(pe, i, b, 0, 1)
                if more:
                    self.turn_rows(pe, i, b + 1)
                self.gate_up(pe, i, b, 1, 0)
                pe.wait_ge(s_hid.sem, self.at(s_hid, 2, i, 2 * b + 1))
                if more:
                    pe.wait_ge(s_pta.sem, self.at(s_pta, 2, i, 2 * b + 2))
                self.turn_hidden(pe, b, 0)
                self.gate_up(pe, i, b, 1, 1)
                pe.wait_ge(s_pta.sem, self.at(s_pta, 2, i, 2 * b + (3 if more else 2)))
                pe.wait_ge(s_ye.sem, self.at(s_ye, 1, i, b + 1))
                ring.ready(pe, self.blocks + 6 * b + 4, i, 12)
                self.down(i, b, 0, range(0, 4))
                pe.wait_ge(s_hid.sem, self.at(s_hid, 2, i, 2 * b + 2))
                if more:
                    pe.wait_ge(s_ptd.sem, self.at(s_ptd, 2, i, 2 * b + 2))
                self.turn_hidden(pe, b, 1)
                ring.ready(pe, self.blocks + 6 * b + 5, i, 12)
                self.down(i, b, 1, range(0, 4))
                pe.wait_ge(s_ptd.sem, self.at(s_ptd, 2, i, 2 * b + (3 if more else 2)))
                self.down(i, b, 0, range(4, 8))
                pe.drain().then_inc(block_used.sem, 1)
                self.down(i, b, 1, range(4, 8)).then_inc(s_pv.sem, 1)
                pe.drain().then_inc(block_used.sem, 1)

            def tensor(self, pe):
                self.turn_rows(pe, 0, 0)
                self.trips(pe, self.expert_pe)

            def half(self, bank):
                return PS[:, bank, :].rearrange("p (a b) -> p a b", a=4)

            def expert_act(self, act, i, b, more):
                act.wait_ge(s_gu.sem, self.at(s_gu, 4, i, 4 * b + 1))
                nc.scalar.activation(self.sa[b][:, 0:512], PS[:, 2, :], ACT.Silu).then_inc(s_act.sem, 1)
                if more:
                    act.wait_ge(s_xet.sem, self.at(s_xet, 1, i, b + 2))
                    nc.scalar.activation(self.xet[1 - b][:, 0:4, :], self.half(0), ACT.Copy).then_inc(s_pta.sem, 1)
                act.wait_ge(s_gu.sem, self.at(s_gu, 4, i, 4 * b + 3))
                nc.scalar.activation(self.sa[b][:, 512:1024], PS[:, 3, :], ACT.Silu).then_inc(s_act.sem, 1)
                act.wait_ge(s_pt.sem, self.at(s_pt, 2, i, 2 * b + 1))
                nc.scalar.activation(self.hgt[b][:, 0:4, :], self.half(0), ACT.Copy).then_inc(s_pta.sem, 1)

            def scalar(self, act):
                act.wait_ge(s_xet.sem, self.b[s_xet] + 1)
                nc.scalar.activation(self.xet[0][:, 0:4, :], self.half(0), ACT.Copy).then_inc(s_pta.sem, 1)
                self.trips(act, self.expert_act)

            def hidden(self, dve, i, b, h):
                dve.wait_ge(s_act.sem, self.at(s_act, 2, i, 2 * b + h + 1))
                dve.wait_ge(s_gu.sem, self.at(s_gu, 4, i, 4 * b + 2 * h + 2))
                nc.vector.tensor_tensor(self.hg[b][:, 512 * h:512 * h + 512], self.sa[b][:, 512 * h:512 * h + 512],
                                        PS[:, 4 + h, :], ALU.mult).then_inc(s_hid.sem, 1)

            def expert_dve(self, dve, i, b, more):
                self.hidden(dve, i, b, 0)
                if more:
                    dve.wait_ge(s_xet.sem, self.at(s_xet, 1, i, b + 2))
                    nc.vector.tensor_copy(self.xet[1 - b][:, 4:8, :], self.half(1)).then_inc(s_ptd.sem, 1)
                self.hidden(dve, i, b, 1)
                dve.wait_ge(s_pt.sem, self.at(s_pt, 2, i, 2 * b + 2))
                nc.vector.tensor_copy(self.hgt[b][:, 4:8, :], self.half(1)).then_inc(s_ptd.sem, 1)
                dve.wait_ge(s_pv.sem, self.at(s_pv, 1, i, b + 1))
                dve.wait_ge(s_scatter.sem, self.at(s_scatter, 16, i, 16 * (b - 1)))
                gate = GT[:, bass.ds(i * 2 + b, 1)]
                nc.vector.tensor_scalar(self.ye[b].rearrange("p (a b) -> p a b", a=2), PS[:, 6:8, :], gate, None,
                                        ALU.mult).then_inc(s_ye.sem, 1)

            def vector(self, dve):
                dve.sem_inc(s_ye.sem, 1)
                dve.wait_ge(s_xet.sem, self.b[s_xet] + 1)
                nc.vector.tensor_copy(self.xet[0][:, 4:8, :], self.half(1)).then_inc(s_ptd.sem, 1)
                self.trips(dve, self.expert_dve)

            def gather(self, gp, n):
                b = n % 2
                gp.indirect_dma_start(self.xe[b], None, h2_dram,
                                      bass.IndirectOffsetOnAxis(ap=IDX[:, n:n + 1], axis=0)).then_inc(s_gather[b].sem, 16)

            def pool(self, gp):
                self.gather(gp, 0)
                self.gather(gp, 1)
                for n in range(N_EXP):
                    if n + 2 < N_EXP:
                        gp.wait_ge(s_xet.sem, self.b[s_xet] + n + 1)
                        self.gather(gp, n + 2)
                    gp.wait_ge(s_ye.sem, self.b[s_ye] + n + 2)
                    gp.wait_ge(s_scatter.sem, self.b[s_scatter] + 16 * n)
                    gp.indirect_dma_start(y_dram, bass.IndirectOffsetOnAxis(ap=IDX[:, n:n + 1], axis=0), self.ye[n % 2], None,
                                          compute_op=ALU.add).then_inc(s_scatter.sem, 16)
                gp.wait_ge(s_scatter.sem, self.b[s_scatter] + 16 * N_EXP)

        class Finish(Stage):

            def __init__(self, y, gf):
                self.y, self.gf = y, gf
                self.sq = squares.span(8)
                self.rt = roots.span(8)
                self.nm = normed.span(8)
                self.fin = rows_final.span(8)
                self.o = out_dma.span(128)
                self.y_in = 16 * (N_EXP // 2) + 16

            def load(self, sp):
                for t in range(8):
                    sp.wait_ge(rows_final.sem, self.fin + t + 1)
                    sp.dma_start(out[0, P * t:P * t + P, :], X[:, t, :]).then_inc(out_dma.sem, 16)
                sp.wait_ge(out_dma.sem, self.o + 128)

            def pool(self, gp):
                rows = y_dram.rearrange("(t p) d -> p t d", p=P)
                for h in range(2):
                    gp.dma_start(self.y[:, 4 * h:4 * h + 4, :], rows[:, 4 * h:4 * h + 4, :]).then_inc(s_gather[h].sem, 16)
                for h in range(2):
                    gp.wait_ge(s_gather[h].sem, self.y_in)

            def vector(self, dve):
                lag = 2
                for s in range(8 + lag):
                    if s < 8:
                        if s % 4 == 0:
                            dve.wait_ge(s_gather[s // 4].sem, self.y_in)
                        dstep(dve, nc.vector.tensor_tensor(self.y[:, s, :], self.y[:, s, :], GATE[:, :], ALU.mult))
                        nc.vector.tensor_tensor(X[:, s, :], X[:, s, :], self.y[:, s, :], ALU.add).then_inc(normed.sem, 1)
                    if s >= lag:
                        t = s - lag
                        dve.wait_ge(roots.sem, self.rt + t + 1)
                        dstep(dve, nc.vector.reciprocal(stat(16 + t, 17 + t), stat(8 + t, 9 + t)))
                        nc.vector.scalar_tensor_tensor(X[:, t, :], X[:, t, :], stat(16 + t, 17 + t), self.gf, ALU.mult,
                                                       ALU.mult).then_inc(rows_final.sem, 1)

            def scalar(self, act):
                for t in range(8):
                    act.wait_ge(normed.sem, self.nm + t + 1)
                    nc.scalar.activation(self.y[:, t, :], X[:, t, :], ACT.Square, accum_out=stat(t, t + 1)).then_inc(squares.sem, 1)
                    act.wait_ge(squares.sem, self.sq + t + 1)
                    nc.scalar.activation(stat(8 + t, 9 + t), stat(t, t + 1), ACT.Sqrt, bias=EPSC[:, :], scale=1.0 / D).then_inc(roots.sem, 1)

        def second_block():
            w_in = A["w_in_2"][0]
            dq, dk, dv = area(8192, 8, 512), area(12288, 8, 512), area(16384, 8, 512)
            p672 = area(12288, 8, 672)
            ckvt = area(0, 2, 1024)
            cqt = [area(20480, 1024), area(21504, 1024), area(7168, 1024)]
            kv = area(12288, 8, 1024)
            q = area(0, 8, 768)
            dil = area(20480, 1920)

            def tok(t, c0, c1, width=512):
                return lambda n, k: (HT[:, k, P * t:P * t + P],
                                     WB[:, n % RING, 0:8 * width].rearrange("p (k n) -> p k n", k=8)[:, k, c0:c1])

            def heads(x, d):
                return x.rearrange("p t (h d) -> p t h d", d=d)

            st = [Norm(X, 8, DER[:, 0, 0, :], MODC[:, 0, 0:8], HT, area(8192, 8, D)),
                  Beside(Rotations(), Product([(rows_of(w_in, 672 + 512 * b, 1184 + 512 * b), SLOT) for b in range(3)],
                          [(b, tok(t, 0, 512), 512, "act" if t % 2 else "dve", to(dst[:, t, :]))
                           for b, dst in enumerate((dq, dk, dv)) for t in range(8)], KD)),
                  RotateHeads([heads(dq, 64), heads(dk, 64)], 0, 16, 8, 64),
                  LoadTable(dil, consts["dil"])]

            sq, sk = xarea(0, 8, 128), xarea(1024, 8, 128)
            kt = xarea(3072, 1024)

            def stage_d(i):
                nc.vector.tensor_copy(sq, dq[:, :, bass.ts(i, 128)])
                return nc.vector.tensor_copy(sk, dk[:, :, bass.ts(i, 128)])

            def keys_d(h, t, bank_a, bank_b):
                b = 64 * (h % 2)
                return [(bank_a, kt[b:b + 64, 0:512]), (bank_b, kt[b:b + 64, 512:1024])]

            st.append(Attention(4, 2, 8, 64, 0.125, sq, xarea(2048, 1024), xarea(4096, 2, 1024), xarea(6144, 2, 1024), steps=48,
                                sk=sk, kt=kt, stage=stage_d, keys=keys_d,
                                values=lambda i, h, t, j: dv[:, j, bass.ds(i * 128 + 64 * h, 64)],
                                out=lambda i, h, t: dq[:, t, bass.ds(i * 128 + 64 * h, 64)],
                                local=lambda t: (0, 8), masked=dil, wide=1))

            st.append(Product([(rows_of(w_in, 0, 512), SLOT), (rows_of(w_in, 512, 672), 1280)],
                              [(0, tok(t, 0, 512), 512, "act" if t % 2 else "dve", to(p672[:, t, 0:512])) for t in range(8)]
                              + [(1, tok(t, 0, 160, 160), 160, "act" if t % 2 else "dve", to(p672[:, t, 512:672])) for t in range(8)], KD))
            st += [Norm(p672[:, :, 0:384], 8, VEC[:, 2, ROW2_Q:ROW2_Q + 3], None, cqt, xarea(0, 8, 384), width=384),
                   Norm(p672[:, :, 384:640], 8, VEC[:, 2, ROW2_KV:ROW2_KV + 2], None, ckvt, xarea(3072, 8, 256), width=256),
                   RotateHeads([heads(p672[:, :, 640:672], 32)], 0, 32, 1, 0),
                   Copy(KR, p672[:, :, 640:672])]

            def small(x, K, width, c0, c1):
                def ops(n, k):
                    w = WB[:, n % RING, 0:K * width].rearrange("p (k n) -> p k n", k=K)
                    return x(k), w[:, k, c0:c1]
                return ops

            st.append(Product([(A["w_ukv_2"][0].rearrange("(k p) n -> p k n", p=P), 2048)],
                              [(0, small(lambda k, t=t: ckvt[:, k, P * t:P * t + P], 2, 1024, 512 * n, 512 * n + 512), 512,
                                "act" if n else "dve", to(kv[:, t, 512 * n:512 * n + 512])) for t in range(8) for n in range(2)], 2))
            st.append(Product([(A["w_uq_2"][0].rearrange("(k p) n -> p k n", p=P), 2304)],
                              [(0, small(lambda k, t=t: cqt[k][:, P * t:P * t + P], 3, 768, 384 * n, 384 * n + 384), 384,
                                "act" if n else "dve", to(q[:, t, 384 * n:384 * n + 384])) for t in range(8) for n in range(2)], 3))
            st.append(RotateHeads([heads(q, 96)], 64, 32, 8, 0))

            sq2, sk2 = area(6144, 8, 192), area(20480, 8, 192)
            kt2 = xarea(2048, 2048)

            def stage_m(i):
                nc.vector.tensor_copy(sq2, q[:, :, bass.ts(i, 192)])
                for h in range(2):
                    nc.vector.tensor_copy(sk2[:, :, 96 * h:96 * h + 64], kv[:, :, bass.ds(i * 256 + 128 * h, 64)])
                    ins = nc.vector.tensor_copy(sk2[:, :, 96 * h + 64:96 * h + 96], KR)
                return ins

            def keys_m(h, t, bank_a, bank_b):
                return [(bank_a, kt2[0:96, 1024 * h:1024 * h + 512]), (bank_b, kt2[0:96, 1024 * h + 512:1024 * h + 1024])]

            st.append(Attention(4, 2, 8, 96, 96.0 ** -0.5, sq2, xarea(0, 2048), xarea(4096, 2, 1024), xarea(6144, 2, 1024), steps=32,
                                sk=sk2, kt=kt2, stage=stage_m, keys=keys_m,
                                values=lambda i, h, t, j: kv[:, j, bass.ds(i * 256 + 128 * h + 64, 64)],
                                out=lambda i, h, t: q[:, t, bass.ds(i * 128 + 64 * h, 64)], ctx_keys=1024))

            mt = area(12288, 8, 1024)

            def mixed(t, c):
                if c < 4:
                    return q[:, t, P * c:P * c + P]
                return dq[:, t, P * (c - 4):P * (c - 4) + P]

            st += [Turn(8, mixed, lambda c, a, b: mt[:, c, a:b], None),
                   LoadTable(XF, x_spill, Spread(MODC[:, 0, 16:24], GATE[:, :], area(0, 1024)),
                             Spread(DER[:, 0, 1, :], area(20480, 1024), area(1024, 1024), 2),
                             Spread(MODC[:, 0, 24:32], area(21504, 1024), area(2048, 1024), 4)),
                   OutProduct(A["w_out_2"][0], mt, X, 8, False, area(0, 4096)),
                   Norm(X, 8, DER[:, 0, 1, :], MODC[:, 0, 24:32], HT, area(8192, 8, D)),
                   Rows(area(8192, 8, D), area(20480, 1024), area(21504, 1024), area(16384, 1024),
                        area(17408, 8, N_EXP),
                        (Spread(MODC[:, 0, 40:48], GATE[:, :], area(19456, 1024), 2),
                         Spread(VEC[:, 2, ROW2_FINAL:ROW2_FINAL + 8], area(18432, 1024), area(20480, 1024), 4))),
                   Route(8192),
                   Experts(),
                   Finish(area(8192, 8, D), area(18432, 1024))]
            return st

        stages = [Setup(), Modulate(0)] + layer_stream(0, 1, XC, 2) + layer_stream(0, 0, X, 8)
        stages += [Gains(1)] + context_kv(1) + layer_stream(1, 0, X, 8)
        stages += [Gains(2)] + second_block()
        fence_no = {e: 0 for e in stage_end}

        def fence(eng, me):
            eng.drain().then_inc(stage_end[me], 1)
            fence_no[me] += 1
            for other in stage_end:
                if other != me:
                    eng.wait_ge(stage_end[other], fence_no[me])

        block = ctx.enter_context(nc.Block())

        @block.sync
        def _(sp):
            for st in stages:
                st.load(sp)

        @block.tensor
        def _(pe):
            for st in stages:
                st.tensor(pe)
                fence(pe, "pe")

        @block.scalar
        def _(act):
            for st in stages:
                st.scalar(act)
                fence(act, "act")

        @block.vector
        def _(dve):
            for st in stages:
                st.vector(dve)
                fence(dve, "dve")

        @block.gpsimd
        def _(gp):
            for st in stages:
                st.pool(gp)
                fence(gp, "pool")


def shape_tables():
    import numpy as np

    t = {"ident": np.eye(128, dtype=np.float32)}
    n_freq = 16
    inv = (10000.0 ** (-np.arange(n_freq, dtype=np.float32) / n_freq)).astype(np.float32)
    row = np.repeat(np.arange(16), 64).astype(np.float32)
    col = np.tile(np.arange(64), 16).astype(np.float32)
    ar, ac = row[:, None] * inv[None], col[:, None] * inv[None]
    cos = np.cos(np.concatenate([ar, ar, ac, ac], -1))
    sin = np.sin(np.concatenate([-ar, ar, -ac, ac], -1))
    rope = np.stack([cos, sin]).reshape(2, 8, 128, 64).transpose(2, 0, 1, 3).reshape(128, 2, 512)
    t["rope"] = np.ascontiguousarray(rope, dtype=np.float32)
    q, k = np.arange(128)[:, None], np.arange(384)[None] - 128
    t["wmask"] = np.where(np.abs(k - q) <= 128, 0.0, -1e30).astype(np.float32)
    rel = np.arange(1920)[None] - 896 - np.arange(128)[:, None]
    count = sum(((rel % d == 0) & (np.abs(rel) <= 64 * d)).astype(np.float64) for d in (1, 4, 16))
    t["dil"] = np.where(count > 0, np.log(np.maximum(count, 1)), -1e30).astype(np.float32)
    a = 2 * np.pi * np.outer(np.arange(64), np.arange(64)) / 64
    f = np.zeros((128, 256))
    for g in range(2):
        f[64 * g:64 * g + 64, 64 * g:64 * g + 64] = np.cos(a)
        f[64 * g:64 * g + 64, 128 + 64 * g:128 + 64 * g + 64] = -np.sin(a)
    t["dftf"] = f.astype(np.float32)

    def seq(n):
        m = np.outer(np.arange(n), np.arange(n)) % n
        cs = np.stack([np.cos(2 * np.pi * m / n), np.sin(2 * np.pi * m / n)])
        cs = cs.reshape(2, n // 128, 128, n // 256, 256).transpose(3, 2, 1, 0, 4)
        return np.ascontiguousarray(cs.reshape(n // 256, 128, -1), dtype=np.float32)

    t["dfts"] = seq(1024)
    t["dftc"] = seq(256)[0]
    inv_m = 1.0 / (500000.0 ** (np.arange(0, 32, 2, dtype=np.float32) / np.float32(32)))
    inv_d = 1.0 / (500000.0 ** (np.arange(0, 16, 2, dtype=np.float32) / np.float32(16)))
    t["inv"] = np.tile(np.concatenate([inv_m, inv_d]).astype(np.float32)[None], (128, 1))
    return t


_INS = ["x", "c", "ctx", "c_ctx", "w_ada", "b_ada", "g_pre_mix", "w_in", "sink", "w_sgu", "b_sgu", "g_sgu", "g_mix", "w_out",
        "g_post_mix", "g_pre_ff", "w_ff1", "w_ff2", "g_post_ff", "c_2", "positions_2", "w_ada_2", "b_ada_2", "g_mix_2",
        "w_in_2", "g_q_2", "w_uq_2", "g_kv_2", "w_ukv_2", "w_out_2", "g_ffn_2", "w_router_2", "b_router_2", "w_gate_2",
        "w_up_2", "w_down_2", "g_final_2"]


def kernel(**inputs):
    import numpy as _np
    import concourse.bacc as _bacc
    from concourse import mybir as _mybir
    from concourse.bass_utils import run_bass_kernel_spmd as _run

    nc = _bacc.Bacc("TRN2", target_bir_lowering=False, num_devices=1)
    arrays, args, consts = {}, {}, {}
    for name in _INS:
        a = _np.ascontiguousarray(inputs[name])
        arrays[f"in_{name}_dram"] = a
        args[name] = nc.dram_tensor(f"in_{name}_dram", a.shape, _mybir.dt.from_np(a.dtype), kind="ExternalInput").ap()
    for name, a in shape_tables().items():
        arrays[f"table_{name}_dram"] = a
        consts[name] = nc.dram_tensor(f"table_{name}_dram", a.shape, _mybir.dt.from_np(a.dtype), kind="ExternalInput").ap()
    out = nc.dram_tensor("out_0_dram", (1, 1024, 1024), _mybir.dt.float32, kind="ExternalOutput").ap()
    build(nc, args, consts, out)
    r = _run(nc, [arrays], core_ids=[0])
    return r.results[0]["out_0_dram"]
```
